# Optimizing a Trainium2 kernel written in Bass

```python
import math
import functools
import jax
import jax.numpy as jnp
from jax import lax
import numpy as np
import jax, jax.numpy as jnp

D_MODEL = 1024
BATCH = 1
SEQ = 256
DEPTH = 2

GRID_W = 64
CTX_LEN = 256
N_EVEN = (DEPTH + 1) // 2
N_ODD = DEPTH // 2
EPS = 1e-6

GLA_HEADS = 4
GLA_DK = D_MODEL // 16
GLA_DV = D_MODEL // 8
GLA_RANK = 16
GLA_TAU = 16.0
GLA_CHUNK = 64

ML_HEADS = 4
ML_D = D_MODEL // 8
ML_CONV = 3
ML_CHUNK = 64

D_INNER = 2 * D_MODEL
SSD_HEADDIM = 64
SSD_HEADS = D_INNER // SSD_HEADDIM
SSD_GROUPS = 4
SSD_HPG = SSD_HEADS // SSD_GROUPS
SSD_STATE = 128
SSD_CONV = 3
SSD_CHUNK = 128

D_FF = 2816
FFN_CONV = 3

GLA_QK = GLA_HEADS * GLA_DK
GLA_V = GLA_HEADS * GLA_DV
ML_W = ML_HEADS * ML_D
EVEN_SIZES = (GLA_QK, GLA_QK, GLA_V, GLA_V, ML_W, ML_W, ML_W, ML_W, 4 * ML_HEADS)
EVEN_IN = sum(EVEN_SIZES)
SSD_BC = SSD_GROUPS * SSD_STATE
SSD_CONV_CH = D_INNER + 2 * SSD_BC
ODD_SIZES = (D_INNER, SSD_CONV_CH, 2 * SSD_HEADS)
ODD_IN = sum(ODD_SIZES)


def _split(a, sizes):
    return jnp.split(a, [int(s) for s in np.cumsum(sizes)[:-1]], axis=-1)

def rmsnorm(x, g):
    xf = x.astype(jnp.float32)
    y = xf * lax.rsqrt(jnp.mean(xf * xf, axis=-1, keepdims=True) + EPS)
    return (y * g.astype(jnp.float32)).astype(x.dtype)

def modulate(x, g, shift, scale):
    return rmsnorm(x, g) * (1 + scale) + shift

def dwconv1d(x, w, b):
    k_w = w.shape[0]
    t = x.shape[1]
    pad = k_w // 2
    xp = jnp.pad(x, ((0, 0), (pad, pad), (0, 0)))
    return sum(xp[:, j:j + t] * w[j] for j in range(k_w)) + b

def dwconv2d_grid(x, w, b, rows):
    bsz, t, ch = x.shape
    y = lax.conv_general_dilated(x.reshape(bsz, rows, GRID_W, ch), w[:, :, None, :], (1, 1), 'SAME',
                                 dimension_numbers=('NHWC', 'HWIO', 'NHWC'), feature_group_count=ch)
    return y.reshape(bsz, t, ch) + b

def to_chunks(a, size):
    bsz, t = a.shape[:2]
    return jnp.moveaxis(a.reshape(bsz, t // size, size, *a.shape[2:]), 1, 0)

def from_chunks(a):
    a = jnp.moveaxis(a, 0, 1)
    return a.reshape(a.shape[0], a.shape[1] * a.shape[2], *a.shape[3:])

def gla_scan(q, k, v, log_a, s0, with_out):
    size = GLA_CHUNK
    tri = jnp.tril(jnp.ones((size, size), dtype=bool))[None, :, :, None, None]

    def step(s, inp):
        qc, kc, vc, lac = inp
        cum = jnp.cumsum(lac.astype(jnp.float32), axis=1)
        c_end = cum[:, -1]
        k_end = kc * jnp.exp(c_end[:, None] - cum)
        s_new = jnp.exp(c_end)[..., None] * s + jnp.einsum('bshk,bshv->bhkv', k_end, vc)
        if not with_out:
            return s_new, None
        rel = jnp.where(tri, cum[:, :, None] - cum[:, None, :], -jnp.inf)
        att = jnp.einsum('bthk,bshk,btshk->bhts', qc, kc, jnp.exp(rel))
        o = jnp.einsum('bhts,bshv->bthv', att, vc) + jnp.einsum('bthk,bhkv->bthv', qc * jnp.exp(cum), s)
        return s_new, o

    s, o = lax.scan(step, s0, tuple(to_chunks(a, size) for a in (q, k, v, log_a)))
    return (from_chunks(o) if with_out else None), s

def mlstm_scan(q, k, v, li, lf, state0, with_out):
    size = ML_CHUNK
    tri = jnp.tril(jnp.ones((size, size), dtype=bool))[None, :, :, None]

    def step(carry, inp):
        cmat, nvec, m = carry
        qc, kc, vc, lic, lfc = inp
        b = jnp.cumsum(lfc, axis=1)
        b_end = b[:, -1]
        w_end = b_end[:, None] - b + lic
        m_new = jnp.maximum(b_end + m, jnp.max(w_end, axis=1))
        decay = jnp.exp(b_end + m - m_new)
        ws = jnp.exp(w_end - m_new[:, None])
        c_new = decay[..., None, None] * cmat + jnp.einsum('bsh,bshk,bshv->bhkv', ws, kc, vc)
        n_new = decay[..., None] * nvec + jnp.einsum('bsh,bshk->bhk', ws, kc)
        if not with_out:
            return (c_new, n_new, m_new), None
        a_in = b + m[:, None]
        d_log = jnp.where(tri, b[:, :, None] - b[:, None, :] + lic[:, None, :], -jnp.inf)
        m_t = jnp.maximum(a_in, jnp.max(d_log, axis=2))
        dw = jnp.exp(d_log - m_t[:, :, None])
        aw = jnp.exp(a_in - m_t)
        sc = jnp.einsum('bthk,bshk->btsh', qc, kc) * dw
        num = aw[..., None] * jnp.einsum('bthk,bhkv->bthv', qc, cmat) + jnp.einsum('btsh,bshv->bthv', sc, vc)
        den = aw * jnp.einsum('bthk,bhk->bth', qc, nvec) + jnp.sum(sc, axis=2)
        h = num / jnp.maximum(jnp.abs(den), jnp.exp(-m_t))[..., None]
        return (c_new, n_new, m_new), h

    state, h = lax.scan(step, state0, tuple(to_chunks(a, size) for a in (q, k, v, li, lf)))
    return (from_chunks(h) if with_out else None), state

def ssd_scan(x, dt, bm, cm, s0, with_out, A):
    size = SSD_CHUNK
    tri = jnp.tril(jnp.ones((size, size), dtype=bool))[None, :, :, None, None]

    def step(s, inp):
        xc, dtc, bc, cc = inp
        cum = jnp.cumsum(dtc * A, axis=1)
        c_end = cum[:, -1]
        w_end = jnp.exp(c_end[:, None] - cum) * dtc
        s_new = jnp.exp(c_end)[..., None, None] * s + jnp.einsum('bsgh,bsgn,bsghp->bghpn', w_end, bc, xc)
        if not with_out:
            return s_new, None
        seg = jnp.where(tri, cum[:, :, None] - cum[:, None, :], -jnp.inf)
        cb = jnp.einsum('btgn,bsgn->btsg', cc, bc)
        w = jnp.exp(seg) * cb[..., None] * dtc[:, None]
        y = (jnp.einsum('btsgh,bsghp->btghp', w, xc)
             + jnp.exp(cum)[..., None] * jnp.einsum('btgn,bghpn->btghp', cc, s))
        return s_new, y

    s, y = lax.scan(step, s0, tuple(to_chunks(a, size) for a in (x, dt, bm, cm)))
    return (from_chunks(y) if with_out else None), s

def bidir_scan(scan_f, scan_b, ctx_f, lat_f, ctx_b, lat_b, init, ctx_out):
    def one_dir(scan_fn, ctx_args, lat_args):
        yc, s_ctx = scan_fn(*ctx_args, init, ctx_out)
        yl, _ = scan_fn(*lat_args, s_ctx, True)
        return yc, yl

    def rev(a):
        return jnp.flip(a, axis=1)

    yc_f, yl_f = one_dir(scan_f, ctx_f, lat_f)
    yc_b, yl_b = one_dir(scan_b, [rev(a) for a in ctx_b], [rev(a) for a in lat_b])
    yl = yl_f + rev(yl_b)
    yc = (yc_f + rev(yc_b)) if ctx_out else None
    return yc, yl

def even_features(h, w_in, a1, a2, ab, conv_w, conv_b, gate_b):
    bsz, t, _ = h.shape
    gq, gk, gv, gg, mq, mk, mv, mo, mg = _split(h @ w_in, EVEN_SIZES)
    log_a = [(jax.nn.log_sigmoid(((h @ a1[d]) @ a2[d] + ab[d]).astype(jnp.float32)) / GLA_TAU)
             .reshape(bsz, t, GLA_HEADS, GLA_DK) for d in range(2)]
    qk = jax.nn.silu(dwconv1d(jnp.concatenate([mq, mk], axis=-1), conv_w, conv_b))
    mq, mk = jnp.split(qk, 2, axis=-1)
    gates = (mg + gate_b).astype(jnp.float32).reshape(bsz, t, 4, ML_HEADS)
    return {
        'gla_q': gq.reshape(bsz, t, GLA_HEADS, GLA_DK) * GLA_DK ** -0.5,
        'gla_k': gk.reshape(bsz, t, GLA_HEADS, GLA_DK),
        'gla_v': gv.reshape(bsz, t, GLA_HEADS, GLA_DV),
        'gla_g': gg,
        'la_f': log_a[0], 'la_b': log_a[1],
        'ml_q': mq.reshape(bsz, t, ML_HEADS, ML_D),
        'ml_k': mk.reshape(bsz, t, ML_HEADS, ML_D) * ML_D ** -0.5,
        'ml_v': mv.reshape(bsz, t, ML_HEADS, ML_D),
        'ml_o': mo,
        'li_f': gates[:, :, 0], 'lf_f': jax.nn.log_sigmoid(gates[:, :, 1]),
        'li_b': gates[:, :, 2], 'lf_b': jax.nn.log_sigmoid(gates[:, :, 3]),
    }

def even_combine(f, o_gla, h_ml, gla_norm_g, ml_norm_g, w_out):
    bsz, t = o_gla.shape[:2]
    gla = rmsnorm(o_gla, gla_norm_g.reshape(GLA_HEADS, GLA_DV)).reshape(bsz, t, GLA_V) * jax.nn.silu(f['gla_g'])
    ml = jax.nn.sigmoid(f['ml_o']).reshape(bsz, t, ML_HEADS, ML_D) * h_ml
    ml = rmsnorm(ml, ml_norm_g.reshape(ML_HEADS, ML_D)).reshape(bsz, t, ML_W)
    return jnp.concatenate([gla, ml], axis=-1).astype(w_out.dtype) @ w_out

def even_mixer(hc, hl, w_in, a1, a2, ab, conv_w, conv_b, gate_b, gla_norm_g, ml_norm_g, w_out, ctx_out):
    fc = even_features(hc, w_in, a1, a2, ab, conv_w, conv_b, gate_b)
    fl = even_features(hl, w_in, a1, a2, ab, conv_w, conv_b, gate_b)
    bsz = hl.shape[0]

    def g_args(f, d):
        return (f['gla_q'], f['gla_k'], f['gla_v'], f['la_' + d])

    gla_init = jnp.zeros((bsz, GLA_HEADS, GLA_DK, GLA_DV), jnp.float32)
    oc_gla, ol_gla = bidir_scan(gla_scan, gla_scan, g_args(fc, 'f'), g_args(fl, 'f'),
                                g_args(fc, 'b'), g_args(fl, 'b'), gla_init, ctx_out)

    def m_args(f, d):
        return (f['ml_q'], f['ml_k'], f['ml_v'], f['li_' + d], f['lf_' + d])

    ml_init = (jnp.zeros((bsz, ML_HEADS, ML_D, ML_D), jnp.float32),
               jnp.zeros((bsz, ML_HEADS, ML_D), jnp.float32),
               jnp.zeros((bsz, ML_HEADS), jnp.float32))
    hc_ml, hl_ml = bidir_scan(mlstm_scan, mlstm_scan, m_args(fc, 'f'), m_args(fl, 'f'),
                              m_args(fc, 'b'), m_args(fl, 'b'), ml_init, ctx_out)
    yl = even_combine(fl, ol_gla, hl_ml, gla_norm_g, ml_norm_g, w_out)
    yc = even_combine(fc, oc_gla, hc_ml, gla_norm_g, ml_norm_g, w_out) if ctx_out else None
    return yc, yl

def odd_features(h, w_in, conv_w, conv_b, dt_bias):
    bsz, t, _ = h.shape
    z, xbc, dt = _split(h @ w_in, ODD_SIZES)
    xs, bm, cm = _split(jax.nn.silu(dwconv1d(xbc, conv_w, conv_b)), (D_INNER, SSD_BC, SSD_BC))
    dt = jax.nn.softplus(dt.astype(jnp.float32).reshape(bsz, t, 2, SSD_HEADS) + dt_bias.astype(jnp.float32))
    dt = dt.reshape(bsz, t, 2, SSD_GROUPS, SSD_HPG)
    return {
        'z': z,
        'x': xs.reshape(bsz, t, SSD_GROUPS, SSD_HPG, SSD_HEADDIM),
        'b': bm.reshape(bsz, t, SSD_GROUPS, SSD_STATE),
        'c': cm.reshape(bsz, t, SSD_GROUPS, SSD_STATE),
        'dt_f': dt[:, :, 0], 'dt_b': dt[:, :, 1],
    }

def odd_mixer(hc, hl, w_in, conv_w, conv_b, dt_bias, a_log, d_skip, norm_g, w_out, ctx_out):
    fc = odd_features(hc, w_in, conv_w, conv_b, dt_bias)
    fl = odd_features(hl, w_in, conv_w, conv_b, dt_bias)
    bsz = hl.shape[0]
    A = -jnp.exp(a_log.astype(jnp.float32)).reshape(2, SSD_GROUPS, SSD_HPG)
    scan_f = functools.partial(ssd_scan, A=A[0])
    scan_b = functools.partial(ssd_scan, A=A[1])

    def s_args(f, d):
        return (f['x'], f['dt_' + d], f['b'], f['c'])

    init = jnp.zeros((bsz, SSD_GROUPS, SSD_HPG, SSD_HEADDIM, SSD_STATE), jnp.float32)
    yc, yl = bidir_scan(scan_f, scan_b, s_args(fc, 'f'), s_args(fl, 'f'),
                        s_args(fc, 'b'), s_args(fl, 'b'), init, ctx_out)

    def combine(f, y):
        b_, t_ = y.shape[:2]
        y = (y + d_skip.reshape(SSD_GROUPS, SSD_HPG)[..., None] * f['x']).reshape(b_, t_, D_INNER)
        y = (y * jax.nn.silu(f['z'])).reshape(b_, t_, SSD_GROUPS, D_INNER // SSD_GROUPS)
        y = rmsnorm(y, norm_g.reshape(SSD_GROUPS, D_INNER // SSD_GROUPS)).reshape(b_, t_, D_INNER)
        return y.astype(w_out.dtype) @ w_out

    return (combine(fc, yc) if ctx_out else None), combine(fl, yl)

def conv_ffn(h, w_up, conv_w, conv_b, w_down, rows):
    u = h @ w_up
    if rows is None:
        u = dwconv1d(u, conv_w[1], conv_b)
    else:
        u = dwconv2d_grid(u, conv_w, conv_b, rows)
    a, g = jnp.split(u, 2, axis=-1)
    return (jax.nn.silu(g) * a) @ w_down

def first_inputs(seed: int = 0) -> dict:
    key = jax.random.key(seed)
    ks = list(jax.random.split(key, 40))
    f32 = jnp.float32

    def nrm(shape, scale):
        return scale * jax.random.normal(ks.pop(), shape, f32)

    def gain(shape):
        return 1.0 + 0.05 * jax.random.normal(ks.pop(), shape, f32)

    gate_base = jnp.concatenate([jnp.zeros((ML_HEADS,), f32), jnp.linspace(3.0, 6.0, ML_HEADS, dtype=f32)] * 2)
    dt0 = jnp.exp(jax.random.uniform(ks.pop(), (N_ODD, 2, SSD_HEADS), f32, math.log(1e-3), math.log(1e-1)))
    return {
        'x': nrm((BATCH, SEQ, D_MODEL), 1.0),
        'c': nrm((BATCH, D_MODEL), 1.0),
        'ctx': nrm((BATCH, CTX_LEN, D_MODEL), 1.0),
        'c_ctx': nrm((D_MODEL,), 1.0),
        'mod_w': nrm((DEPTH, D_MODEL, 6 * D_MODEL), 0.5 * D_MODEL ** -0.5),
        'mod_b': nrm((DEPTH, 6 * D_MODEL), 0.02),
        'norm_mix_g': gain((DEPTH, D_MODEL)),
        'norm_ffn_g': gain((DEPTH, D_MODEL)),
        'final_norm_g': gain((D_MODEL,)),
        'ffn_w_up': nrm((DEPTH, D_MODEL, 2 * D_FF), D_MODEL ** -0.5),
        'ffn_conv_w': nrm((DEPTH, FFN_CONV, FFN_CONV, 2 * D_FF), 1.0 / FFN_CONV),
        'ffn_conv_b': nrm((DEPTH, 2 * D_FF), 0.02),
        'ffn_w_down': nrm((DEPTH, D_FF, D_MODEL), D_FF ** -0.5),
        'even_w_in': nrm((N_EVEN, D_MODEL, EVEN_IN), D_MODEL ** -0.5),
        'gla_a1': nrm((N_EVEN, 2, D_MODEL, GLA_RANK), D_MODEL ** -0.5),
        'gla_a2': nrm((N_EVEN, 2, GLA_RANK, GLA_QK), GLA_RANK ** -0.5),
        'gla_ab': nrm((N_EVEN, 2, GLA_QK), 0.1),
        'ml_conv_w': nrm((N_EVEN, ML_CONV, 2 * ML_W), ML_CONV ** -0.5),
        'ml_conv_b': nrm((N_EVEN, 2 * ML_W), 0.02),
        'ml_gate_b': gate_base[None] + nrm((N_EVEN, 4 * ML_HEADS), 0.1),
        'gla_norm_g': gain((N_EVEN, GLA_V)),
        'ml_norm_g': gain((N_EVEN, ML_W)),
        'even_w_out': nrm((N_EVEN, GLA_V + ML_W, D_MODEL), (GLA_V + ML_W) ** -0.5),
        'ssd_w_in': nrm((N_ODD, D_MODEL, ODD_IN), D_MODEL ** -0.5),
        'ssd_conv_w': nrm((N_ODD, SSD_CONV, SSD_CONV_CH), SSD_CONV ** -0.5),
        'ssd_conv_b': nrm((N_ODD, SSD_CONV_CH), 0.02),
        'ssd_dt_bias': dt0 + jnp.log(-jnp.expm1(-dt0)),
        'ssd_a_log': jnp.log(jax.random.uniform(ks.pop(), (N_ODD, 2, SSD_HEADS), f32, 1.0, 16.0)),
        'ssd_d': gain((N_ODD, SSD_HEADS)),
        'ssd_norm_g': gain((N_ODD, D_INNER)),
        'ssd_w_out': nrm((N_ODD, D_INNER, D_MODEL), D_INNER ** -0.5),
    }

def first_block(x, c, ctx, c_ctx, mod_w, mod_b, norm_mix_g, norm_ffn_g, final_norm_g,
              ffn_w_up, ffn_conv_w, ffn_conv_b, ffn_w_down,
              even_w_in, gla_a1, gla_a2, gla_ab, ml_conv_w, ml_conv_b, ml_gate_b,
              gla_norm_g, ml_norm_g, even_w_out,
              ssd_w_in, ssd_conv_w, ssd_conv_b, ssd_dt_bias, ssd_a_log, ssd_d, ssd_norm_g, ssd_w_out):
    rows = x.shape[1] // GRID_W
    xl, xc = x, ctx
    for layer in range(DEPTH):
        last = layer == DEPTH - 1
        mod_l = (jax.nn.silu(c) @ mod_w[layer] + mod_b[layer])[:, None, :]
        mod_c = (jax.nn.silu(c_ctx) @ mod_w[layer] + mod_b[layer])[None, None, :]
        sh1l, sc1l, g1l, sh2l, sc2l, g2l = jnp.split(mod_l, 6, axis=-1)
        sh1c, sc1c, g1c, sh2c, sc2c, g2c = jnp.split(mod_c, 6, axis=-1)
        hl = modulate(xl, norm_mix_g[layer], sh1l, sc1l)
        hc = modulate(xc, norm_mix_g[layer], sh1c, sc1c)
        if layer % 2 == 0:
            e = layer // 2
            yc, yl = even_mixer(hc, hl, even_w_in[e], gla_a1[e], gla_a2[e], gla_ab[e], ml_conv_w[e], ml_conv_b[e],
                                ml_gate_b[e], gla_norm_g[e], ml_norm_g[e], even_w_out[e], not last)
        else:
            o = layer // 2
            yc, yl = odd_mixer(hc, hl, ssd_w_in[o], ssd_conv_w[o], ssd_conv_b[o], ssd_dt_bias[o], ssd_a_log[o],
                               ssd_d[o], ssd_norm_g[o], ssd_w_out[o], not last)
        xl = xl + g1l * yl
        hl = modulate(xl, norm_ffn_g[layer], sh2l, sc2l)
        xl = xl + g2l * conv_ffn(hl, ffn_w_up[layer], ffn_conv_w[layer], ffn_conv_b[layer], ffn_w_down[layer], rows)
        if not last:
            xc = xc + g1c * yc
            hc = modulate(xc, norm_ffn_g[layer], sh2c, sc2c)
            xc = xc + g2c * conv_ffn(hc, ffn_w_up[layer], ffn_conv_w[layer], ffn_conv_b[layer], ffn_w_down[layer], None)
    return rmsnorm(xl, final_norm_g)


DEPTH_2 = 1

HEAD_DIM = 64
BRANCH_WIDTH = D_MODEL // 2
N_BRANCHES = 4
Q_BLOCK = 128
FOX_HEADS = BRANCH_WIDTH // HEAD_DIM
LRU_BLOCKS = 8
LRU_BLOCK_DIM = BRANCH_WIDTH // LRU_BLOCKS
CONV_WIDTH = 4
LRU_C = 8.0
NSA_HEADS = BRANCH_WIDTH // HEAD_DIM
NSA_KV_HEADS = 2
NSA_GROUP = NSA_HEADS // NSA_KV_HEADS
NSA_KV_WIDTH = NSA_KV_HEADS * HEAD_DIM
CMP_BLOCK = 32
CMP_STRIDE = 16
CMP_HIDDEN = 2 * HEAD_DIM
SLC_BLOCK = 64
SLC_TOPK = 16
SLC_LOCAL = 2
SLC_FORCE_SCORE = 1e6
WINDOW = 512
SG_CHUNK = 128
SG_GROUPS = 8
SG_GROUP_DIM = BRANCH_WIDTH // SG_GROUPS

NORM_EPS = 1e-6
NEG_INF = -1e30


def _in_split_sizes():
    W = BRANCH_WIDTH
    return (W, W, W, FOX_HEADS, W,
            W, W,
            W, NSA_KV_WIDTH, NSA_KV_WIDTH, NSA_KV_WIDTH,
            NSA_KV_WIDTH, NSA_KV_WIDTH, NSA_KV_WIDTH,
            3 * NSA_HEADS, W,
            W, W, W,
            N_BRANCHES * D_MODEL)

def rms_norm(x, g):
    x32 = x.astype(jnp.float32)
    y = x32 * lax.rsqrt(jnp.mean(x32 * x32, axis=-1, keepdims=True) + NORM_EPS)
    return (y * g.astype(jnp.float32)).astype(x.dtype)

def layer_norm(x, g):
    x32 = x.astype(jnp.float32)
    mu = jnp.mean(x32, axis=-1, keepdims=True)
    xc = x32 - mu
    y = xc * lax.rsqrt(jnp.mean(xc * xc, axis=-1, keepdims=True) + NORM_EPS)
    return (y * g.astype(jnp.float32)).astype(x.dtype)

def masked_softmax(s, mask):
    p = jax.nn.softmax(jnp.where(mask, s, NEG_INF), axis=-1)
    return jnp.where(mask, p, 0.0)

def fox_attention(q, k, v, f_logit):
    B, S, H, dh = q.shape
    n_blk = S // Q_BLOCK
    scale = 1.0 / math.sqrt(dh)
    c = jnp.cumsum(jax.nn.log_sigmoid(f_logit.astype(jnp.float32)), axis=1)
    c_k = c.transpose(0, 2, 1)[:, :, None, :]
    qb = q.reshape(B, n_blk, Q_BLOCK, H, dh).transpose(1, 0, 2, 3, 4)
    cb = c.reshape(B, n_blk, Q_BLOCK, H).transpose(1, 0, 2, 3)
    pos_k = jnp.arange(S)

    def block(args):
        q_i, c_i, i = args
        t = i * Q_BLOCK + jnp.arange(Q_BLOCK)
        s = jnp.einsum('bqhd,bkhd->bhqk', q_i, k).astype(jnp.float32) * scale
        s = s + c_i.transpose(0, 2, 1)[..., None] - c_k
        p = masked_softmax(s, pos_k[None, :] <= t[:, None])
        return jnp.einsum('bhqk,bkhd->bqhd', p.astype(v.dtype), v)

    out = lax.map(block, (qb, cb, jnp.arange(n_blk)))
    return out.transpose(1, 0, 2, 3, 4).reshape(B, S, H, dh)

def rg_lru(xb, conv_w, conv_b, w_a, b_a, w_x, b_x, lam):
    B, S, W = xb.shape
    xc = lax.conv_general_dilated(
        xb, conv_w.reshape(CONV_WIDTH, 1, W).astype(xb.dtype), window_strides=(1,),
        padding=[(CONV_WIDTH - 1, 0)], dimension_numbers=('NWC', 'WIO', 'NWC'),
        feature_group_count=W) + conv_b
    xh = xc.reshape(B, S, LRU_BLOCKS, LRU_BLOCK_DIM)
    r = jax.nn.sigmoid((jnp.einsum('bsnd,nde->bsne', xh, w_a).reshape(B, S, W) + b_a).astype(jnp.float32))
    i_g = jax.nn.sigmoid((jnp.einsum('bsnd,nde->bsne', xh, w_x).reshape(B, S, W) + b_x).astype(jnp.float32))
    log_a = -LRU_C * r * jax.nn.softplus(-lam.astype(jnp.float32))
    a = jnp.exp(log_a)
    b = jnp.sqrt(-jnp.expm1(2.0 * log_a)) * (i_g * xc.astype(jnp.float32))

    def combine(left, right):
        a_l, b_l = left
        a_r, b_r = right
        return a_l * a_r, a_r * b_l + b_r

    _, h = lax.associative_scan(combine, (a, b), axis=1)
    return h.astype(xb.dtype)

def _cmp_slc_overlap(n_cmp, n_slc):
    c0 = np.arange(n_cmp) * CMP_STRIDE
    s0 = np.arange(n_slc) * SLC_BLOCK
    ov = np.minimum(c0[:, None] + CMP_BLOCK, s0[None, :] + SLC_BLOCK) - np.maximum(c0[:, None], s0[None, :])
    return (np.clip(ov, 0, None) / CMP_BLOCK).astype(np.float32)

def nsa_attention(q, k_cmp, v_cmp, k_slc, v_slc, k_win, v_win, gates,
                  kn_g, cmp_pos, wk1, wk2, wv1, wv2):
    B, S, H, dh = q.shape
    G, R = NSA_KV_HEADS, NSA_GROUP
    scale = 1.0 / math.sqrt(dh)
    n_cmp = (S - CMP_BLOCK) // CMP_STRIDE + 1
    blk_idx = np.arange(n_cmp)[:, None] * CMP_STRIDE + np.arange(CMP_BLOCK)[None, :]
    cmp_end = jnp.asarray(blk_idx[:, -1])

    def compress(t, w1, w2):
        tb = t[:, blk_idx] + cmp_pos[None, None, :, None, :]
        tb = tb.transpose(0, 1, 3, 2, 4).reshape(B, n_cmp, G, CMP_BLOCK * dh)
        return jax.nn.silu(tb @ w1) @ w2

    k_c = rms_norm(compress(k_cmp, wk1, wk2), kn_g)
    v_c = compress(v_cmp, wv1, wv2)
    n_slc = S // SLC_BLOCK
    top_k = min(SLC_TOPK, n_slc)
    overlap = jnp.asarray(_cmp_slc_overlap(n_cmp, n_slc))
    ks_blk = rms_norm(k_slc, kn_g).reshape(B, n_slc, SLC_BLOCK, G, dh).transpose(0, 3, 1, 2, 4)
    vs_blk = v_slc.reshape(B, n_slc, SLC_BLOCK, G, dh).transpose(0, 3, 1, 2, 4)
    kw_pad = jnp.pad(rms_norm(k_win, kn_g), ((0, 0), (WINDOW, 0), (0, 0), (0, 0)))
    vw_pad = jnp.pad(v_win, ((0, 0), (WINDOW, 0), (0, 0), (0, 0)))
    span = WINDOW + Q_BLOCK

    n_blk = S // Q_BLOCK
    qg = q.reshape(B, n_blk, Q_BLOCK, G, R, dh).transpose(1, 0, 2, 3, 4, 5)
    gb = gates.reshape(B, n_blk, Q_BLOCK, 3, H).transpose(1, 0, 2, 3, 4)
    b_ix = jnp.arange(B)[:, None, None, None]
    g_ix = jnp.arange(G)[None, :, None, None]
    j = jnp.arange(n_slc)

    def block(args):
        q_i, g_i, i = args
        t = i * Q_BLOCK + jnp.arange(Q_BLOCK)
        s_c = jnp.einsum('bqgrd,bcgd->bgrqc', q_i, k_c).astype(jnp.float32) * scale
        p_c = masked_softmax(s_c, cmp_end[None, :] <= t[:, None])
        o_c = jnp.einsum('bgrqc,bcgd->bqgrd', p_c.astype(v_c.dtype), v_c)
        imp = jnp.einsum('bgrqc,cj->bgqj', p_c, overlap)
        jt = t // SLC_BLOCK
        valid = j[None, :] <= jt[:, None]
        forced = (j[None, :] == 0) | (valid & (j[None, :] > jt[:, None] - SLC_LOCAL))
        score = jnp.where(forced, SLC_FORCE_SCORE, jnp.where(valid, imp, -1.0))
        top_val, top_idx = lax.top_k(score, top_k)
        k_sel = ks_blk[b_ix, g_ix, top_idx]
        v_sel = vs_blk[b_ix, g_ix, top_idx]
        key_pos = top_idx[..., None] * SLC_BLOCK + jnp.arange(SLC_BLOCK)
        m_s = (top_val >= 0.0)[..., None] & (key_pos <= t[None, None, :, None, None])
        s_s = jnp.einsum('bqgrd,bgqkld->bgrqkl', q_i, k_sel).astype(jnp.float32) * scale
        n_sel = top_k * SLC_BLOCK
        p_s = masked_softmax(s_s.reshape(B, G, R, Q_BLOCK, n_sel), m_s.reshape(B, G, 1, Q_BLOCK, n_sel))
        o_s = jnp.einsum('bgrqn,bgqnd->bqgrd', p_s.astype(v_sel.dtype),
                         v_sel.reshape(B, G, Q_BLOCK, n_sel, dh))
        k_wi = lax.dynamic_slice_in_dim(kw_pad, i * Q_BLOCK, span, axis=1)
        v_wi = lax.dynamic_slice_in_dim(vw_pad, i * Q_BLOCK, span, axis=1)
        pos_w = i * Q_BLOCK - WINDOW + jnp.arange(span)
        m_w = (pos_w[None, :] >= 0) & (pos_w[None, :] <= t[:, None]) & (pos_w[None, :] > t[:, None] - WINDOW)
        s_w = jnp.einsum('bqgrd,bkgd->bgrqk', q_i, k_wi).astype(jnp.float32) * scale
        p_w = masked_softmax(s_w, m_w)
        o_w = jnp.einsum('bgrqk,bkgd->bqgrd', p_w.astype(v_wi.dtype), v_wi)
        g = g_i.reshape(B, Q_BLOCK, 3, G, R)[..., None]
        return g[:, :, 0] * o_c + g[:, :, 1] * o_s + g[:, :, 2] * o_w

    out = lax.map(block, (qg, gb, jnp.arange(n_blk)))
    return out.transpose(1, 0, 2, 3, 4, 5).reshape(B, S, H * dh)

def spatial_gating(u, v, ln_g, w_s, b_s):
    B, S, W = u.shape
    n_chunk = S // SG_CHUNK
    u = jax.nn.gelu(u, approximate=False)
    v = layer_norm(jax.nn.gelu(v, approximate=False), ln_g)
    vc = v.reshape(B, n_chunk, SG_CHUNK, SG_GROUPS, SG_GROUP_DIM)
    causal = jnp.tril(jnp.ones((SG_CHUNK, SG_CHUNK), dtype=w_s.dtype))
    mixed = jnp.einsum('gts,bcsgd->bctgd', w_s * causal, vc) + b_s.T[None, None, :, :, None]
    return u * mixed.reshape(B, S, W)

def hybrid_layer(x, norm_g, w_in, b_forget, qn_a, kn_a, conv_w, conv_b, w_rg_a, b_rg_a,
                 w_rg_x, b_rg_x, lru_lambda, qn_c, kn_c, cmp_pos, cmp_k_w1, cmp_k_w2,
                 cmp_v_w1, cmp_v_w2, ln_v_g, w_spatial, b_spatial, w_branch, w_out):
    B, S, D = x.shape
    W = BRANCH_WIDTH
    xn = rms_norm(x, norm_g)
    z = xn @ w_in
    split_at = np.cumsum(_in_split_sizes())[:-1].tolist()
    (qa, ka, va, fa, ga, xb, gb, qc, kcc, vcc, ksc, vsc, kwc, vwc, gate_c, gc,
     ud, vd, gd, mg) = jnp.split(z, split_at, axis=-1)
    heads = lambda t, n: t.reshape(B, S, n, HEAD_DIM)
    y_a = fox_attention(rms_norm(heads(qa, FOX_HEADS), qn_a), rms_norm(heads(ka, FOX_HEADS), kn_a),
                        heads(va, FOX_HEADS), fa + b_forget).reshape(B, S, W)
    y_b = rg_lru(xb, conv_w, conv_b, w_rg_a, b_rg_a, w_rg_x, b_rg_x, lru_lambda)
    y_c = nsa_attention(rms_norm(heads(qc, NSA_HEADS), qn_c),
                        heads(kcc, NSA_KV_HEADS), heads(vcc, NSA_KV_HEADS),
                        heads(ksc, NSA_KV_HEADS), heads(vsc, NSA_KV_HEADS),
                        heads(kwc, NSA_KV_HEADS), heads(vwc, NSA_KV_HEADS),
                        jax.nn.sigmoid(gate_c).reshape(B, S, 3, NSA_HEADS),
                        kn_c, cmp_pos, cmp_k_w1, cmp_k_w2, cmp_v_w1, cmp_v_w2)
    y_d = spatial_gating(ud, vd, ln_v_g, w_spatial, b_spatial)
    ys = jnp.stack([y_a * jax.nn.silu(ga), y_b * jax.nn.silu(gb),
                    y_c * jax.nn.silu(gc), y_d * jax.nn.silu(gd)], axis=2)
    proj = jnp.einsum('bsnw,nwd->bsnd', ys, w_branch)
    merged = jnp.sum(jax.nn.sigmoid(mg.reshape(B, S, N_BRANCHES, D)) * proj, axis=2)
    return x + merged @ w_out

def second_inputs(seed: int = 0) -> dict:
    key = jax.random.key(seed)
    ks = iter(jax.random.split(key, 32))
    L, D, W, dh = DEPTH_2, D_MODEL, BRANCH_WIDTH, HEAD_DIM

    def nrm(shape, scale):
        return jax.random.normal(next(ks), shape, jnp.float32) * scale

    w_in_width = sum(_in_split_sizes())
    x = nrm((BATCH, SEQ, D), 1.0)
    norm_g = 1.0 + nrm((L, D), 0.05)
    w_in = nrm((L, D, w_in_width), D ** -0.5)
    b_forget = 3.0 + nrm((L, FOX_HEADS), 0.5)
    qn_a = 1.0 + nrm((L, dh), 0.05)
    kn_a = 1.0 + nrm((L, dh), 0.05)
    conv_w = nrm((L, CONV_WIDTH, W), CONV_WIDTH ** -0.5)
    conv_b = nrm((L, W), 0.01)
    w_rg_a = nrm((L, LRU_BLOCKS, LRU_BLOCK_DIM, LRU_BLOCK_DIM), LRU_BLOCK_DIM ** -0.5)
    b_rg_a = nrm((L, W), 0.01)
    w_rg_x = nrm((L, LRU_BLOCKS, LRU_BLOCK_DIM, LRU_BLOCK_DIM), LRU_BLOCK_DIM ** -0.5)
    b_rg_x = nrm((L, W), 0.01)
    a_c = jax.random.uniform(next(ks), (L, W), jnp.float32, 0.9, 0.999)
    a0 = a_c ** (1.0 / LRU_C)
    lru_lambda = jnp.log(a0) - jnp.log1p(-a0)
    qn_c = 1.0 + nrm((L, dh), 0.05)
    kn_c = 1.0 + nrm((L, dh), 0.05)
    cmp_pos = nrm((L, CMP_BLOCK, dh), 0.02)
    cmp_k_w1 = nrm((L, CMP_BLOCK * dh, CMP_HIDDEN), (CMP_BLOCK * dh) ** -0.5)
    cmp_k_w2 = nrm((L, CMP_HIDDEN, dh), CMP_HIDDEN ** -0.5)
    cmp_v_w1 = nrm((L, CMP_BLOCK * dh, CMP_HIDDEN), (CMP_BLOCK * dh) ** -0.5)
    cmp_v_w2 = nrm((L, CMP_HIDDEN, dh), CMP_HIDDEN ** -0.5)
    ln_v_g = 1.0 + nrm((L, W), 0.05)
    w_spatial = nrm((L, SG_GROUPS, SG_CHUNK, SG_CHUNK), SG_CHUNK ** -0.5)
    b_spatial = 1.0 + nrm((L, SG_GROUPS, SG_CHUNK), 0.1)
    w_branch = nrm((L, N_BRANCHES, W, D), W ** -0.5)
    w_out = nrm((L, D, D), D ** -0.5)
    return {"x": x, "norm_g": norm_g, "w_in": w_in, "b_forget": b_forget, "qn_a": qn_a,
            "kn_a": kn_a, "conv_w": conv_w, "conv_b": conv_b, "w_rg_a": w_rg_a,
            "b_rg_a": b_rg_a, "w_rg_x": w_rg_x, "b_rg_x": b_rg_x, "lru_lambda": lru_lambda,
            "qn_c": qn_c, "kn_c": kn_c, "cmp_pos": cmp_pos, "cmp_k_w1": cmp_k_w1,
            "cmp_k_w2": cmp_k_w2, "cmp_v_w1": cmp_v_w1, "cmp_v_w2": cmp_v_w2,
            "ln_v_g": ln_v_g, "w_spatial": w_spatial, "b_spatial": b_spatial,
            "w_branch": w_branch, "w_out": w_out}

def second_block(x, norm_g, w_in, b_forget, qn_a, kn_a, conv_w, conv_b, w_rg_a, b_rg_a,
              w_rg_x, b_rg_x, lru_lambda, qn_c, kn_c, cmp_pos, cmp_k_w1, cmp_k_w2,
              cmp_v_w1, cmp_v_w2, ln_v_g, w_spatial, b_spatial, w_branch, w_out):
    for l in range(DEPTH_2):
        x = hybrid_layer(x, norm_g[l], w_in[l], b_forget[l], qn_a[l], kn_a[l], conv_w[l],
                         conv_b[l], w_rg_a[l], b_rg_a[l], w_rg_x[l], b_rg_x[l], lru_lambda[l],
                         qn_c[l], kn_c[l], cmp_pos[l], cmp_k_w1[l], cmp_k_w2[l], cmp_v_w1[l],
                         cmp_v_w2[l], ln_v_g[l], w_spatial[l], b_spatial[l], w_branch[l], w_out[l])
    return x


def setup_inputs(seed=0):
    out = dict(first_inputs(seed))
    for name, value in second_inputs(seed + 1).items():
        if name != "x":
            out[name + "_2"] = value
    return out


def reference(
    x, c, ctx, c_ctx, mod_w, mod_b, norm_mix_g, norm_ffn_g, final_norm_g, ffn_w_up, ffn_conv_w,
    ffn_conv_b, ffn_w_down, even_w_in, gla_a1, gla_a2, gla_ab, ml_conv_w, ml_conv_b, ml_gate_b,
    gla_norm_g, ml_norm_g, even_w_out, ssd_w_in, ssd_conv_w, ssd_conv_b, ssd_dt_bias, ssd_a_log,
    ssd_d, ssd_norm_g, ssd_w_out, norm_g_2, w_in_2, b_forget_2, qn_a_2, kn_a_2, conv_w_2,
    conv_b_2, w_rg_a_2, b_rg_a_2, w_rg_x_2, b_rg_x_2, lru_lambda_2, qn_c_2, kn_c_2, cmp_pos_2,
    cmp_k_w1_2, cmp_k_w2_2, cmp_v_w1_2, cmp_v_w2_2, ln_v_g_2, w_spatial_2, b_spatial_2,
    w_branch_2, w_out_2,
):
    x = first_block(
        x, c, ctx, c_ctx, mod_w, mod_b, norm_mix_g, norm_ffn_g, final_norm_g, ffn_w_up,
        ffn_conv_w, ffn_conv_b, ffn_w_down, even_w_in, gla_a1, gla_a2, gla_ab, ml_conv_w,
        ml_conv_b, ml_gate_b, gla_norm_g, ml_norm_g, even_w_out, ssd_w_in, ssd_conv_w,
        ssd_conv_b, ssd_dt_bias, ssd_a_log, ssd_d, ssd_norm_g, ssd_w_out,
    )
    return second_block(
        x, norm_g_2, w_in_2, b_forget_2, qn_a_2, kn_a_2, conv_w_2, conv_b_2, w_rg_a_2, b_rg_a_2,
        w_rg_x_2, b_rg_x_2, lru_lambda_2, qn_c_2, kn_c_2, cmp_pos_2, cmp_k_w1_2, cmp_k_w2_2,
        cmp_v_w1_2, cmp_v_w2_2, ln_v_g_2, w_spatial_2, b_spatial_2, w_branch_2, w_out_2,
    )


_drawn_inputs = setup_inputs


def setup_inputs(seed=0):
    import zlib

    import numpy as np

    out = dict(_drawn_inputs(seed))
    spreads = {}
    factors = {'norm_ffn_g': 2.996,
     'ffn_conv_b': 6.872,
     'gla_ab': 7.436,
     'ml_conv_b': 8.0,
     'gla_norm_g': 7.282,
     'ml_norm_g': 3.371,
     'ssd_conv_b': 6.172,
     'ssd_d': 6.419,
     'ssd_norm_g': 3.463,
     'b_forget_2': 21.368,
     'qn_a_2': 8.0,
     'kn_a_2': 8.0,
     'conv_b_2': 5.325,
     'b_rg_a_2': 180.331,
     'b_rg_x_2': 62.397,
     'qn_c_2': 8.0,
     'kn_c_2': 8.0,
     'cmp_pos_2': 29.034,
     'ln_v_g_2': 7.893,
     'b_spatial_2': 2.904}
    for name, (base, spread) in spreads.items():
        noise = np.random.default_rng([zlib.crc32(name.encode()), seed]).standard_normal(out[name].shape)
        drawn = base * np.exp(spread * noise) if base else spread * noise
        out[name] = jnp.asarray(drawn.astype(out[name].dtype))
    for name, factor in factors.items():
        out[name] = (out[name] * factor).astype(out[name].dtype)
    return out
```

```python
from contextlib import ExitStack

import numpy as np

import concourse.bass as bass
from concourse import mybir

F32 = mybir.dt.float32
I32 = mybir.dt.int32
ALU = mybir.AluOpType
ACT = mybir.ActivationFunctionType
AX = mybir.AxisListType

P = 128
D = 1024
KD = D // P
CTX, LAT = 256, 256
T = CTX + LAT
TT = T // P
LT = LAT // P
GRID_W = 64
ROWS = LAT // GRID_W
EPS = 1e-6
FF = 2816
KF = FF // P
GH, GK, GV = 4, 64, 128
GW = GH * GV
GLEVELS = 7
GTAU = 16.0
MH, MD = 4, 128
SH, SP, SN, SG = 32, 64, 128, 4
SI = SH * SP
KI = SI // P
HD = 64
NH = 8
BW = 512
KB = BW // P
CB, CS = 32, 16
NC = (LAT - CB) // CS + 1
BANKS = 8
TPB = 8
RING = 10

SEGMENTS = [
    ("mod0", 48 * KD), ("even_in", 28 * KD), ("even_out", 8 * 8), ("up0", 2 * KF * KD), ("down0", 8 * KF),
    ("mod1", 48 * KD), ("ssd_in", 40 * KD), ("ssd_out", 8 * KI), ("up1", 2 * KF * KD), ("down1", 8 * KF),
    ("in2", 84 * KD), ("branch2", 8 * 4 * KB), ("out2", 8 * KD),
]
FIRST_TILE = {}
_n = 0
for _name, _count in SEGMENTS:
    FIRST_TILE[_name] = _n
    _n += _count
    assert _count % TPB == 0
N_BLOCKS = _n // TPB

COLUMNS = [
    ("mod_b0", 48), ("mod_b1", 48), ("mix_g0", 8), ("mix_g1", 8), ("ffn_g0", 8), ("ffn_g1", 8), ("final_g", 8),
    ("conv_w0", 9 * 44), ("conv_w1", 9 * 44), ("conv_b0", 44), ("conv_b1", 44), ("gla_ab", 4),
    ("ml_conv_w", 24), ("ml_conv_b", 8), ("gla_norm", 4), ("ml_norm", 4), ("ml_li_b", 1), ("ml_lf_b", 1),
    ("ssd_conv_w", 72), ("ssd_conv_b", 24), ("ssd_d", 16), ("ssd_norm", 16), ("ssd_dt_b", 1), ("ssd_a_log", 1),
    ("norm2", 8), ("qn_a", 1), ("kn_a", 1), ("qn_c", 1), ("kn_c", 1), ("b_forget", 1), ("lru_conv_w", 16),
    ("lru_conv_b", 4), ("b_rg_a", 4), ("b_rg_x", 4), ("lam", 4), ("cmp_pos", 32), ("cond", 16),
]
COL = {}
_n = 0
for _name, _count in COLUMNS:
    COL[_name] = _n
    _n += _count
N_COLS = _n


class Count:

    def __init__(self, sem):
        self.sem, self.base, self.total = sem, 0, 0

    def up(self, n=1):
        self.total += n
        return self.sem, n

    def at(self, n):
        return self.sem, self.base + n

    def now(self):
        return self.sem, self.total


class Kit:

    def __init__(self, nc, ctx, dram):
        self.nc, self.dram = nc, dram

        def sb(name, shape):
            return ctx.enter_context(nc.sbuf_tensor(name, shape, F32))

        self.ring = sb("weight_ring", [P, RING, TPB * P])
        self.x = sb("x", [P, KD, T])
        self.h = sb("h", [P, KD, T])
        self.cols = sb("columns", [P, N_COLS])
        self.mod = sb("modulation", [P, 2, 48, 2])
        self.ident = sb("identity", [P, P])
        self.ones = sb("ones", [P, P])
        self.head_ones = sb("head_ones", [P, P])
        self.tri_f = sb("tri_f", [P, P])
        self.tri_b = sb("tri_b", [P, P])
        self.small = sb("small", [P, 8])
        self.arena = sb("arena", [P, ARENA])
        self.bank = ctx.enter_context(nc.psum_tensor("banks", [P, BANKS, 512], F32))
        self.loaded = [Count(ctx.enter_context(nc.semaphore(f"weights_loaded{i}"))) for i in range(RING)]
        self.used = Count(ctx.enter_context(nc.semaphore("weights_used")))
        self.done = Count(ctx.enter_context(nc.semaphore("products_done")))
        self.release = {}
        self.pool = [Count(ctx.enter_context(nc.semaphore(f"stage_signal{i}"))) for i in range(40)]
        self.free = list(self.pool)
        self.issued = 0
        self.top = 0

    def col(self, name, i=0, n=1, rows=slice(0, P)):
        return self.cols[rows, COL[name] + i:COL[name] + i + n]

    def issued_tile(self):
        return max(0, self.issued - RING) * TPB

    def counts(self, n):
        return [self.free.pop() for _ in range(n)]

    def stage_end(self):
        for s in self.pool:
            s.base = s.total
        self.free = list(self.pool)

    def take(self, *shape):
        n = int(np.prod(shape))
        assert self.top + n <= ARENA, (self.top, n, ARENA)
        a = self.arena[:, self.top:self.top + n]
        self.top += n
        names = "abcd"[:len(shape)]
        if len(shape) > 1:
            a = a.rearrange(f"p ({' '.join(names)}) -> p {' '.join(names)}", **dict(zip(names[1:], shape[1:])))
        return a

    def wtile(self, tile, n=1):
        block, at = tile // TPB, tile % TPB
        return self.ring[:, block % RING, at * P:(at + n) * P]


ARENA = 32400


def load_weights(K, sync, last_tile):
    last = min(N_BLOCKS, last_tile // TPB + RING)
    while K.issued < last:
        b = K.issued
        if b >= RING:
            sync.wait_ge(*K.release[b - RING])
        sync.dma_start(K.ring[:, b % RING, :], K.dram["weights"][b]).then_inc(K.loaded[b % RING].sem, 16)
        K.issued += 1


class Link:

    def __init__(self, eng, step):
        self.eng, self.step = eng, step

    def __call__(self, ins):
        ins.then_inc(*self.step.up())
        self.eng.wait_ge(*self.step.now())


def bc(ap, shape):
    return ap.broadcast_to(shape)


def mid(ap, n):
    return ap.unsqueeze(1).broadcast_to([ap.shape[0], n, ap.shape[1]])


def last(ap, n):
    return ap.unsqueeze(2).broadcast_to([ap.shape[0], ap.shape[1], n])



class Product:

    def __init__(self, out, lhsT, rhs, start, stop, tile=None, ends=None):
        self.out, self.lhsT, self.rhs, self.start, self.stop = out, lhsT, rhs, start, stop
        self.tile, self.ends = tile, ends


class Item:

    def __init__(self, products, empty, on="act", conv=None):
        self.products, self.empty, self.on, self.conv = products, empty, on, conv


class Conv:

    def __init__(self, n, centre, bias, taps, finish, post=None):
        self.n, self.centre, self.bias, self.taps, self.finish, self.post = n, centre, bias, taps, finish, post


def tile_products(K, tile, nk, rhs, n):
    return [Product(lambda o: o[:, 0:n], K.wtile(tile + k), rhs(k), k == 0, k == nk - 1, tile + k,
                    (tile + k) // TPB if (tile + k) % TPB == TPB - 1 else None) for k in range(nk)]


def own_products(pairs, m, n):
    return [Product(lambda o: o[0:m, 0:n], a, b, i == 0, i == len(pairs) - 1) for i, (a, b) in enumerate(pairs)]


def token_products(K, tile, tokens, width):
    n = width // P
    groups = [[] for _ in tokens]
    for k in range(KD):
        t = tile + k * n
        for i, tok in enumerate(tokens):
            ends = t // TPB if i == len(tokens) - 1 and (t + n) % TPB == 0 else None
            groups[i].append(Product(lambda o: o[:, 0:width], K.h[:, k, tok * P:tok * P + P], K.wtile(t, n),
                                     k == 0, k == KD - 1, t, ends))
    return groups


def run_products(K, rounds, last_tile):
    nc = K.nc
    free_act, free_dve, tapped, finished, posted, vector_step = K.counts(6)
    items = [it for r in rounds for it in r]
    free = {"act": free_act, "dve": free_dve}
    rank, count = [], {"act": 0, "dve": 0}
    for it in items:
        count[it.on] += 1
        rank.append(count[it.on])
    convs = [e for e, it in enumerate(items) if it.conv]
    RAW, ACC, LAG = 4, 8, 2
    finishes = np.cumsum([items[e].conv.finish is not None for e in convs]).tolist()
    posts = np.cumsum([items[e].conv.post is not None for e in convs]).tolist()
    if convs:
        raw, acc = K.take(RAW, T), K.take(ACC, T)
    done0 = K.done.total

    with nc.Block() as block:
        @block.tensor
        def _(pe):
            e, block_seen = 0, -1
            for r in rounds:
                for j in range(len(r)):
                    if e + j >= BANKS:
                        q = e + j - BANKS
                        pe.wait_ge(*free[items[q].on].at(rank[q]))
                for k in range(len(r[0].products)):
                    for j, it in enumerate(r):
                        p = it.products[k]
                        if p.tile is not None and p.tile // TPB != block_seen:
                            block_seen = p.tile // TPB
                            pe.wait_ge(K.loaded[block_seen % RING].sem, 16 * (block_seen // RING + 1))
                        mm = pe.matmul(p.out(K.bank[:, (e + j) % BANKS, :]), p.lhsT, p.rhs,
                                       start=p.start, stop=p.stop)
                        signal = K.done if k == len(it.products) - 1 else K.used if p.ends is not None else None
                        if signal is not None:
                            mm.then_inc(*signal.up())
                        if p.ends is not None:
                            K.release[p.ends] = signal.now()
                e += len(r)

        @block.sync
        def _(sync):
            load_weights(K, sync, last_tile)

        @block.scalar
        def _(act):
            def finish(i):
                c = items[convs[i]].conv
                if c.finish is None:
                    return
                act.wait_ge(*tapped.at(i + 1))
                c.finish(act, acc[:, i % ACC, 0:c.n]).then_inc(*finished.up())

            n_conv = 0
            for e, it in enumerate(items):
                if it.on != "act":
                    continue
                act.wait_ge(K.done.sem, done0 + e + 1)
                bank = K.bank[:, e % BANKS, :]
                if not it.conv:
                    it.empty(act, bank).then_inc(*free_act.up())
                    continue
                c, i = it.conv, n_conv
                if i >= RAW:
                    act.wait_ge(*tapped.at(i - RAW + 1))
                if i >= ACC:
                    old = posts[i - ACC + 1] if items[convs[i - ACC + 1]].conv.post else posts[i - ACC]
                    if old:
                        act.wait_ge(*posted.at(old))
                act.activation(acc[:, i % ACC, 0:c.n], bank[:, 0:c.n], ACT.Identity, bias=c.bias, scale=c.centre)
                act.activation(raw[:, i % RAW, 0:c.n], bank[:, 0:c.n], ACT.Copy).then_inc(*free_act.up())
                n_conv += 1
                if i >= LAG:
                    finish(i - LAG)
            for i in range(max(0, n_conv - LAG), n_conv):
                finish(i)

        @block.vector
        def _(dve):
            def post(i):
                c = items[convs[i]].conv
                if c.post is not None:
                    dve.wait_ge(*finished.at(finishes[i]))
                    c.post(dve, acc[:, (i - 1) % ACC, 0:c.n], acc[:, i % ACC, 0:c.n]).then_inc(*posted.up())

            link = Link(dve, vector_step)
            i = 0
            for e, it in enumerate(items):
                if it.on == "dve":
                    dve.wait_ge(K.done.sem, done0 + e + 1)
                    it.empty(dve, link, K.bank[:, e % BANKS, :]).then_inc(*free_dve.up())
                    dve.wait_ge(*free_dve.now())
                if it.conv:
                    dve.wait_ge(*free_act.at(rank[e]))
                    for t, (region, shift, w) in enumerate(it.conv.taps):
                        o = region(acc[:, i % ACC, 0:it.conv.n])
                        ins = dve.scalar_tensor_tensor(o, shift(raw[:, i % RAW, 0:it.conv.n]), w, o, ALU.mult, ALU.add)
                        if t == len(it.conv.taps) - 1:
                            ins.then_inc(*tapped.up())
                        else:
                            link(ins)
                    if i >= LAG + 1:
                        post(i - LAG - 1)
                    i += 1
            for j in range(max(0, i - LAG - 1), i):
                post(j)
    K.stage_end()


def conv_taps_1d(w, n_regions=2):
    def view(a):
        return a.rearrange("p (r t) -> p r t", r=n_regions)
    n = 256
    return [(lambda o: view(o)[:, :, 1:n], lambda r: view(r)[:, :, 0:n - 1], w(0)),
            (lambda o: view(o)[:, :, 0:n - 1], lambda r: view(r)[:, :, 1:n], w(2))]


def conv_taps_ffn(w, with_ctx):
    taps = []
    lat0 = CTX if with_ctx else 0

    def grid(a, r0, r1, c0, c1):
        return a[:, lat0:lat0 + LAT].rearrange("p (r c) -> p r c", c=GRID_W)[:, r0:r1, c0:c1]

    for i in range(3):
        for j in range(3):
            if i == 1 and j == 1:
                continue
            di, dj = i - 1, j - 1
            r0, r1 = max(0, -di), ROWS - max(0, di)
            c0, c1 = max(0, -dj), GRID_W - max(0, dj)
            taps.append((lambda o, r0=r0, r1=r1, c0=c0, c1=c1: grid(o, r0, r1, c0, c1),
                         lambda a, r0=r0 + di, r1=r1 + di, c0=c0 + dj, c1=c1 + dj: grid(a, r0, r1, c0, c1),
                         w(3 * i + j)))
    if with_ctx:
        taps.append((lambda o: o[:, 1:CTX], lambda a: a[:, 0:CTX - 1], w(3)))
        taps.append((lambda o: o[:, 0:CTX - 1], lambda a: a[:, 1:CTX], w(5)))
    return taps


REGIONS = [(0, CTX, 1), (CTX, T, 0)]


def residual_items(K, segment, nk, rhs, t0, gate):
    items = []
    for n in range(KD):
        def empty(dve, link, bank, n=n):
            for a, b, which in REGIONS:
                if a < t0:
                    continue
                xs, ps = K.x[:, n, a:b], bank[:, a - t0:b - t0]
                if gate is None:
                    ins = dve.tensor_tensor(xs, ps, xs, ALU.add)
                else:
                    ins = dve.scalar_tensor_tensor(xs, ps, gate(n, which), xs, ALU.mult, ALU.add)
            return ins
        items.append([Item(tile_products(K, FIRST_TILE[segment] + n * nk, nk, rhs, T - t0), empty, "dve")])
    return items


def normalise(K, t0, out, gain, shift_scale=None):
    nc, n = K.nc, T - t0
    squared, summed, rooted, scaled, normed, vector_step = K.counts(6)
    mark = K.top
    sq, std, rstd, amp = K.take(KD, n), K.take(n), K.take(n), K.take(2, KD)

    with nc.Block() as block:
        @block.scalar
        def _(act):
            for k in range(KD):
                act.activation(sq[:, k, :], K.x[:, k, t0:T], ACT.Square).then_inc(*squared.up())
            act.wait_ge(*summed.at(1))
            act.activation(std, K.bank[:, 0, 0:n], ACT.Sqrt, bias=K.small[:, 0:1], scale=1.0 / D).then_inc(*rooted.up())
            if shift_scale:
                layer, shift, scale = shift_scale
                act.wait_ge(*scaled.at(1))
                for k in range(KD):
                    act.wait_ge(*normed.at(k + 1))
                    for a, b, which in REGIONS:
                        if a >= t0:
                            act.activation(out(k)[:, a - t0:b - t0], out(k)[:, a - t0:b - t0], ACT.Identity,
                                           bias=K.mod[:, layer, shift + k, which:which + 1],
                                           scale=amp[:, which, k:k + 1])

        @block.tensor
        def _(pe):
            for k in range(KD):
                pe.wait_ge(*squared.at(k + 1))
                mm = pe.matmul(K.bank[:, 0, 0:n], K.ones[:], sq[:, k, :], start=(k == 0), stop=(k == KD - 1))
            mm.then_inc(*summed.up())

        @block.vector
        def _(dve):
            link = Link(dve, vector_step)
            if shift_scale:
                layer, shift, scale = shift_scale
                for which in range(2):
                    ins = dve.scalar_tensor_tensor(amp[:, which, :], K.mod[:, layer, scale:scale + KD, which], 1.0,
                                                   K.col(gain, 0, KD), ALU.add, ALU.mult)
                ins.then_inc(*scaled.up())
            dve.wait_ge(*rooted.at(1))
            link(dve.reciprocal(rstd, std))
            for k in range(KD):
                if shift_scale:
                    dve.tensor_tensor(out(k), K.x[:, k, t0:T], rstd, ALU.mult).then_inc(*normed.up())
                else:
                    dve.scalar_tensor_tensor(out(k), K.x[:, k, t0:T], K.col(gain, k), rstd, ALU.mult, ALU.mult)

        @block.sync
        def _(sync):
            load_weights(K, sync, K.issued_tile())
    K.top = mark
    K.stage_end()


def setup(K):
    nc = K.nc
    filled, loads = K.counts(2)

    with nc.Block() as block:
        @block.gpsimd
        def _(pool):
            link = Link(pool, filled)
            for i, v in enumerate((EPS, 1.0, 0.0)):
                link(pool.memset(K.small[:, i:i + 1], v))
            for a, v in ((K.ones, 1.0), (K.ident, 0.0), (K.head_ones, 0.0), (K.tri_f, 1.0), (K.tri_b, 1.0)):
                link(pool.memset(a[:], v))
            link(pool.memset(K.head_ones[0:HD, 0:HD], 1.0))
            link(pool.memset(K.head_ones[HD:P, HD:P], 1.0))
            link(pool.affine_select(out=K.ident[:], in_=K.ident[:], compare_op=ALU.not_equal, fill=1.0, base=0,
                                    pattern=[[-1, P]], channel_multiplier=1))
            link(pool.affine_select(out=K.tri_f[:], in_=K.tri_f[:], compare_op=ALU.is_ge, fill=0.0, base=0,
                                    pattern=[[1, P]], channel_multiplier=-1))
            link(pool.affine_select(out=K.tri_b[:], in_=K.tri_b[:], compare_op=ALU.is_ge, fill=0.0, base=0,
                                    pattern=[[-1, P]], channel_multiplier=1))

        @block.sync
        def _(sync):
            sync.dma_start(K.cols[:], K.dram["columns"]).then_inc(*loads.up(16))
            sync.dma_start(K.x[:], K.dram["tokens"]).then_inc(*loads.up(16))
            load_weights(K, sync, 0)
            sync.wait_ge(*loads.at(32))
    K.stage_end()


def modulations(K, layer):
    nc = K.nc
    (silued,) = K.counts(1)
    mark = K.top
    cond = K.take(KD, 2)
    with nc.Block() as block:
        @block.scalar
        def _(act):
            act.activation(cond, K.col("cond", 0, 2 * KD).rearrange("p (k c) -> p k c", c=2), ACT.Silu)
    K.stage_end()
    first = FIRST_TILE[f"mod{layer}"]
    mms = []
    for j in range(48):
        for k in range(KD):
            t = first + j * KD + k
            mms.append(Product(lambda o, j=j: o[:, 2 * j:2 * j + 2], K.wtile(t), cond[:, k, :], k == 0, k == KD - 1,
                               t, t // TPB if t % TPB == TPB - 1 else None))

    def empty(dve, link, bank):
        return dve.tensor_tensor(K.mod[:, layer, :, :], bank[:, 0:96].rearrange("p (j c) -> p j c", c=2),
                                 last(K.col(f"mod_b{layer}", 0, 48), 2), ALU.add)
    run_products(K, [[Item(mms, empty, "dve")]], first + 48 * KD)
    K.top = mark


def feed_forward(K, layer, t0):
    n = T - t0
    normalise(K, t0, lambda k: K.h[:, k, t0:T], f"ffn_g{layer}", (layer, 24, 32))
    mark = K.top
    gated = K.take(KF, n)
    rounds = []
    first = FIRST_TILE[f"up{layer}"]
    for j in range(KF):
        for half in range(2):
            c = half * KF + j

            def finish(act, acc):
                return act.activation(acc, acc, ACT.Silu)

            def post(dve, a, g, j=j):
                return dve.tensor_tensor(gated[:, j, :], a, g, ALU.mult)
            conv = Conv(n, K.col(f"conv_w{layer}", 4 * 44 + c), K.col(f"conv_b{layer}", c),
                        conv_taps_ffn(lambda tap, c=c: K.col(f"conv_w{layer}", tap * 44 + c), t0 == 0),
                        finish if half else None, post if half else None)
            rounds.append([Item(tile_products(K, first + (2 * j + half) * KD, KD, lambda k: K.h[:, k, t0:T], n),
                                None, "act", conv)])
    run_products(K, rounds, first + 2 * KF * KD)
    first = FIRST_TILE[f"down{layer}"]
    rounds = residual_items(K, f"down{layer}", KF, lambda k: gated[:, k, :], t0,
                            lambda m, which: K.mod[:, layer, 40 + m, which:which + 1])
    run_products(K, rounds, first + 8 * KF)
    K.top = mark

def even_mixer(K):
    mark = K.top
    f = {}
    f["gq"], f["gk"], f["gg"] = K.take(2, T), K.take(2, T), K.take(4, T)
    f["mq"], f["mk"] = K.take(4, T), K.take(4, T)
    f["gv"], f["mv"], f["mo"] = K.take(TT, GW), K.take(TT, MH, MD + 1), K.take(TT, GW)
    f["low"], f["li"], f["lf"] = K.take(T), K.take(T), K.take(T)
    cum = K.take(4, T)
    work = K.top
    small, a2 = K.take(KD, 176), K.take(256)
    even_projection(K, f, small, a2)
    gla_decays(K, f, a2, cum)
    K.top = work
    gla(K, f, cum)
    K.top = work
    mlstm(K, f)
    K.top = mark
    first = FIRST_TILE["even_out"]
    run_products(K, residual_items(K, "even_out", KD, lambda k: K.h[:, k, :], 0,
                                   lambda m, which: K.mod[:, 0, 16 + m, which:which + 1]), first + 64)


def even_projection(K, f, small, a2):
    nc = K.nc
    (loads,) = K.counts(1)
    with nc.Block() as block:
        @block.sync
        def _(sync):
            sync.dma_start(small, K.dram["even_small"]).then_inc(*loads.up(16))
            sync.dma_start(a2[0:48, :], K.dram["gla_a2"]).then_inc(*loads.up(16))
            sync.wait_ge(*loads.at(32))

        @block.gpsimd
        def _(pool):
            pool.memset(f["mv"][:, :, :, MD:MD + 1], 1.0)
    K.stage_end()

    first = FIRST_TILE["even_in"]
    rounds, tile = [], first

    def h(k):
        return K.h[:, k, :]

    def put(dest, func, scale=1.0):
        return lambda act, bank: act.activation(dest, bank[0:dest.shape[0], :], func, scale=scale)

    for name, n, func, scale in (("gq", 2, ACT.Copy, GK ** -0.5), ("gk", 2, ACT.Copy, 1.0), ("gg", 4, ACT.Silu, 1.0)):
        for j in range(n):
            rounds.append([Item(tile_products(K, tile, KD, h, T), put(f[name][:, j, :], func, scale))])
            tile += KD
    for name in ("gv", "mv", "mo"):
        groups = token_products(K, tile, range(TT), GW)

        def empty(i, name=name):
            if name == "mv":
                return lambda act, bank: act.activation(f["mv"][:, i, :, 0:MD],
                                                        bank.rearrange("p (h v) -> p h v", v=MD), ACT.Copy)
            return put(f[name][:, i, :], ACT.Sigmoid if name == "mo" else ACT.Copy)
        rounds.append([Item(g, empty(i)) for i, g in enumerate(groups)])
        tile += 4 * KD
    for dest, a, b, func, bias in ((f["low"], 0, 48, None, None), (f["li"], 48, 112, 36, "ml_li_b"),
                                   (f["lf"], 112, 176, 36, "ml_lf_b")):
        m = b - a

        def empty(act, bank, dest=dest, m=m, bias=bias):
            if bias is None:
                return act.activation(dest[0:m, :], bank[0:m, :], ACT.Copy)
            return act.activation(dest[0:m, :], bank[0:m, :], ACT.Identity, bias=K.col(bias, rows=slice(0, m)), scale=1.0)
        rounds.append([Item(own_products([(small[:, k, a:b], h(k)) for k in range(KD)], m, T), empty)])
    for name, base in (("mq", 0), ("mk", 4)):
        for j in range(4):
            c = base + j

            def finish(act, acc, name=name, j=j):
                return act.activation(f[name][:, j, :], acc, ACT.Silu)
            conv = Conv(T, K.col("ml_conv_w", 8 + c), K.col("ml_conv_b", c),
                        conv_taps_1d(lambda tap, c=c: K.col("ml_conv_w", tap * 8 + c)), finish)
            rounds.append([Item(tile_products(K, tile, KD, h, T), None, "act", conv)])
            tile += KD
    top = K.top
    run_products(K, rounds, first + 28 * KD)
    K.top = top


def gla_decays(K, f, a2, la):
    nc = K.nc
    ready, biased, absed, logged, combined, vector_step, scalar_step = K.counts(7)
    e = K.take(4, T)
    z = la
    with nc.Block() as block:
        @block.tensor
        def _(pe):
            for d in range(2):
                for pair in range(2):
                    r = slice(32 * d, 32 * d + 16)
                    pe.matmul(K.bank[:, 2 * d + pair, :], a2[r, pair * P:pair * P + P], f["low"][r, :],
                              start=True, stop=True).then_inc(*ready.up())

        @block.scalar
        def _(act):
            link = Link(act, scalar_step)
            for i in range(4):
                act.wait_ge(*ready.at(i + 1))
                link(act.activation(z[:, i, :], K.bank[:, i, :], ACT.Identity, bias=K.col("gla_ab", i), scale=1.0))
            link(act.activation(e, z, ACT.Abs))
            link(act.activation(e, e, ACT.Exp, scale=-1.0))
            act.activation(e, e, ACT.Ln, bias=K.small[:, 1:2], scale=1.0).then_inc(*logged.up())

        @block.vector
        def _(dve):
            link = Link(dve, vector_step)
            dve.wait_ge(*logged.at(1))
            link(dve.tensor_scalar(z, z, 0.0, 1.0 / GTAU, ALU.min, ALU.mult))
            link(dve.scalar_tensor_tensor(e, e, -1.0 / GTAU, z, ALU.mult, ALU.add))
            for d in range(2):
                for pair in range(2):
                    for c in range(TT):
                        a, o = e[:, 2 * d + pair, c * P:c * P + P], z[:, 2 * d + pair, c * P:c * P + P]
                        if d:
                            a, o = a[:, ::-1], o[:, ::-1]
                        dve.tensor_tensor_scan(o, K.ones[:], a, 0.0, ALU.mult, ALU.add)
    K.stage_end()


CHUNK_ORDER = ([0, 1, 2, 3], [1, 0, 3, 2])


def gla(K, f, cum):
    nc = K.nc
    dp = 4
    factor = K.take(dp, T)
    qe, ke = K.take(dp, T), K.take(dp, T)
    att = K.take(2, TT, 2, P)
    masks = K.take(2 * GLEVELS, P)
    kend_t = K.take(dp, TT, P)
    state = K.take(dp, 3, P)
    cend = K.take(dp, TT)
    qv = lambda: f["gq"].unsqueeze(1).broadcast_to([P, 2, 2, T])
    kv = lambda: f["gk"].unsqueeze(1).broadcast_to([P, 2, 2, T])
    as4 = lambda a: a.rearrange("p (d q) t -> p d q t", q=2)

    (mask_step,) = K.counts(1)
    with nc.Block() as block:
        @block.gpsimd
        def _(pool):
            link = Link(pool, mask_step)
            link(pool.memset(masks, 0.0))
            for d in range(2):
                for l in range(1, GLEVELS + 1):
                    size, half = 1 << l, 1 << (l - 1)
                    m = masks[:, d * GLEVELS + l - 1, :].rearrange("p (b w) -> p b w", w=size)
                    t_half = m[:, :, half:size] if d == 0 else m[:, :, 0:half]
                    s_from = half if d else 0
                    n = P // size
                    link(pool.memset(t_half, 1.0))
                    link(pool.affine_select(out=t_half, in_=t_half, compare_op=ALU.is_ge, fill=0.0, base=-s_from,
                                            pattern=[[-size, n], [0, half]], channel_multiplier=1))
                    link(pool.affine_select(out=t_half, in_=t_half, compare_op=ALU.is_ge, fill=0.0,
                                            base=s_from + half - 1, pattern=[[size, n], [0, half]],
                                            channel_multiplier=-1))
    K.stage_end()

    differences, exps, qe_done, ke_done, read, scored, taken, vector_step, scalar_step = K.counts(9)
    done0 = [0]
    with nc.Block() as block:
        @block.vector
        def _(dve):
            link = Link(dve, vector_step)
            n_bank = 0

            def take_scores(l, d):
                nonlocal n_bank
                for i in range(4):
                    n_bank += 1
                    dve.wait_ge(*scored.at(n_bank))
                    if n_bank > 4:
                        dve.wait_ge(*taken.at(n_bank - 4))
                    b = K.bank[:, (n_bank - 1) % BANKS, :].rearrange("p (h t) -> p h t", t=P)
                    o = att[:, i % 2, 2 * (i // 2):2 * (i // 2) + 2, :, :].rearrange("p c h t -> p (c h) t")
                    if l == 0:
                        dve.tensor_scalar(o, b, 2.0, None, ALU.mult).then_inc(*taken.up())
                    else:
                        m = mid(masks[:, d * GLEVELS + l - 1, :].bitcast(I32), 4)
                        dve.copy_predicated(o, m, b).then_inc(*taken.up())

            for l in range(1, GLEVELS + 1):
                size, half = 1 << l, 1 << (l - 1)
                for d in range(2):
                    view = cum[:, 2 * d:2 * d + 2, :].rearrange("p a (b w) -> p (a b) w", w=size)
                    at = half if d else half - 1
                    o = factor[:, 2 * d:2 * d + 2, :].rearrange("p a (b w) -> p (a b) w", w=size)
                    ins = dve.tensor_tensor(o, view, view[:, :, at:at + 1].broadcast_to([P, 2 * T // size, size]),
                                            ALU.subtract)
                ins.then_inc(*differences.up())
                if l == 1:
                    take_scores(0, 0)
                else:
                    for d in range(2):
                        take_scores(l - 1, d)
                dve.wait_ge(*exps.at(l))
                dve.tensor_tensor(as4(qe), as4(factor), qv(), ALU.mult).then_inc(*qe_done.up())
                dve.tensor_tensor(as4(ke), as4(factor), kv(), ALU.mult).then_inc(*ke_done.up())
                dve.wait_ge(*ke_done.now())
            for d in range(2):
                take_scores(GLEVELS, d)
            for d in range(2):
                view = cum[:, 2 * d:2 * d + 2, :].rearrange("p a (b w) -> p (a b) w", w=P)
                at = 0 if d else P - 1
                o = factor[:, 2 * d:2 * d + 2, :].rearrange("p a (b w) -> p (a b) w", w=P)
                dve.tensor_copy(cend[:, 2 * d:2 * d + 2, :].rearrange("p a b -> p (a b)").unsqueeze(2),
                                view[:, :, at:at + 1])
                ins = dve.tensor_tensor(o, view, view[:, :, at:at + 1].broadcast_to([P, 2 * TT, P]), ALU.subtract)
            ins.then_inc(*differences.up())
            dve.wait_ge(*exps.at(GLEVELS + 1))
            dve.tensor_tensor(as4(ke), as4(factor), kv(), ALU.mult).then_inc(*qe_done.up())
            dve.wait_ge(*exps.at(GLEVELS + 2))
            dve.tensor_tensor(as4(qe), as4(cum), qv(), ALU.mult)

        @block.scalar
        def _(act):
            link = Link(act, scalar_step)
            for l in range(1, GLEVELS + 2):
                act.wait_ge(*differences.at(l))
                link(act.activation(factor, factor, ACT.Abs))
                act.activation(factor, factor, ACT.Exp, scale=-1.0).then_inc(*exps.up())
            act.activation(cend, cend, ACT.Exp)
            act.activation(cum, cum, ACT.Exp).then_inc(*exps.up())

        @block.tensor
        def _(pe):
            n = 0

            def scores(q, k):
                nonlocal n
                for i in range(4):
                    if n >= BANKS:
                        pe.wait_ge(*taken.at(n - BANKS + 1))
                    r = slice(GK * (i % 2), GK * (i % 2) + GK)
                    for j in range(4):
                        c, pair = 2 * (i // 2) + j // 2, j % 2
                        mm = pe.matmul(K.bank[:, n % BANKS, j * P:j * P + P], k[r, pair, c * P:c * P + P],
                                       q[r, pair, c * P:c * P + P], start=True, stop=True)
                    mm.then_inc(*scored.up())
                    n += 1
            scores(f["gq"], f["gk"])
            for l in range(1, GLEVELS + 1):
                pe.wait_ge(*ke_done.at(l))
                for d in range(2):
                    scores(qe[:, 2 * d:2 * d + 2, :], ke[:, 2 * d:2 * d + 2, :])
    K.stage_end()
    gla_states(K, f, ke, kend_t, cend, state)
    gla_outputs(K, f, att, qe, state, factor, ke)


def gla_states(K, f, ke, kend_t, cend, state):
    nc = K.nc
    turned, kept, summed, updated = K.counts(4)
    with nc.Block() as block:
        @block.tensor
        def _(pe):
            for i in range(4):
                for c in range(TT):
                    mm = pe.transpose(K.bank[:, i, c * P:c * P + P], ke[:, i, c * P:c * P + P], K.ident[:])
                mm.then_inc(*turned.up())
            for step in range(3):
                for i in range(4):
                    c = CHUNK_ORDER[i // 2][step]
                    if step == 0:
                        pe.wait_ge(*kept.at(i + 1))
                    if step:
                        pe.wait_ge(*updated.at(4 * (step - 1) + i + 1))
                    for h in range(2):
                        head = 2 * (i % 2) + h
                        mm = pe.matmul(K.bank[GK * h:GK * h + GK, 4 + i, 0:GV], kend_t[:, i, c, GK * h:GK * h + GK],
                                       f["gv"][:, c, head * GV:head * GV + GV], start=True, stop=True)
                    mm.then_inc(*summed.up())

        @block.scalar
        def _(act):
            for i in range(4):
                act.wait_ge(*turned.at(i + 1))
                act.activation(kend_t[:, i, :, :], K.bank[:, i, :].rearrange("p (c k) -> p c k", k=P),
                               ACT.Copy).then_inc(*kept.up())

        @block.vector
        def _(dve):
            for step in range(3):
                for i in range(4):
                    c = CHUNK_ORDER[i // 2][step]
                    dve.wait_ge(*summed.at(4 * step + i + 1))
                    if step == 0:
                        dve.tensor_copy(state[:, i, 0, :], K.bank[:, 4 + i, 0:GV]).then_inc(*updated.up())
                    else:
                        dve.wait_ge(*updated.at(4 * (step - 1) + i + 1))
                        dve.scalar_tensor_tensor(state[:, i, step, :], state[:, i, step - 1, :], cend[:, i, c:c + 1],
                                                 K.bank[:, 4 + i, 0:GV], ALU.mult, ALU.add).then_inc(*updated.up())
    K.stage_end()


def gla_outputs(K, f, att, qc, state, spare, unread):
    nc = K.nc
    made, squared, rooted, scaled, turned, gated, vector_step = K.counts(7)
    on = spare.rearrange("p a t -> p (a t)").rearrange("p (c v) -> p c v", v=GW)
    squares = unread.rearrange("p a t -> p (a t)").rearrange("p (i v) -> p i v", v=GV)
    ss, rt = K.take(TT, GH), K.take(TT, GH)

    def bank(c, h):
        return K.bank[:, 4 * (h % 2) + c, (h // 2) * GV:(h // 2) * GV + GV]

    with nc.Block() as block:
        @block.tensor
        def _(pe):
            for c in range(TT):
                for h in range(GH):
                    o = bank(c, h)
                    mms = [(att[:, h % 2, c, h // 2, :], f["gv"][:, c, h * GV:h * GV + GV])]
                    r = slice(GK * (h % 2), GK * (h % 2) + GK)
                    for d in range(2):
                        pos = CHUNK_ORDER[d].index(c)
                        if pos:
                            i = 2 * d + h // 2
                            mms.append((qc[r, i, c * P:c * P + P], state[r, i, pos - 1, :]))
                    for j, (a, b) in enumerate(mms):
                        mm = pe.matmul(o, a, b, start=(j == 0), stop=(j == len(mms) - 1))
                mm.then_inc(*made.up())
            for c in range(TT):
                pe.wait_ge(*scaled.at(c + 1))
                for h in range(GH):
                    mm = pe.transpose(K.bank[:, c, h * P:h * P + P], on[:, c, h * GV:h * GV + GV], K.ident[:])
                mm.then_inc(*turned.up())

        @block.scalar
        def _(act):
            for c in range(TT):
                act.wait_ge(*made.at(c + 1))
                for h in range(GH):
                    ins = act.activation(squares[:, GH * c + h, :], bank(c, h), ACT.Square,
                                         accum_out=ss[:, c, h:h + 1])
            ins.then_inc(*squared.up())
            act.wait_ge(*squared.at(1))
            act.activation(rt, ss, ACT.Sqrt, bias=K.small[:, 0:1], scale=1.0 / GV).then_inc(*rooted.up())

        @block.vector
        def _(dve):
            link = Link(dve, vector_step)
            dve.wait_ge(*rooted.at(1))
            link(dve.reciprocal(rt, rt))
            for c in range(TT):
                for e in range(2):
                    ins = dve.tensor_tensor(on[:, c, :].rearrange("p (h v) -> p h v", v=GV)[:, e:GH:2, :],
                                            K.bank[:, 4 * e + c, 0:2 * GV].rearrange("p (h v) -> p h v", v=GV),
                                            last(rt[:, c, e:GH:2], GV), ALU.mult)
                ins.then_inc(*scaled.up())
            for c in range(TT):
                dve.wait_ge(*turned.at(c + 1))
                for h in range(GH):
                    dve.scalar_tensor_tensor(K.h[:, h, c * P:c * P + P], K.bank[:, c, h * P:h * P + P],
                                             K.col("gla_norm", h), f["gg"][:, h, c * P:c * P + P], ALU.mult, ALU.mult)
    K.stage_end()


def mlstm_key_tiles(d):
    if d == 0:
        return [(s, [(s, TT)]) for s in range(TT)]
    return [(0, [(0, 1), (2, 4)]), (1, [(0, 4)]), (2, [(2, 3)]), (3, [(2, 4)])]


def mlstm(K, f):
    nc = K.nc
    R = 36
    li, lf = f["li"][0:R, :], f["lf"][0:R, :]
    e, run, peak, em = K.take(T)[0:R, :], K.take(T)[0:R, :], K.take(T)[0:R, :], K.take(T)[0:R, :]
    gcol, ecol = K.take(TT, R), K.take(TT, R)
    step_a, step_v, logged, peaks, ems = K.counts(5)
    ones_r = K.take(T)
    with nc.Block() as block:
        @block.gpsimd
        def _(pool):
            pool.memset(ones_r, 1.0).then_inc(*peaks.up())
            pool.memset(run, 0.0).then_inc(*peaks.up())
            pool.memset(peak, 0.0).then_inc(*peaks.up())

        @block.scalar
        def _(act):
            link = Link(act, step_a)
            link(act.activation(e, lf, ACT.Abs))
            link(act.activation(e, e, ACT.Exp, scale=-1.0))
            act.activation(e, e, ACT.Ln, bias=K.small[0:R, 1:2], scale=1.0).then_inc(*logged.up())
            act.wait_ge(*ems.at(1))
            act.activation(em, em, ACT.Exp, scale=-1.0)

        @block.vector
        def _(dve):
            link = Link(dve, step_v)
            dve.wait_ge(*logged.at(1))
            link(dve.scalar_tensor_tensor(e, lf, 0.0, e, ALU.min, ALU.subtract))
            dve.wait_ge(*peaks.at(3))

            def scans(out, data0, src, op0, op1):
                link(dve.tensor_tensor_scan(out[0:4, :], data0(0, slice(0, T)), src[0:4, :], 0.0, op0, op1))
                b = slice(32, 36)
                link(dve.tensor_tensor_scan(out[b, 0:CTX][:, ::-1], data0(32, slice(0, CTX))[:, ::-1],
                                            src[b, 0:CTX][:, ::-1], 0.0, op0, op1))
                link(dve.tensor_tensor_scan(out[b, CTX:T][:, ::-1], data0(32, slice(CTX, T))[:, ::-1],
                                            src[b, CTX:T][:, ::-1], out[b, 0:1], op0, op1))
            scans(run, lambda r, c: ones_r[r:r + 4, c], e, ALU.mult, ALU.add)
            link(dve.tensor_tensor(li, li, run, ALU.subtract))
            scans(peak, lambda r, c: li[r:r + 4, c], li, ALU.max, ALU.max)
            dve.tensor_tensor(em, run, peak, ALU.add).then_inc(*ems.up())
    K.stage_end()

    turned, = K.counts(1)
    with nc.Block() as block:
        @block.tensor
        def _(pe):
            for c in range(TT):
                pe.transpose(K.bank[:, 0, c * R:c * R + R], li[:, c * P:c * P + P], K.ident[0:R, 0:R])
                mm = pe.transpose(K.bank[:, 1, c * R:c * R + R], em[:, c * P:c * P + P], K.ident[0:R, 0:R])
            mm.then_inc(*turned.up())

        @block.scalar
        def _(act):
            act.wait_ge(*turned.at(1))
            act.activation(gcol.rearrange("p c r -> p (c r)"), K.bank[:, 0, 0:TT * R], ACT.Copy)
            act.activation(ecol.rearrange("p c r -> p (c r)"), K.bank[:, 1, 0:TT * R], ACT.Copy)
    K.stage_end()

    W = K.take(2, TT, T)
    hacc = K.take(TT, GW)
    den = K.take(2, TT)
    raised, qk_done, bounded, exped, weighted, used, made, unit_done, vector_step = K.counts(9)
    PEAK, QK, OUT = 0, 1, 5
    with nc.Block() as block:
        @block.tensor
        def _(pe):
            def scores(h):
                if h:
                    pe.wait_ge(*weighted.at(2 * h))
                for s in range(TT):
                    mm = pe.matmul(K.bank[:, QK + s, :], f["mk"][:, h, s * P:s * P + P], f["mq"][:, h, :],
                                   start=True, stop=True)
                mm.then_inc(*qk_done.up())

            def spread(u):
                h, d = u // 2, u % 2
                if u:
                    pe.wait_ge(*bounded.at(u))
                r = h + 32 * d
                pe.matmul(K.bank[:, PEAK, :], K.ident[0:R, r:r + 1].broadcast_to([R, P]), peak,
                          start=True, stop=True).then_inc(*raised.up())

            spread(0)
            for u in range(2 * MH):
                h, d = u // 2, u % 2
                if d == 0:
                    scores(h)
                if u + 1 < 2 * MH:
                    spread(u + 1)
                pe.wait_ge(*weighted.at(u + 1))
                if u:
                    pe.wait_ge(*unit_done.at(u))
                tiles = mlstm_key_tiles(d)
                for t in range(TT):
                    seen = [s for s, ranges in tiles if any(a <= t < b for a, b in ranges)]
                    o = K.bank[:, OUT + t // 2, (t % 2) * 256:(t % 2) * 256 + MD + 1]
                    for j, s in enumerate(seen):
                        mm = pe.matmul(o, W[:, u % 2, s, t * P:t * P + P], f["mv"][:, s, h, :],
                                       start=(j == 0), stop=(j == len(seen) - 1))
                mm.then_inc(*made.up())

        @block.vector
        def _(dve):
            link = Link(dve, vector_step)

            def bound(u):
                h, d = u // 2, u % 2
                r = h + 32 * d
                dve.wait_ge(*raised.at(u + 1))
                if u >= 2:
                    dve.wait_ge(*made.at(u - 1))
                tiles = mlstm_key_tiles(d)
                for s, ranges in tiles:
                    for a, b in ranges:
                        ins = dve.tensor_scalar(W[:, u % 2, s, a * P:b * P], K.bank[:, PEAK, a * P:b * P],
                                                gcol[:, s, r:r + 1], 0.0, ALU.subtract, ALU.max)
                ins.then_inc(*bounded.up())

            def weigh(u):
                h, d = u // 2, u % 2
                dve.wait_ge(*exped.at(u + 1))
                dve.wait_ge(*qk_done.at(h + 1))
                tiles = mlstm_key_tiles(d)
                for s, ranges in tiles:
                    for a, b in ranges:
                        ins = dve.scalar_tensor_tensor(W[:, u % 2, s, a * P:b * P], K.bank[:, QK + s, a * P:b * P],
                                                       MD ** -0.5, W[:, u % 2, s, a * P:b * P], ALU.mult, ALU.mult)
                link(ins)
                tri = K.tri_b if d else K.tri_f
                for s in range(TT):
                    diag = W[:, u % 2, s, s * P:s * P + P]
                    ins = dve.tensor_tensor(diag, diag, tri[:], ALU.mult)
                ins.then_inc(*weighted.up())

            def divide(u):
                h, d = u // 2, u % 2
                r = h + 32 * d
                dve.wait_ge(*made.at(u + 1))
                dn = den[:, u % 2, :]
                total = K.bank[:, OUT:OUT + 2, :].rearrange("p b (u x) -> p b u x", x=256)[:, :, :, MD]
                floor = ecol[:, :, r].rearrange("p (b u) -> p b u", u=2)
                dn2 = dn.rearrange("p (b u) -> p b u", u=2)
                link(dve.scalar_tensor_tensor(dn2, total, -1.0, floor, ALU.mult, ALU.max))
                link(dve.tensor_tensor(dn2, total, dn2, ALU.max))
                link(dve.reciprocal(dn, dn))
                for t in range(TT):
                    o = K.bank[:, OUT + t // 2, (t % 2) * 256:(t % 2) * 256 + MD]
                    acc = hacc[:, t, h * MD:h * MD + MD]
                    if d == 0:
                        ins = dve.tensor_scalar(acc, o, dn[:, t:t + 1], None, ALU.mult)
                    else:
                        ins = dve.scalar_tensor_tensor(acc, o, dn[:, t:t + 1], acc, ALU.mult, ALU.add)
                ins.then_inc(*unit_done.up())
                dve.wait_ge(*unit_done.now())

            bound(0)
            for u in range(2 * MH):
                if u + 1 < 2 * MH:
                    bound(u + 1)
                weigh(u)
                if u:
                    divide(u - 1)
            divide(2 * MH - 1)

        @block.scalar
        def _(act):
            for u in range(2 * MH):
                d = u % 2
                act.wait_ge(*bounded.at(u + 1))
                tiles = mlstm_key_tiles(d)
                for s, ranges in tiles:
                    for a, b in ranges:
                        w = W[:, u % 2, s, a * P:b * P]
                        ins = act.activation(w, w, ACT.Exp, scale=-1.0)
                ins.then_inc(*exped.up())
    K.stage_end()

    gatedh, squared, rooted, scaled, turned, vector_step = K.counts(6)
    squares = W.rearrange("p u s t -> p (u s t)").rearrange("p (i v) -> p i v", v=MD)
    ss, rt = K.take(TT, MH), K.take(TT, MH)
    with nc.Block() as block:
        @block.vector
        def _(dve):
            link = Link(dve, vector_step)
            dve.tensor_tensor(hacc, hacc, f["mo"], ALU.mult).then_inc(*gatedh.up())
            dve.wait_ge(*rooted.at(1))
            link(dve.reciprocal(rt, rt))
            for c in range(TT):
                v = hacc[:, c, :].rearrange("p (h v) -> p h v", v=MD)
                dve.tensor_tensor(v, v, last(rt[:, c, :], MD), ALU.mult).then_inc(*scaled.up())
            for c in range(TT):
                dve.wait_ge(*turned.at(c + 1))
                for h in range(MH):
                    dve.tensor_scalar(K.h[:, 4 + h, c * P:c * P + P], K.bank[:, c, h * P:h * P + P],
                                      K.col("ml_norm", h), None, ALU.mult)

        @block.scalar
        def _(act):
            act.wait_ge(*gatedh.at(1))
            for c in range(TT):
                for h in range(MH):
                    ins = act.activation(squares[:, MH * c + h, :], hacc[:, c, h * MD:h * MD + MD], ACT.Square,
                                         accum_out=ss[:, c, h:h + 1])
            ins.then_inc(*squared.up())
            act.wait_ge(*squared.at(1))
            act.activation(rt, ss, ACT.Sqrt, bias=K.small[:, 0:1], scale=1.0 / MD).then_inc(*rooted.up())

        @block.tensor
        def _(pe):
            for c in range(TT):
                pe.wait_ge(*scaled.at(c + 1))
                for h in range(MH):
                    mm = pe.transpose(K.bank[:, c, h * P:h * P + P], hacc[:, c, h * MD:h * MD + MD], K.ident[:])
                mm.then_inc(*turned.up())
    K.stage_end()

def log1p_small(link, dve, e, t, w, w2):
    link(dve.tensor_scalar(t, e, 2.0, None, ALU.add))
    link(dve.reciprocal(t, t))
    link(dve.tensor_tensor(w, e, t, ALU.mult))
    link(dve.tensor_tensor(w2, w, w, ALU.mult))
    link(dve.tensor_scalar(t, w2, 1.0 / 17.0, None, ALU.mult))
    for n in (15, 13, 11, 9, 7, 5, 3):
        link(dve.scalar_tensor_tensor(t, t, 1.0 / n, w2, ALU.add, ALU.mult))
    link(dve.scalar_tensor_tensor(t, t, 1.0, w, ALU.add, ALU.mult))
    link(dve.tensor_scalar(e, t, 2.0, None, ALU.mult))


def odd_mixer(K):
    nc = K.nc
    mark = K.top
    zs, xl, xc = K.take(KI, LAT), K.take(KI, LAT), K.take(KI, CTX)
    bt, ct = K.take(SG, T), K.take(SG, LAT)
    xt = K.take(TT, SI)
    cum = K.take(T)[0:64, :]
    dcol = K.take(8, 64)
    K.top -= TT * SI + T + 8 * 64
    dt = K.take(T)[0:64, :]
    dt_w = K.take(KD, 64)
    ssd_projection(K, zs, xl, xc, bt, ct, dt, dt_w)
    K.top -= KD * 64 + T
    dt_src = dt
    xt = K.take(TT, SI)
    cum, dcol = K.take(T)[0:64, :], K.take(8, 64)
    work = K.top
    ssd_steps(K, dt_src, cum, dcol, xt)
    K.top = work
    bs = K.take(LT, SG, SN)
    state = K.take(2, SI)
    ssd_turn(K, xc, xl, bt, xt, bs)
    wx = xc.rearrange("p a t -> p (a t)").rearrange("p (c x) -> p c x", c=2)
    ssd_context(K, wx, xt, bs, dcol, state)
    y = xt[:, 0:2, :]
    ssd_entering(K, y, ct, state, dcol, wx)
    cb = state.rearrange("p d x -> p (d x)")[:, 0:2 * SG * 3 * P].rearrange("p (d g b t) -> p d g b t", d=2, g=SG, b=3)
    ssd_inside(K, y, xt, bt, ct, cb, cum, dcol, bs, state)
    ssd_combine(K, y, xl, zs, xc)
    K.top = mark
    hv = K.h[:].rearrange("p k t -> p (k t)").rearrange("p (k t) -> p k t", t=LAT)
    first = FIRST_TILE["ssd_out"]
    run_products(K, residual_items(K, "ssd_out", KI, lambda k: hv[:, k, :], CTX,
                                   lambda m, which: K.mod[:, 1, 16 + m, which:which + 1]), first + 8 * KI)


def ssd_projection(K, zs, xl, xc, bt, ct, dt, dt_w):
    nc = K.nc
    (loads,) = K.counts(1)
    with nc.Block() as block:
        @block.sync
        def _(sync):
            sync.dma_start(dt_w, K.dram["ssd_dt_w"]).then_inc(*loads.up(16))
            sync.wait_ge(*loads.at(16))
    K.stage_end()
    first = FIRST_TILE["ssd_in"]
    rounds, tile = [], first
    for c in range(24):
        n = T if c < 20 else LAT

        def finish(act, acc, c=c):
            if c < 16:
                act.activation(xc[:, c, :], acc[:, 0:CTX], ACT.Silu)
                return act.activation(xl[:, c, :], acc[:, CTX:T], ACT.Silu)
            return act.activation(bt[:, c - 16, :] if c < 20 else ct[:, c - 20, :], acc, ACT.Silu)
        conv = Conv(n, K.col("ssd_conv_w", 24 + c), K.col("ssd_conv_b", c),
                    conv_taps_1d(lambda tap, c=c: K.col("ssd_conv_w", tap * 24 + c), n // 256), finish)
        rounds.append([Item(tile_products(K, tile, KD, lambda k, n=n: K.h[:, k, T - n:T], n), None, "act", conv)])
        tile += KD
    for c in range(KI):
        rounds.append([Item(tile_products(K, tile, KD, lambda k: K.h[:, k, CTX:T], LAT),
                            lambda act, bank, c=c: act.activation(zs[:, c, :], bank[:, 0:LAT], ACT.Silu))])
        tile += KD
    rounds.append([Item(own_products([(dt_w[:, k, :], K.h[:, k, :]) for k in range(KD)], 64, T),
                        lambda act, bank: act.activation(dt, bank[0:64, :], ACT.Identity,
                                                         bias=K.col("ssd_dt_b", rows=slice(0, 64)), scale=1.0))])
    top = K.top
    run_products(K, rounds, first + 40 * KD)
    K.top = top


def ssd_steps(K, dt, cum, dcol, xt):
    nc = K.nc
    flat = K.take(8, T)
    R = slice(0, 64)
    e, t, w, w2, la, wend, ecum = (flat[R, i, :] for i in range(7))
    acol = K.take(2)[R, :]
    step_a, step_v, exped, summed, decayed, ready, turned = K.counts(7)
    with nc.Block() as block:
        @block.scalar
        def _(act):
            link = Link(act, step_a)
            link(act.activation(acol[:, 0:1], K.col("ssd_a_log", rows=R), ACT.Exp))
            link(act.activation(e, dt, ACT.Abs))
            act.activation(e, e, ACT.Exp, scale=-1.0).then_inc(*exped.up())
            act.wait_ge(*summed.at(1))
            act.activation(ecum[:, 0:LAT], cum[:, CTX:T], ACT.Exp)
            act.activation(wend[:, 0:CTX], wend[:, 0:CTX], ACT.Exp, scale=-1.0).then_inc(*decayed.up())

        @block.vector
        def _(dve):
            link = Link(dve, step_v)
            dve.wait_ge(*exped.at(1))
            log1p_small(link, dve, e, t, w, w2)
            link(dve.scalar_tensor_tensor(dt, dt, 0.0, e, ALU.max, ALU.add))
            link(dve.tensor_scalar(la, dt, acol[:, 0:1], -1.0, ALU.mult, ALU.mult))
            one = w
            link(dve.memset(one, 1.0))
            for a, b in ((0, CTX), (CTX, T)):
                link(dve.tensor_tensor_scan(cum[0:32, a:b], one[0:32, a:b], la[0:32, a:b], 0.0, ALU.mult, ALU.add))
                link(dve.tensor_tensor_scan(cum[32:64, a:b][:, ::-1], one[32:64, a:b], la[32:64, a:b][:, ::-1], 0.0,
                                            ALU.mult, ALU.add))
            dve.tensor_scalar(wend[0:32, 0:CTX], cum[0:32, 0:CTX], cum[0:32, CTX - 1:CTX], None, ALU.subtract)
            dve.tensor_scalar(wend[32:64, 0:CTX], cum[32:64, 0:CTX], cum[32:64, 0:1], None,
                              ALU.subtract).then_inc(*summed.up())
            dve.wait_ge(*decayed.at(1))
            dve.tensor_tensor(wend[:, 0:CTX], wend[:, 0:CTX], dt[:, 0:CTX], ALU.mult).then_inc(*ready.up())
            dve.wait_ge(*turned.at(1))
            dve.tensor_copy(dcol.rearrange("p i h -> p (i h)"), K.bank[:, 0, :])

        @block.tensor
        def _(pe):
            pe.wait_ge(*ready.at(1))
            for i, src in enumerate((wend[:, 0:CTX], dt[:, CTX:T], cum[:, CTX:T], ecum[:, 0:LAT])):
                for c in range(LT):
                    mm = pe.transpose(K.bank[:, 0, (2 * i + c) * 64:(2 * i + c) * 64 + 64], src[:, c * P:c * P + P],
                                      K.ident[R, 0:64])
            mm.then_inc(*turned.up())
    K.stage_end()


WEND, DT, CUM, ECUM = 0, 2, 4, 6


def ssd_turn(K, xc, xl, bt, xt, bs):
    nc = K.nc
    turned, kept = K.counts(2)
    jobs = []
    for c in range(TT):
        for q in range(KI // 4):
            src = [(xc if c < LT else xl)[:, 4 * q + i, (c % LT) * P:(c % LT) * P + P] for i in range(4)]
            jobs.append((src, xt[:, c, q * 512:q * 512 + 512]))
    for c in range(LT):
        jobs.append(([bt[:, g, c * P:c * P + P] for g in range(SG)], bs[:, c, :, :].rearrange("p g n -> p (g n)")))
    with nc.Block() as block:
        @block.tensor
        def _(pe):
            for j, (src, _d) in enumerate(jobs):
                if j >= BANKS:
                    pe.wait_ge(*kept.at(j - BANKS + 1))
                for i, a in enumerate(src):
                    mm = pe.transpose(K.bank[:, j % BANKS, i * P:i * P + P], a, K.ident[:])
                mm.then_inc(*turned.up())

        @block.scalar
        def _(act):
            for j, (_s, dest) in enumerate(jobs):
                act.wait_ge(*turned.at(j + 1))
                act.activation(dest, K.bank[:, j % BANKS, :], ACT.Copy).then_inc(*kept.up())
    K.stage_end()


def ssd_context(K, wx, xt, bs, dcol, state):
    nc = K.nc
    weighted, summed = K.counts(2)
    with nc.Block() as block:
        @block.vector
        def _(dve):
            for d in range(2):
                if d:
                    dve.wait_ge(*summed.at(SG))
                for c in range(LT):
                    dve.tensor_tensor(wx[:, c, :].rearrange("p (h x) -> p h x", x=SP),
                                      xt[:, c, :].rearrange("p (h x) -> p h x", x=SP),
                                      last(dcol[:, WEND + c, 32 * d:32 * d + 32], SP), ALU.mult).then_inc(*weighted.up())

        @block.tensor
        def _(pe):
            for d in range(2):
                pe.wait_ge(*weighted.at(2 * d + 2))
                for g in range(SG):
                    for c in range(LT):
                        mm = pe.matmul(K.bank[:, SG * d + g, :], bs[:, c, g, :], wx[:, c, g * 512:g * 512 + 512],
                                       start=(c == 0), stop=(c == LT - 1))
                    mm.then_inc(*summed.up())

        @block.scalar
        def _(act):
            for i in range(2 * SG):
                act.wait_ge(*summed.at(i + 1))
                act.activation(state[:, i // SG, (i % SG) * 512:(i % SG) * 512 + 512], K.bank[:, i, :], ACT.Copy)
    K.stage_end()


def ssd_entering(K, y, ct, state, dcol, tmp):
    nc = K.nc
    made, taken, vector_step = K.counts(3)
    units = [(d, t, g) for d in range(2) for t in range(LT) for g in range(SG)]
    with nc.Block() as block:
        @block.tensor
        def _(pe):
            for u, (d, t, g) in enumerate(units):
                if u >= BANKS:
                    pe.wait_ge(*taken.at(u - BANKS + 1))
                pe.matmul(K.bank[:, u % BANKS, :], ct[:, g, t * P:t * P + P], state[:, d, g * 512:g * 512 + 512],
                          start=True, stop=True).then_inc(*made.up())

        @block.vector
        def _(dve):
            link = Link(dve, vector_step)
            for u, (d, t, g) in enumerate(units):
                dve.wait_ge(*made.at(u + 1))
                yv = y[:, t, g * 512:g * 512 + 512]
                o = tmp[:, 0, 0:512] if d else yv
                ins = dve.tensor_tensor(o.rearrange("p (h x) -> p h x", x=SP),
                                        K.bank[:, u % BANKS, :].rearrange("p (h x) -> p h x", x=SP),
                                        last(dcol[:, ECUM + t, 32 * d + 8 * g:32 * d + 8 * g + 8], SP), ALU.mult)
                ins.then_inc(*taken.up())
                if d:
                    dve.wait_ge(*taken.now())
                    link(dve.tensor_tensor(yv, yv, o, ALU.add))
    K.stage_end()


def ssd_inside(K, y, xt, bt, ct, cb, cum, dcol, bs, state):
    nc = K.nc
    blocks = (((0, 0, True), (0, 1, False), (1, 1, True)), ((1, 0, False), (1, 1, True), (0, 0, True)))
    made, = K.counts(1)
    with nc.Block() as block:
        @block.tensor
        def _(pe):
            for g in range(SG):
                for s in range(LT):
                    mm = pe.matmul(K.bank[:, g, s * LAT:s * LAT + LAT], bt[:, g, CTX + s * P:CTX + s * P + P],
                                   ct[:, g, :], start=True, stop=True)
                mm.then_inc(*made.up())

        @block.vector
        def _(dve):
            for g in range(SG):
                dve.wait_ge(*made.at(g + 1))
                for d in range(2):
                    for b, (s, t, diag) in enumerate(blocks[d]):
                        src = K.bank[:, g, s * LAT + t * P:s * LAT + t * P + P]
                        if diag:
                            dve.tensor_tensor(cb[:, d, g, b, :], src, (K.tri_b if d else K.tri_f)[:], ALU.mult)
                        else:
                            dve.tensor_copy(cb[:, d, g, b, :], src)
    K.stage_end()

    NW, NX = 4, 4
    W = K.take(NW, 3, P)
    units = [(g, h, d) for g in range(SG) for h in range(8) for d in range(2)]
    raised, bounded, exped, weighted, used, finished, added = K.counts(7)
    with nc.Block() as block:
        @block.tensor
        def _(pe):
            def spread(u):
                g, h, d = units[u]
                if u >= NX:
                    pe.wait_ge(*bounded.at(u - NX + 1))
                r = 32 * d + 8 * g + h
                pe.matmul(K.bank[:, u % NX, 0:LAT], K.ident[0:64, r:r + 1].broadcast_to([64, P]), cum[:, CTX:T],
                          start=True, stop=True).then_inc(*raised.up())

            for u in range(NX - 1):
                spread(u)
            for u, (g, h, d) in enumerate(units):
                if u + NX - 1 < len(units):
                    spread(u + NX - 1)
                pe.wait_ge(*weighted.at(u + 1))
                if h == 0 and d == 0 and g >= 2:
                    pe.wait_ge(*added.at(g - 1))
                head = 8 * g + h
                for b, (s, t, diag) in enumerate(blocks[d]):
                    first = (d == 0 and b == 0) if t == 0 else (d == 0 and b == 1)
                    stop = (d == 1 and b == 2) if t == 0 else (d == 1 and b == 1)
                    mm = pe.matmul(K.bank[:, NX + 2 * (g % 2) + t, h * SP:h * SP + SP], W[:, u % NW, b, :],
                                   xt[:, LT + s, head * SP:head * SP + SP], start=first, stop=stop)
                mm.then_inc(*used.up())

        @block.vector
        def _(dve):
            def bound(u):
                g, h, d = units[u]
                r = 32 * d + 8 * g + h
                dve.wait_ge(*raised.at(u + 1))
                if u >= NW:
                    dve.wait_ge(*used.at(u - NW + 1))
                sa, sb = blocks[d][0][0], blocks[d][2][0]
                tb = blocks[d][2][1]
                w = W[:, u % NW, :, :].rearrange("p b t -> p (b t)")
                dve.tensor_scalar(w[:, 0:LAT], K.bank[:, u % NX, 0:LAT], dcol[:, CUM + sa, r:r + 1], 0.0,
                                  ALU.subtract, ALU.min)
                dve.tensor_scalar(w[:, LAT:LAT + P], K.bank[:, u % NX, tb * P:tb * P + P], dcol[:, CUM + sb, r:r + 1],
                                  0.0, ALU.subtract, ALU.min).then_inc(*bounded.up())

            def weigh(u):
                g, h, d = units[u]
                r = 32 * d + 8 * g + h
                sa, sb = blocks[d][0][0], blocks[d][2][0]
                w = W[:, u % NW, :, :].rearrange("p b t -> p (b t)")
                c = cb[:, d, g, :, :].rearrange("p b t -> p (b t)")
                dve.wait_ge(*exped.at(u + 1))
                dve.scalar_tensor_tensor(w[:, 0:LAT], w[:, 0:LAT], dcol[:, DT + sa, r:r + 1], c[:, 0:LAT],
                                         ALU.mult, ALU.mult)
                dve.scalar_tensor_tensor(w[:, LAT:LAT + P], w[:, LAT:LAT + P], dcol[:, DT + sb, r:r + 1],
                                         c[:, LAT:LAT + P], ALU.mult, ALU.mult).then_inc(*weighted.up())

            def add(g):
                dve.wait_ge(*used.at(16 * g + 16))
                for t in range(LT):
                    yv = y[:, t, g * 512:g * 512 + 512]
                    ins = dve.tensor_tensor(yv, yv, K.bank[:, NX + 2 * (g % 2) + t, :], ALU.add)
                ins.then_inc(*added.up())

            AHEAD = 2
            for u in range(AHEAD):
                bound(u)
            for u in range(len(units)):
                if u + AHEAD < len(units):
                    bound(u + AHEAD)
                weigh(u)
                if u % 16 == 4 and u > 16:
                    add(u // 16 - 1)
            add(SG - 1)

        @block.scalar
        def _(act):
            for u in range(len(units)):
                act.wait_ge(*bounded.at(u + 1))
                w = W[:, u % NW, :, :]
                act.activation(w, w, ACT.Exp).then_inc(*exped.up())
    K.stage_end()


def ssd_combine(K, y, xl, zs, sq):
    nc = K.nc
    turned, gated, squared, summed, rooted, vector_step, scalar_step = K.counts(7)
    hv = K.h[:].rearrange("p k t -> p (k t)").rearrange("p (k t) -> p k t", t=LAT)
    rstd = K.take(SG, LAT)
    with nc.Block() as block:
        @block.tensor
        def _(pe):
            for c in range(KI):
                for t in range(LT):
                    mm = pe.transpose(K.bank[:, c // 2, (c % 2) * LAT + t * P:(c % 2) * LAT + t * P + P],
                                      y[:, t, c * P:c * P + P], K.ident[:])
                mm.then_inc(*turned.up())
            for g in range(SG):
                pe.wait_ge(*squared.at(4 * g + 4))
                for c in range(4):
                    mm = pe.matmul(K.bank[:, 2 * g, 0:LAT], K.ones[:], sq[:, 4 * g + c, :], start=(c == 0), stop=(c == 3))
                mm.then_inc(*summed.up())

        @block.vector
        def _(dve):
            link = Link(dve, vector_step)
            for c in range(KI):
                dve.wait_ge(*turned.at(c // 2 * 2 + 2))
                link(dve.scalar_tensor_tensor(xl[:, c, :], xl[:, c, :], K.col("ssd_d", c),
                                              K.bank[:, c // 2, (c % 2) * LAT:(c % 2) * LAT + LAT], ALU.mult, ALU.add))
                dve.tensor_tensor(xl[:, c, :], xl[:, c, :], zs[:, c, :], ALU.mult).then_inc(*gated.up())
            for g in range(SG):
                dve.wait_ge(*rooted.at(g + 1))
                link(dve.reciprocal(rstd[:, g, :], rstd[:, g, :]))
                for c in range(4 * g, 4 * g + 4):
                    dve.scalar_tensor_tensor(hv[:, c, :], xl[:, c, :], K.col("ssd_norm", c), rstd[:, g, :],
                                             ALU.mult, ALU.mult)

        @block.scalar
        def _(act):
            for c in range(KI):
                act.wait_ge(*gated.at(c + 1))
                act.activation(sq[:, c, :], xl[:, c, :], ACT.Square).then_inc(*squared.up())
            for g in range(SG):
                act.wait_ge(*summed.at(g + 1))
                act.activation(rstd[:, g, :], K.bank[:, 2 * g, 0:LAT], ACT.Sqrt, bias=K.small[:, 0:1],
                               scale=1.0 / 512).then_inc(*rooted.up())
    K.stage_end()


IN2 = [("qa", 4, "Copy"), ("ka", 4, "Copy"), ("qc", 4, "Copy"), ("kd", 4, "Copy"), ("xb", 4, "Copy"), ("kc", 1, "Copy"),
       ("vc", 1, "Copy"), ("ud", 4, "Gelu"), ("ga", 4, "Silu"), ("gb", 4, "Silu"), ("gc", 4, "Silu"), ("gd", 4, "Silu"),
       ("mg", 32, "Sigmoid")]


def hybrid_layer(K, out):
    nc = K.nc
    normalise(K, CTX, lambda k: K.x[:, k, CTX:T], "final_g")
    normalise(K, CTX, lambda k: K.h[:, k, CTX:T], "norm2")
    mark = K.top
    f = {name: K.take(n, LAT) for name, n, _func in IN2}
    f["va"], f["vd"], f["vs"] = K.take(LT, BW), K.take(LT, BW), K.take(LT, 256)
    f["gate"] = K.take(LT, 24)
    f["fa"] = K.take(LAT)
    own_fa, own_gate = K.take(KD, 8), K.take(KD, 24)
    project2(K, f, own_fa, own_gate)
    K.top -= KD * 32
    work = K.top
    qk_norms(K, f)
    K.top = work
    forget_sums(K, f)
    addmask = K.take(2 * P)
    attention_mask(K, addmask)
    o = K.take(LT, BW)
    sums = K.take(LT, NH)
    inner = K.top

    def head_rows(h):
        return slice(HD * (h % 2), HD * (h % 2) + HD)

    attention(K, lambda h: f["qa"][head_rows(h), h // 2, :], lambda h: f["ka"][head_rows(h), h // 2, :],
              lambda s, h: f["va"][:, s, h * HD:h * HD + HD], addmask, f["fa"], o, sums, None, False)
    turn_gate(K, o, f["ga"])
    K.top = inner
    compressed_attention(K, f, o, sums)
    K.top = inner
    for branch, (kt, vt) in ((1, (0, 0)), (2, (2, 128))):
        attention(K, lambda h: f["qc"][head_rows(h), h // 2, :],
                  lambda h, kt=kt: f["kd"][head_rows(h), kt + h // 4, :],
                  lambda s, h, vt=vt: f["vs"][:, s, vt + (h // 4) * HD:vt + (h // 4) * HD + HD],
                  addmask, None, o, sums, lambda t, b=branch: f["gate"][:, t, NH * b:NH * b + NH], True)
        K.top = inner
    turn_gate(K, o, f["gc"])
    K.top = work
    recurrence(K, f)
    K.top = work
    spatial_gating(K, f)
    K.top = work
    merge(K, f, out)
    K.top = mark


def project2(K, f, own_fa, own_gate):
    nc = K.nc
    (loads,) = K.counts(1)
    with nc.Block() as block:
        @block.sync
        def _(sync):
            sync.dma_start(own_fa, K.dram["fa_w"]).then_inc(*loads.up(16))
            sync.dma_start(own_gate, K.dram["gate_w"]).then_inc(*loads.up(16))
            sync.wait_ge(*loads.at(32))
    K.stage_end()
    first = FIRST_TILE["in2"]
    rounds, tile = [], first
    func_of = {"Copy": ACT.Copy, "Gelu": ACT.Gelu, "Silu": ACT.Silu, "Sigmoid": ACT.Sigmoid}

    def h(k):
        return K.h[:, k, CTX:T]

    def token_round(name, width, func):
        groups = token_products(K, tile, range(LT, TT), width)
        rounds.append([Item(g, lambda act, bank, i=i: act.activation(f[name][:, i, :], bank[:, 0:width], func))
                       for i, g in enumerate(groups)])

    for name, n, func in IN2:
        if name == "ud":
            token_round("va", BW, ACT.Copy)
            tile += 4 * KD
            token_round("vs", 256, ACT.Copy)
            tile += 2 * KD
            rounds.append([Item(own_products([(own_fa[:, k, :], h(k)) for k in range(KD)], 8, LAT),
                                lambda act, bank: act.activation(f["fa"][0:8, :], bank[0:8, 0:LAT], ACT.Identity,
                                                                 bias=K.col("b_forget", rows=slice(0, 8)), scale=1.0))])
            token_round("vd", BW, ACT.Gelu)
            tile += 4 * KD
        for j in range(n):
            dest = f[name][:, j, :]
            rounds.append([Item(tile_products(K, tile, KD, h, LAT),
                                lambda act, bank, dest=dest, func=func: act.activation(dest, bank[:, 0:LAT], func_of[func]))])
            tile += KD
    for t in range(LT):
        rounds.append([Item(own_products([(K.h[:, k, CTX + t * P:CTX + t * P + P], own_gate[:, k, :]) for k in range(KD)],
                                         P, 24),
                            lambda act, bank, t=t: act.activation(f["gate"][:, t, :], bank[:, 0:24], ACT.Sigmoid))])
    run_products(K, rounds, first + 84 * KD)


def qk_norms(K, f):
    nc = K.nc
    squared, summed, rooted, vector_step = K.counts(4)
    sets = (("qa", "qn_a"), ("ka", "kn_a"), ("qc", "qn_c"), ("kd", "kn_c"))
    sq, rt = K.take(4, 4, LAT), K.take(4, 4, LAT)
    with nc.Block() as block:
        @block.scalar
        def _(act):
            for i, (name, _g) in enumerate(sets):
                act.activation(sq[:, i, :, :], f[name], ACT.Square).then_inc(*squared.up())
            for i in range(4):
                act.wait_ge(*summed.at(i + 1))
                act.activation(rt[:, i, :, :].rearrange("p (b a) t -> p b (a t)", a=2), K.bank[:, 2 * i:2 * i + 2, :],
                               ACT.Sqrt, bias=K.small[:, 0:1], scale=1.0 / HD).then_inc(*rooted.up())

        @block.tensor
        def _(pe):
            for i in range(4):
                pe.wait_ge(*squared.at(i + 1))
                for half in range(2):
                    mm = pe.matmul(K.bank[:, 2 * i + half, :], K.head_ones[:],
                                   sq[:, i, 2 * half:2 * half + 2, :].rearrange("p a t -> p (a t)"), start=True, stop=True)
                mm.then_inc(*summed.up())

        @block.vector
        def _(dve):
            link = Link(dve, vector_step)
            for i, (name, gain) in enumerate(sets):
                dve.wait_ge(*rooted.at(i + 1))
                link(dve.reciprocal(rt[:, i, :, :], rt[:, i, :, :]))
                dve.scalar_tensor_tensor(f[name], f[name], K.col(gain), rt[:, i, :, :], ALU.mult, ALU.mult)
    K.stage_end()


def forget_sums(K, f):
    nc = K.nc
    logged, vector_step, scalar_step = K.counts(3)
    e, one = K.take(LAT)[0:8, :], K.take(LAT)[0:8, :]
    z = f["fa"][0:8, :]
    with nc.Block() as block:
        @block.scalar
        def _(act):
            link = Link(act, scalar_step)
            link(act.activation(e, z, ACT.Abs))
            link(act.activation(e, e, ACT.Exp, scale=-1.0))
            act.activation(e, e, ACT.Ln, bias=K.small[0:8, 1:2], scale=1.0).then_inc(*logged.up())

        @block.vector
        def _(dve):
            link = Link(dve, vector_step)
            link(dve.memset(one, 1.0))
            dve.wait_ge(*logged.at(1))
            link(dve.scalar_tensor_tensor(e, z, 0.0, e, ALU.min, ALU.subtract))
            link(dve.tensor_tensor_scan(z, one, e, 0.0, ALU.mult, ALU.add))
            dve.tensor_scalar(z, z, -float(HD) ** 0.5, None, ALU.mult)
    K.stage_end()


NEG = 1e30


def attention_mask(K, addmask):
    with K.nc.Block() as block:
        @block.vector
        def _(dve):
            dve.memset(addmask[:, 0:P], 0.0)
            dve.tensor_scalar(addmask[:, P:2 * P], K.tri_b[:], 1.0, NEG, ALU.subtract, ALU.mult)


def attention(K, q, k, v, addmask, row_bias, o, sums, gate, add):
    nc = K.nc
    NS = 4
    s = K.take(NS, LAT)
    pt = K.take(NS, LT, P)
    top = K.take(NS, 2)
    tmp = K.take(BW)
    units = [(t, h) for t in range(LT) for h in range(NH)]
    scored, masked, negated, exped, turned, kept, used, finished, vector_step = K.counts(9)
    SCORE, TURN, OUT = 0, 2, 4
    with nc.Block() as block:
        @block.tensor
        def _(pe):
            def score(u):
                t, h = units[u]
                n = (t + 1) * P
                if u >= 2:
                    pe.wait_ge(*masked.at(u - 1))
                b = K.bank[:, SCORE + u % 2, 0:n]
                mm = pe.matmul(b, q(h)[:, t * P:t * P + P], k(h)[:, 0:n], start=True, stop=row_bias is None)
                if row_bias is not None:
                    mm = pe.matmul(b, K.ident[0:NH, h:h + 1].broadcast_to([NH, P]), row_bias[0:NH, 0:n],
                                   start=False, stop=True)
                mm.then_inc(*scored.up())

            def turn(u):
                t, h = units[u]
                pe.wait_ge(*exped.at(u + 1))
                if u >= 2:
                    pe.wait_ge(*kept.at(u - 1))
                for c in range(t + 1):
                    mm = pe.transpose(K.bank[:, TURN + u % 2, c * P:c * P + P], s[:, u % NS, c * P:c * P + P], K.ident[:])
                mm.then_inc(*turned.up())

            def weigh(u):
                t, h = units[u]
                pe.wait_ge(*kept.at(u + 1))
                for c in range(t + 1):
                    mm = pe.matmul(K.bank[:, OUT + t, h * HD:h * HD + HD], pt[:, u % NS, c, :], v(c, h),
                                   start=(c == 0), stop=(c == t))
                mm.then_inc(*used.up())

            n = len(units)
            for u in range(n + 3):
                if u < n:
                    score(u)
                if 1 <= u <= n:
                    turn(u - 1)
                if 2 <= u <= n + 1:
                    weigh(u - 2)

        @block.vector
        def _(dve):
            link = Link(dve, vector_step)
            for u, (t, h) in enumerate(units):
                n = (t + 1) * P
                w = s[:, u % NS, 0:n]
                dve.wait_ge(*scored.at(u + 1))
                if u >= NS:
                    dve.wait_ge(*turned.at(u - NS + 1))
                dve.scalar_tensor_tensor(w, K.bank[:, SCORE + u % 2, 0:n], HD ** -0.5, addmask[:, 2 * P - n:2 * P],
                                         ALU.mult, ALU.add).then_inc(*masked.up())
                dve.wait_ge(*masked.now())
                m = top[:, u % NS, :]
                link(dve.reduce_max(m[:, 0:1], w, AX.X))
                dve.tensor_scalar(m[:, 1:2], m[:, 0:1], -1.0, None, ALU.mult).then_inc(*negated.up())
            for t in range(LT):
                dve.wait_ge(*used.at(NH * t + NH))
                link(dve.reciprocal(sums[:, t, :], sums[:, t, :]))
                if gate is not None:
                    link(dve.tensor_tensor(sums[:, t, :], sums[:, t, :], gate(t), ALU.mult))
                dest = tmp if add else o[:, t, :]
                link(dve.tensor_tensor(dest.rearrange("p (h v) -> p h v", v=HD),
                                       K.bank[:, OUT + t, :].rearrange("p (h v) -> p h v", v=HD),
                                       last(sums[:, t, :], HD), ALU.mult))
                if add:
                    link(dve.tensor_tensor(o[:, t, :], o[:, t, :], tmp, ALU.add))

        @block.scalar
        def _(act):
            n = len(units)

            def keep(u):
                t, h = units[u]
                act.wait_ge(*turned.at(u + 1))
                if u >= NS:
                    act.wait_ge(*used.at(u - NS + 1))
                act.activation(pt[:, u % NS, 0:t + 1, :].rearrange("p c t -> p (c t)"),
                               K.bank[:, TURN + u % 2, 0:(t + 1) * P], ACT.Copy).then_inc(*kept.up())
            for u, (t, h) in enumerate(units):
                act.wait_ge(*negated.at(u + 1))
                w = s[:, u % NS, 0:(t + 1) * P]
                act.activation(w, w, ACT.Exp, bias=top[:, u % NS, 1:2], scale=1.0,
                               accum_out=sums[:, t, h:h + 1]).then_inc(*exped.up())
                if u:
                    keep(u - 1)
            keep(n - 1)
    K.stage_end()


def turn_gate(K, o, gate):
    nc = K.nc
    (turned,) = K.counts(1)
    with nc.Block() as block:
        @block.tensor
        def _(pe):
            for j in range(KB):
                for t in range(LT):
                    mm = pe.transpose(K.bank[:, j, t * P:t * P + P], o[:, t, j * P:j * P + P], K.ident[:])
                mm.then_inc(*turned.up())

        @block.vector
        def _(dve):
            for j in range(KB):
                dve.wait_ge(*turned.at(j + 1))
                dve.tensor_tensor(gate[:, j, :], gate[:, j, :], K.bank[:, j, 0:LAT], ALU.mult)
    K.stage_end()


def compressed_attention(K, f, o, sums):
    nc = K.nc
    S = 32
    w1 = (K.h[:].rearrange("p k t -> p (k t)").rearrange("p (c n) -> p c n", n=P), K.take(CB, P))
    w2 = K.take(2, P)
    tb = K.take(2, CB, NC)
    hid = K.take(4, NC)
    kn, rt, sq = K.take(2, NC), K.take(2, NC), K.take(2, NC)
    vblk = K.take(2, 4, HD)
    mask, neg = K.take(LT, NC), K.take(LT, NC)
    prob = K.take(LT, NH, S)
    peak = K.take(LT, NH)
    turned_p = K.take(LT, 2, P)
    loads, cleared, masks, posed, hidden, silued, keyed, squared, summed, rooted, normed, valued = K.counts(12)
    pool_step, vector_step = K.counts(2)
    with nc.Block() as block:
        @block.sync
        def _(sync):
            for i in range(2):
                sync.dma_start(w1[i], K.dram["cmp_w1"][:, i, :, :]).then_inc(*loads.up(16))
            sync.dma_start(w2, K.dram["cmp_w2"]).then_inc(*loads.up(16))

        @block.gpsimd
        def _(pool):
            link = Link(pool, pool_step)
            pool.memset(vblk, 0.0).then_inc(*cleared.up())
            pool.memset(prob, 0.0).then_inc(*cleared.up())
            link(pool.memset(mask, 1.0))
            for t in range(LT):
                pool.affine_select(out=mask[:, t, :], in_=mask[:, t, :], compare_op=ALU.is_ge, fill=0.0,
                                   base=t * P - (CB - 1), pattern=[[-CS, NC]], channel_multiplier=1).then_inc(*masks.up())

        @block.vector
        def _(dve):
            link = Link(dve, vector_step)
            for i, name in enumerate(("kc", "vc")):
                src = f[name][:, 0, :].rearrange("p (c b) -> p b c", b=CS)
                for a in range(CB // CS):
                    dve.tensor_tensor(tb[:, i, a * CS:a * CS + CS, :], src[:, :, a:a + NC],
                                      last(K.col("cmp_pos", a * CS, CS), NC), ALU.add).then_inc(*posed.up())
            dve.wait_ge(*masks.at(2))
            dve.tensor_scalar(neg, mask, 1.0, NEG, ALU.subtract, ALU.mult)
            dve.wait_ge(*rooted.at(1))
            link(dve.reciprocal(rt, rt))
            dve.scalar_tensor_tensor(kn, K.bank[:, 1, 0:2 * NC].rearrange("p (g c) -> p g c", c=NC), K.col("kn_c"), rt,
                                     ALU.mult, ALU.mult).then_inc(*normed.up())
            dve.wait_ge(*valued.at(1))
            dve.wait_ge(*cleared.at(2))
            for g in range(2):
                for j in range(4):
                    r = slice(S * j, S * j + NC)
                    dve.tensor_copy(vblk[r, g, j, :], K.bank[r, 3, g * HD:g * HD + HD])

        @block.tensor
        def _(pe):
            pe.wait_ge(*loads.at(48))
            pe.wait_ge(*posed.at(4))
            for i in range(2):
                for g in range(2):
                    r = slice(HD * g, HD * g + HD)
                    for c in range(CB):
                        mm = pe.matmul(K.bank[:, 4 * g, i * NC:i * NC + NC], w1[i][r, c, :],
                                       tb[r, i, c, :], start=(c == 0), stop=(c == CB - 1))
            mm.then_inc(*hidden.up())
            pe.wait_ge(*silued.at(1))
            for g in range(2):
                mm = pe.matmul(K.bank[:, 1, g * NC:g * NC + NC], w2[:, 0, :], hid[:, g, :], start=True, stop=True)
            mm.then_inc(*keyed.up())
            for g in range(2):
                for j in range(4):
                    mm = pe.matmul(K.bank[S * j:S * j + NC, 3, g * HD:g * HD + HD], hid[:, 2 + g, :], w2[:, 1, 0:HD],
                                   start=True, stop=True)
            mm.then_inc(*valued.up())
            pe.wait_ge(*squared.at(1))
            pe.matmul(K.bank[:, 2, 0:2 * NC], K.head_ones[:], sq.rearrange("p g c -> p (g c)"), start=True,
                      stop=True).then_inc(*summed.up())

        @block.scalar
        def _(act):
            act.wait_ge(*hidden.at(1))
            for g in range(2):
                ins = act.activation(hid[:, g:g + 3:2, :], K.bank[:, 4 * g, 0:2 * NC].rearrange("p (i c) -> p i c", c=NC),
                                     ACT.Silu)
            ins.then_inc(*silued.up())
            act.wait_ge(*keyed.at(1))
            act.activation(sq.rearrange("p g c -> p (g c)"), K.bank[:, 1, 0:2 * NC], ACT.Square).then_inc(*squared.up())
            act.wait_ge(*summed.at(1))
            act.activation(rt.rearrange("p g c -> p (g c)"), K.bank[:, 2, 0:2 * NC], ACT.Sqrt, bias=K.small[:, 0:1],
                           scale=1.0 / HD).then_inc(*rooted.up())
    K.stage_end()

    scored, shifted, exped, ready, turned, kept, made, vector_step = K.counts(8)
    live = prob[:, :, :, 0:NC]
    with nc.Block() as block:
        @block.tensor
        def _(pe):
            for t in range(LT):
                for h in range(NH):
                    r = slice(HD * (h % 2), HD * (h % 2) + HD)
                    mm = pe.matmul(K.bank[:, 2 * t + h % 2, (h // 2) * S:(h // 2) * S + NC], f["qc"][r, h // 2, t * P:t * P + P], kn[r, h // 4, :],
                                   start=True, stop=True)
                mm.then_inc(*scored.up())
            for t in range(LT):
                pe.wait_ge(*ready.at(t + 1))
                for g in range(2):
                    mm = pe.transpose(K.bank[:, 4 + t, g * P:g * P + P],
                                      prob[:, t, 4 * g:4 * g + 4, :].rearrange("p h s -> p (h s)"), K.ident[:])
                mm.then_inc(*turned.up())
            for t in range(LT):
                pe.wait_ge(*kept.at(t + 1))
                for g in range(2):
                    mm = pe.matmul(K.bank[:, 6 + t, g * 256:g * 256 + 256], turned_p[:, t, g, :],
                                   vblk[:, g, :, :].rearrange("p j v -> p (j v)"), start=True, stop=True)
                mm.then_inc(*made.up())

        @block.vector
        def _(dve):
            link = Link(dve, vector_step)
            for t in range(LT):
                dve.wait_ge(*scored.at(t + 1))
                for e in range(2):
                    sv = K.bank[:, 2 * t + e, 0:4 * S].rearrange("p (h s) -> p h s", s=S)[:, :, 0:NC]
                    link(dve.scalar_tensor_tensor(live[:, t, e:NH:2, :], sv, HD ** -0.5, mid(neg[:, t, :], 4), ALU.mult,
                                                  ALU.add))
                link(dve.tensor_reduce(peak[:, t, :], live[:, t, :, :], AX.X, ALU.max))
                dve.tensor_tensor(live[:, t, :, :], live[:, t, :, :], last(peak[:, t, :], NC),
                                  ALU.subtract).then_inc(*shifted.up())
            for t in range(LT):
                dve.wait_ge(*exped.at(t + 1))
                link(dve.tensor_reduce(sums[:, t, :], live[:, t, :, :], AX.X, ALU.add))
                dve.tensor_tensor(live[:, t, :, :], live[:, t, :, :], mid(mask[:, t, :], NH), ALU.mult).then_inc(*ready.up())
            for t in range(LT):
                dve.wait_ge(*made.at(t + 1))
                link(dve.reciprocal(sums[:, t, :], sums[:, t, :]))
                link(dve.tensor_tensor(sums[:, t, :], sums[:, t, :], f["gate"][:, t, 0:NH], ALU.mult))
                dve.tensor_tensor(o[:, t, :].rearrange("p (h v) -> p h v", v=HD),
                                  K.bank[:, 6 + t, :].rearrange("p (h v) -> p h v", v=HD),
                                  last(sums[:, t, :], HD), ALU.mult)

        @block.scalar
        def _(act):
            for t in range(LT):
                act.wait_ge(*shifted.at(t + 1))
                act.activation(live[:, t, :, :], live[:, t, :, :], ACT.Exp).then_inc(*exped.up())
            for t in range(LT):
                act.wait_ge(*turned.at(t + 1))
                act.activation(turned_p[:, t, :, :].rearrange("p g t -> p (g t)"), K.bank[:, 4 + t, 0:2 * P],
                               ACT.Copy).then_inc(*kept.up())
    K.stage_end()


def recurrence(K, f):
    nc = K.nc
    W = 4
    xc, r, ig, a, m = (K.take(KB, LAT) for _ in range(5))
    wg = K.take(2, KB, P)
    sp = K.take(5, KB)
    loads, centred, conved, gated, sigmoided, absed, logged, decays, exped, tanhed, scaled, rooted = K.counts(12)
    vector_step, scalar_step = K.counts(2)
    with nc.Block() as block:
        @block.sync
        def _(sync):
            sync.dma_start(wg, K.dram["rg_w"]).then_inc(*loads.up(16))

        @block.scalar
        def _(act):
            link = Link(act, scalar_step)
            for j in range(KB):
                ins = act.activation(xc[:, j, :], f["xb"][:, j, :], ACT.Identity, bias=K.col("lru_conv_b", j),
                                     scale=K.col("lru_conv_w", 3 * KB + j))
            ins.then_inc(*centred.up())
            link(act.activation(sp[:, 0, :], K.col("lam", 0, KB), ACT.Abs))
            act.activation(sp[:, 0, :], sp[:, 0, :], ACT.Exp, scale=-1.0).then_inc(*absed.up())
            act.wait_ge(*gated.at(1))
            for j in range(KB):
                act.activation(r[:, j, :], K.bank[:, j, 0:LAT], ACT.Sigmoid, bias=K.col("b_rg_a", j), scale=1.0)
                ins = act.activation(ig[:, j, :], K.bank[:, j, LAT:2 * LAT], ACT.Sigmoid, bias=K.col("b_rg_x", j), scale=1.0)
            ins.then_inc(*sigmoided.up())
            act.wait_ge(*decays.at(1))
            act.activation(a, r, ACT.Exp, scale=-1.0).then_inc(*exped.up())
            act.activation(m, r, ACT.Tanh).then_inc(*tanhed.up())
            act.wait_ge(*scaled.at(1))
            act.activation(m, m, ACT.Sqrt).then_inc(*rooted.up())

        @block.vector
        def _(dve):
            link = Link(dve, vector_step)
            dve.wait_ge(*centred.at(1))
            for j in range(KB):
                for tap in range(W - 1):
                    s = W - 1 - tap
                    ins = dve.scalar_tensor_tensor(xc[:, j, s:LAT], f["xb"][:, j, 0:LAT - s],
                                                   K.col("lru_conv_w", tap * KB + j), xc[:, j, s:LAT], ALU.mult, ALU.add)
                    if j == KB - 1 and tap == W - 2:
                        ins.then_inc(*conved.up())
                    else:
                        link(ins)
            dve.wait_ge(*absed.at(1))
            log1p_small(link, dve, sp[:, 0, :], sp[:, 1, :], sp[:, 2, :], sp[:, 3, :])
            link(dve.tensor_scalar(sp[:, 4, :], K.col("lam", 0, KB), -1.0, 0.0, ALU.mult, ALU.max))
            link(dve.tensor_tensor(sp[:, 0, :], sp[:, 0, :], sp[:, 4, :], ALU.add))
            dve.wait_ge(*sigmoided.at(1))
            for j in range(KB):
                ins = dve.tensor_scalar(r[:, j, :], r[:, j, :], sp[:, 0, j:j + 1], 8.0, ALU.mult, ALU.mult)
            ins.then_inc(*decays.up())
            link(dve.tensor_tensor(ig, ig, xc, ALU.mult))
            dve.wait_ge(*tanhed.at(1))
            link(dve.tensor_tensor(xc, a, a, ALU.mult))
            dve.scalar_tensor_tensor(m, xc, 1.0, m, ALU.add, ALU.mult).then_inc(*scaled.up())
            dve.wait_ge(*rooted.at(1))
            link(dve.tensor_tensor(m, m, ig, ALU.mult))
            for j in range(KB):
                link(dve.tensor_tensor_scan(xc[:, j, :], a[:, j, :], m[:, j, :], 0.0, ALU.mult, ALU.add))
            dve.tensor_tensor(f["gb"], f["gb"], xc, ALU.mult)

        @block.tensor
        def _(pe):
            pe.wait_ge(*loads.at(16))
            pe.wait_ge(*conved.at(1))
            for j in range(KB):
                for gate in range(2):
                    mm = pe.matmul(K.bank[:, j, gate * LAT:gate * LAT + LAT], wg[:, gate, j, :], xc[:, j, :],
                                   start=True, stop=True)
            mm.then_inc(*gated.up())
    K.stage_end()


def spatial_gating(K, f):
    nc = K.nc
    ws, bs, ln = K.take(8, P), K.take(P), K.take(BW)
    mean, var = K.take(LT), K.take(LT)
    squares = K.take(LT, BW)
    loads, masked, centred, squared, rooted, normed, mixed, vector_step = K.counts(8)
    with nc.Block() as block:
        @block.sync
        def _(sync):
            sync.dma_start(ws, K.dram["spatial_w"]).then_inc(*loads.up(16))
            sync.dma_start(bs[0:8, :], K.dram["spatial_b"]).then_inc(*loads.up(16))
            sync.dma_start(ln, K.dram["ln_v_g"].partition_broadcast(P)).then_inc(*loads.up(16))

        @block.vector
        def _(dve):
            link = Link(dve, vector_step)
            for t in range(LT):
                link(dve.reduce_sum(mean[:, t:t + 1], f["vd"][:, t, :], AX.X))
                link(dve.tensor_scalar(mean[:, t:t + 1], mean[:, t:t + 1], 1.0 / BW, None, ALU.mult))
                dve.tensor_scalar(f["vd"][:, t, :], f["vd"][:, t, :], mean[:, t:t + 1], None,
                                  ALU.subtract).then_inc(*centred.up())
            dve.wait_ge(*loads.at(48))
            link(dve.tensor_tensor(ws, ws, mid(K.tri_f[:], 8), ALU.mult))
            dve.wait_ge(*rooted.at(1))
            link(dve.reciprocal(var, var))
            for t in range(LT):
                dve.scalar_tensor_tensor(f["vd"][:, t, :], f["vd"][:, t, :], var[:, t:t + 1], ln, ALU.mult,
                                         ALU.mult).then_inc(*normed.up())
            for j in range(KB):
                dve.wait_ge(*mixed.at(j + 1))
                link(dve.tensor_tensor(f["ud"][:, j, :], f["ud"][:, j, :], K.bank[:, j, 0:LAT], ALU.mult))
                dve.tensor_tensor(f["gd"][:, j, :], f["gd"][:, j, :], f["ud"][:, j, :], ALU.mult)

        @block.scalar
        def _(act):
            for t in range(LT):
                act.wait_ge(*centred.at(t + 1))
                ins = act.activation(squares[:, t, :], f["vd"][:, t, :], ACT.Square, accum_out=var[:, t:t + 1])
            ins.then_inc(*squared.up())
            act.wait_ge(*squared.at(1))
            act.activation(var, var, ACT.Sqrt, bias=K.small[:, 0:1], scale=1.0 / BW).then_inc(*rooted.up())

        @block.tensor
        def _(pe):
            pe.wait_ge(*normed.at(LT))
            for j in range(KB):
                for c in range(LT):
                    for e in range(2):
                        g = 2 * j + e
                        b = K.bank[HD * e:HD * e + HD, j, c * P:c * P + P]
                        pe.matmul(b, f["vd"][:, c, g * HD:g * HD + HD], ws[:, g, :], start=True, stop=False)
                        mm = pe.matmul(b, K.ident[0:8, g:g + 1].broadcast_to([8, HD]), bs[0:8, :], start=False, stop=True)
                mm.then_inc(*mixed.up())
    K.stage_end()


def merge(K, f, out):
    nc = K.nc
    branches = ("ga", "gb", "gc", "gd")
    tmp = K.take(LAT)
    first = FIRST_TILE["branch2"]
    rounds = []
    for n in range(KD):
        for b, name in enumerate(branches):
            def empty(dve, link, bank, n=n, b=b):
                dest = K.h[:, n, 0:LAT]
                if b == 0:
                    return dve.tensor_tensor(dest, bank[:, 0:LAT], f["mg"][:, b * KD + n, :], ALU.mult)
                link(dve.tensor_tensor(tmp, bank[:, 0:LAT], f["mg"][:, b * KD + n, :], ALU.mult))
                return dve.tensor_tensor(dest, dest, tmp, ALU.add)
            rounds.append([Item(tile_products(K, first + (n * 4 + b) * KB, KB, lambda k, name=name: f[name][:, k, :], LAT),
                                empty, "dve")])
    run_products(K, rounds, first + KD * 4 * KB)
    run_products(K, residual_items(K, "out2", KD, lambda k: K.h[:, k, 0:LAT], CTX, None), FIRST_TILE["out2"] + 64)
    (stored,) = K.counts(1)
    with nc.Block() as block:
        @block.sync
        def _(sync):
            sync.dma_start(out, K.x[:, :, CTX:T]).then_inc(*stored.up(16))
            sync.wait_ge(*stored.at(16))
    K.stage_end()


def build(nc, dram, out, stop=None):
    with ExitStack() as ctx:
        K = Kit(nc, ctx, dram)
        setup(K)
        modulations(K, 0)
        normalise(K, 0, lambda k: K.h[:, k, :], "mix_g0", (0, 0, 8))
        even_mixer(K)
        feed_forward(K, 0, 0)
        modulations(K, 1)
        normalise(K, 0, lambda k: K.h[:, k, :], "mix_g1", (1, 0, 8))
        odd_mixer(K)
        feed_forward(K, 1, CTX)
        hybrid_layer(K, out)


def feature_columns(a):
    return a.reshape(-1, P).T


def feature_tiles(w):
    k, n = w.shape
    return w.reshape(k // P, P, n // P, P).transpose(2, 0, 1, 3).reshape(-1, P, P)


def token_tiles(w):
    k, n = w.shape
    return w.reshape(k // P, P, n // P, P).transpose(0, 2, 1, 3).reshape(-1, P, P)


def rows_to_partitions(w):
    return w.reshape(-1, P, w.shape[1]).transpose(1, 0, 2)


def lay_out(v):
    f32 = np.float32
    parts = {}
    for l in range(2):
        parts[f"mod{l}"] = [feature_tiles(v["mod_w"][l])]
        up = v["ffn_w_up"][l]
        pair = np.concatenate([up[:, :FF].reshape(D, KF, 1, P), up[:, FF:].reshape(D, KF, 1, P)], axis=2)
        parts[f"up{l}"] = [feature_tiles(pair.reshape(D, 2 * FF))]
        parts[f"down{l}"] = [feature_tiles(v["ffn_w_down"][l])]
    w = v["even_w_in"][0]
    gq, gk, gv, gg, mq, mk, mv, mo, mg = np.split(w, np.cumsum([256, 256, 512, 512, 512, 512, 512, 512]), axis=1)
    parts["even_in"] = [feature_tiles(x) for x in (gq, gk, gg)] + [token_tiles(x) for x in (gv, mv, mo)] + \
                       [feature_tiles(x) for x in (mq, mk)]
    parts["even_out"] = [feature_tiles(v["even_w_out"][0])]
    small = np.zeros((D, 176), f32)
    small[:, 0:16], small[:, 32:48] = v["gla_a1"][0, 0], v["gla_a1"][0, 1]
    small[:, 48:52], small[:, 80:84] = mg[:, 0:4], mg[:, 8:12]
    small[:, 112:116], small[:, 144:148] = mg[:, 4:8], mg[:, 12:16]
    a2 = np.zeros((48, 256), f32)
    a2[0:16], a2[32:48] = v["gla_a2"][0, 0], v["gla_a2"][0, 1]

    w = v["ssd_w_in"][0]
    parts["ssd_in"] = [feature_tiles(w[:, SI:SI + 3072]), feature_tiles(w[:, 0:SI])]
    parts["ssd_out"] = [feature_tiles(v["ssd_w_out"][0])]

    w = v["w_in_2"][0]
    names = ["qa", "ka", "va", "fa", "ga", "xb", "gb", "qc", "kc", "vc", "ks", "vs", "kw", "vw", "gate", "gc", "ud", "vd",
             "gd", "mg"]
    sizes = [BW, BW, BW, NH, BW, BW, BW, BW] + [128] * 6 + [24] + [BW] * 4 + [4096]
    z = dict(zip(names, np.split(w, np.cumsum(sizes)[:-1], axis=1)))
    z["kd"] = np.concatenate([z[n][:, g * HD:g * HD + HD] for n in ("ks", "kw") for g in (0, 0, 1, 1)], axis=1)
    parts["in2"] = []
    for name, n, _func in IN2:
        if name == "ud":
            parts["in2"] += [token_tiles(z["va"]), token_tiles(np.concatenate([z["vs"], z["vw"]], axis=1)),
                             token_tiles(z["vd"])]
        parts["in2"].append(feature_tiles(z[name]))
    wb = v["w_branch_2"][0].reshape(4, KB, P, KD, P).transpose(3, 0, 1, 2, 4)
    parts["branch2"] = [wb.reshape(-1, P, P)]
    parts["out2"] = [feature_tiles(v["w_out_2"][0])]
    tiles = np.concatenate([t for name, _n in SEGMENTS for t in parts[name]], axis=0)
    weights = tiles.reshape(N_BLOCKS, TPB, P, P).transpose(0, 2, 1, 3).reshape(N_BLOCKS, P, TPB * P)

    cols = np.zeros((P, N_COLS), f32)

    def put(name, a):
        a = np.asarray(a)
        cols[0:a.shape[0], COL[name]:COL[name] + a.shape[1]] = a

    def taps(w):
        return np.concatenate([feature_columns(t) for t in w], axis=1)

    for l in range(2):
        put(f"mod_b{l}", feature_columns(v["mod_b"][l]))
        put(f"mix_g{l}", feature_columns(v["norm_mix_g"][l]))
        put(f"ffn_g{l}", feature_columns(v["norm_ffn_g"][l]))
        put(f"conv_w{l}", taps(v["ffn_conv_w"][l].reshape(9, 2 * FF)))
        put(f"conv_b{l}", feature_columns(v["ffn_conv_b"][l]))
    put("final_g", feature_columns(v["final_norm_g"]))
    put("gla_ab", feature_columns(v["gla_ab"][0].reshape(-1)))
    put("ml_conv_w", taps(v["ml_conv_w"][0]))
    put("ml_conv_b", feature_columns(v["ml_conv_b"][0]))
    put("gla_norm", feature_columns(v["gla_norm_g"][0]))
    put("ml_norm", feature_columns(v["ml_norm_g"][0]))
    gb = v["ml_gate_b"][0]
    for name, a in (("ml_li_b", 0), ("ml_lf_b", 4)):
        cols[0:4, COL[name]], cols[32:36, COL[name]] = gb[a:a + 4], gb[8 + a:12 + a]
    put("ssd_conv_w", taps(v["ssd_conv_w"][0]))
    put("ssd_conv_b", feature_columns(v["ssd_conv_b"][0]))
    put("ssd_d", feature_columns(np.repeat(v["ssd_d"][0], SP)))
    put("ssd_norm", feature_columns(v["ssd_norm_g"][0]))
    put("ssd_dt_b", v["ssd_dt_bias"][0].reshape(64, 1))
    put("ssd_a_log", v["ssd_a_log"][0].reshape(64, 1))
    put("norm2", feature_columns(v["norm_g_2"][0]))
    for name in ("qn_a", "kn_a", "qn_c", "kn_c"):
        put(name, np.tile(v[name + "_2"][0], 2).reshape(P, 1))
    put("b_forget", v["b_forget_2"][0].reshape(NH, 1))
    put("lru_conv_w", taps(v["conv_w_2"][0]))
    put("lru_conv_b", feature_columns(v["conv_b_2"][0]))
    put("b_rg_a", feature_columns(v["b_rg_a_2"][0]))
    put("b_rg_x", feature_columns(v["b_rg_x_2"][0]))
    put("lam", feature_columns(v["lru_lambda_2"][0]))
    put("cmp_pos", np.tile(v["cmp_pos_2"][0].T, (2, 1)))
    put("cond", np.stack([feature_columns(v["c"][0]), feature_columns(v["c_ctx"])], axis=2).reshape(P, 16))

    tokens = np.concatenate([v["ctx"][0], v["x"][0]], axis=0)
    w1 = np.stack([v["cmp_k_w1_2"][0], v["cmp_v_w1_2"][0]]).reshape(2, CB, HD, P).transpose(2, 0, 1, 3)
    w2 = np.stack([np.tile(v[n][0], (1, 2)) for n in ("cmp_k_w2_2", "cmp_v_w2_2")], axis=1)
    rg = np.zeros((2, HD, 2, KB, 2, HD), f32)
    for gate, name in enumerate(("w_rg_a_2", "w_rg_x_2")):
        for e in range(2):
            rg[e, :, gate, :, e, :] = v[name][0][e::2].transpose(1, 0, 2)
    return {
        "weights": weights,
        "columns": cols,
        "tokens": rows_to_partitions(tokens.T),
        "even_small": rows_to_partitions(small),
        "gla_a2": a2,
        "ssd_dt_w": rows_to_partitions(v["ssd_w_in"][0][:, SI + 3072:]),
        "fa_w": rows_to_partitions(z["fa"]),
        "gate_w": rows_to_partitions(z["gate"]),
        "cmp_w1": np.concatenate([w1, w1], axis=0),
        "cmp_w2": w2,
        "rg_w": rg.reshape(P, 2, KB, P),
        "spatial_w": v["w_spatial_2"][0].transpose(2, 0, 1),
        "spatial_b": v["b_spatial_2"][0],
        "ln_v_g": v["ln_v_g_2"][0],
    }


def kernel(**inputs):
    import concourse.bacc as bacc
    from concourse.bass_utils import run_bass_kernel_spmd

    laid = {name: np.ascontiguousarray(a) for name, a in lay_out({k: np.asarray(a) for k, a in inputs.items()}).items()}
    nc = bacc.Bacc("TRN2", target_bir_lowering=False, num_devices=1)
    dram = {name: nc.dram_tensor("in_" + name, a.shape, F32, kind="ExternalInput").ap() for name, a in laid.items()}
    out = nc.dram_tensor("out", (P, KD, LAT), F32, kind="ExternalOutput").ap()
    build(nc, dram, out)
    r = run_bass_kernel_spmd(nc, [{"in_" + name: a for name, a in laid.items()}], core_ids=[0])
    y = r.results[0]["out"]
    return y.transpose(2, 1, 0).reshape(1, LAT, D)
```

```python
from contextlib import ExitStack, contextmanager

import numpy as np

import concourse.bass as bass
from concourse import mybir

F32 = mybir.dt.float32
F32R = mybir.dt.float32r
BF16 = mybir.dt.bfloat16
I32 = mybir.dt.int32
ALU = mybir.AluOpType
ACT = mybir.ActivationFunctionType
AX = mybir.AxisListType

P = 128
D = 1024
KD = D // P
CTX, LAT = 256, 256
T = CTX + LAT
TT = T // P
LT = LAT // P
GRID_W = 64
ROWS = LAT // GRID_W
EPS = 1e-6
FF = 2816
KF = FF // P
GH, GK, GV = 4, 64, 128
GW = GH * GV
GLEVELS = 7
GTAU = 16.0
MH, MD = 4, 128
SH, SP, SN, SG = 32, 64, 128, 4
SI = SH * SP
KI = SI // P
HD = 64
NH = 8
BW = 512
KB = BW // P
CB, CS = 32, 16
NC = (LAT - CB) // CS + 1
BANKS = 8
TPB = 8
RING = 5
PARTS = 3

SEGMENTS = [
    ("mod0", 48 * KD), ("mod1", 48 * KD), ("even_in", 31 * KD), ("even_out", 8 * 8), ("up0", 2 * KF * KD),
    ("down0", 8 * KF), ("ssd_in", 41 * KD), ("ssd_out", 8 * KI), ("up1", 2 * KF * KD), ("down1", 8 * KF),
    ("in2", 86 * KD), ("branch2", 8 * 4 * KB), ("out2", 8 * KD),
]
FIRST_TILE, N_TILES = {}, {}
_n = 0
for _name, _count in SEGMENTS:
    FIRST_TILE[_name], N_TILES[_name] = _n, _count
    _n += _count
    assert _count % TPB == 0
N_BLOCKS = _n // TPB


def blocks_of(name):
    first = FIRST_TILE[name] // TPB
    return list(range(first, first + N_TILES[name] // TPB))


def spread_among(few, many):
    out, placed = [], 0
    for i, b in enumerate(many):
        while placed < len(few) * (i + 1) // len(many):
            out.append(few[placed])
            placed += 1
        out.append(b)
    return out


MOD_FIRST = 16
MOD_EVEN = 16
STREAM = blocks_of("mod0")[:MOD_FIRST] \
    + spread_among(blocks_of("mod0")[MOD_FIRST:] + blocks_of("mod1")[:MOD_EVEN], blocks_of("even_in")) \
    + blocks_of("even_out") + blocks_of("up0") + spread_among(blocks_of("mod1")[MOD_EVEN:], blocks_of("down0"))
for _name in ("ssd_in", "ssd_out", "up1", "down1", "in2", "branch2", "out2"):
    STREAM += blocks_of(_name)
PLACE = {b: i for i, b in enumerate(STREAM)}
assert sorted(STREAM) == list(range(N_BLOCKS))

COLUMNS = [
    ("mod_b0", 48), ("mod_b1", 48), ("mix_g0", 8), ("mix_g1", 8), ("ffn_g0", 8), ("ffn_g1", 8), ("final_g", 8),
    ("conv_w0", 9 * 44), ("conv_w1", 9 * 44), ("conv_b0", 44), ("conv_b1", 44), ("gla_ab", 4),
    ("ml_conv_w", 24), ("ml_conv_b", 8), ("gla_norm", 4), ("ml_norm", 4), ("ml_li_b", 1), ("ml_lf_b", 1),
    ("ssd_conv_w", 72), ("ssd_conv_b", 24), ("ssd_d", 16), ("ssd_norm", 16), ("ssd_dt_b", 1), ("ssd_a_log", 1),
    ("norm2", 8), ("qn_a", 1), ("kn_a", 1), ("qn_c", 1), ("kn_c", 1), ("b_forget", 1), ("lru_conv_w", 16),
    ("lru_conv_b", 4), ("b_rg_a", 4), ("b_rg_x", 4), ("lam", 4), ("cmp_pos", 32),
]
COL = {}
_n = 0
for _name, _count in COLUMNS:
    COL[_name] = _n
    _n += _count
N_COLS = _n


class Count:

    def __init__(self, sem):
        self.sem, self.base, self.total = sem, 0, 0

    def up(self, n=1):
        self.total += n
        return self.sem, n

    def at(self, n):
        return self.sem, self.base + n

    def now(self):
        return self.sem, self.total


class Kit:

    def __init__(self, nc, ctx, dram):
        self.nc, self.dram = nc, dram
        self.scopes = [ctx]
        self.n_taken = 0

        def sb(name, shape, dtype=F32):
            return ctx.enter_context(nc.sbuf_tensor(name, shape, dtype))

        self.ring = sb("weight_ring", [P, RING, TPB * P])
        self.x = sb("x", [P, KD, T])
        self.h_hi, self.h_lo = sb("h_high", [P, KD * T], F32R), sb("h_low", [P, KD * T], F32R)
        self.cols = sb("columns", [P, N_COLS])
        self.mod = sb("modulation", [P, 2, 48, 2])
        self.ident = sb("identity", [P, P])
        self.ones = sb("ones", [P, P])
        self.head_ones = sb("head_ones", [P, P])
        self.tri_f = sb("tri_f", [P, P])
        self.tri_b = sb("tri_b", [P, P])
        self.small = sb("small", [P, 8])
        self.bank = ctx.enter_context(nc.psum_tensor("banks", [P, BANKS, 512], F32))

        def count(name):
            return Count(ctx.enter_context(nc.semaphore(name)))

        self.loaded = [count(f"weights_loaded{i}") for i in range(RING)]
        self.mod_done = count("modulation_steps")
        self.high_done = count("weights_high_done")
        self.low_done = {"dve": count("weights_low_done_dve"), "pool": count("weights_low_done_pool")}
        self.used = count("weights_used")
        self.done = count("products_done")
        self.release = {}
        self.parts_ready = []
        self.parts_used = []
        self.pool = [count(f"stage_signal{i}") for i in range(40)]
        self.free = list(self.pool)
        self.issued = 0

    def col(self, name, i=0, n=1, rows=slice(0, P)):
        return self.cols[rows, COL[name] + i:COL[name] + i + n]

    def counts(self, n):
        return [self.free.pop() for _ in range(n)]

    def stage_end(self):
        for s in self.pool:
            s.base = s.total
        self.free = list(self.pool)

    @contextmanager
    def scope(self):
        with ExitStack() as ctx:
            self.scopes.append(ctx)
            yield
            self.scopes.pop()

    def take(self, *shape, dtype=F32):
        self.n_taken += 1
        t = self.scopes[-1].enter_context(self.nc.sbuf_tensor(f"m{self.n_taken}", [P, int(np.prod(shape))], dtype))
        names = "abcde"[:len(shape)]
        if len(shape) == 1:
            return t[:]
        return t[:].rearrange(f"p ({' '.join(names)}) -> p {' '.join(names)}", **dict(zip(names[1:], shape[1:])))

    def h_parts(self, width, k, a=0, b=None):
        b = width if b is None else b
        return self.h_hi[:, k * width + a:k * width + b], self.h_lo[:, k * width + a:k * width + b]


def load_weights(K, sync, last_place):
    last = min(N_BLOCKS, last_place + RING)
    while K.issued < last:
        i = K.issued
        if i >= RING:
            sync.wait_ge(*K.release[i - RING])
        sync.dma_start(K.ring[:, i % RING, :], K.dram["weights"][i]).then_inc(*K.loaded[i % RING].up(16))
        K.issued += 1


def wait_loaded(K, eng, place):
    eng.wait_ge(K.loaded[place % RING].sem, 16 * (place // RING + 1))


class Link:

    def __init__(self, eng, step):
        self.eng, self.step = eng, step

    def __call__(self, ins):
        ins.then_inc(*self.step.up())
        self.eng.wait_ge(*self.step.now())


def bc(ap, shape):
    return ap.broadcast_to(shape)


def mid(ap, n):
    return ap.unsqueeze(1).broadcast_to([ap.shape[0], n, ap.shape[1]])


def last(ap, n):
    return ap.unsqueeze(2).broadcast_to([ap.shape[0], ap.shape[1], n])



class Product:

    def __init__(self, out, tile, a, start, stop, ends, n=1, moving=False):
        self.out, self.tile, self.a, self.start, self.stop, self.ends = out, tile, a, start, stop, ends
        self.n, self.moving = n, moving


class Item:

    def __init__(self, products, empty, on="act", conv=None):
        self.products, self.empty, self.on, self.conv = products, empty, on, conv


class Conv:

    def __init__(self, n, centre, bias, taps, finish, post=None):
        self.n, self.centre, self.bias, self.taps, self.finish, self.post = n, centre, bias, taps, finish, post


def tile_products(tile, nk, a, n):
    return [Product(lambda o: o[:, 0:n], tile + k, a(k), k == 0, k == nk - 1, (tile + k) % TPB == TPB - 1)
            for k in range(nk)]


def token_products(K, tile, width_h, tokens, width, cols=None):
    n = -(-width // P)
    groups = [[] for _ in tokens]
    for k in range(KD):
        t = tile + k * n
        for i, tok in enumerate(tokens):
            ends = i == len(tokens) - 1 and (t + n) % TPB == 0
            groups[i].append(Product(lambda o: o[:, 0:width], t, K.h_parts(width_h, k, tok * P, tok * P + P),
                                     k == 0, k == KD - 1, ends, width / P, True))
    return groups


def run_products(K, rounds, low_on="dve", mods=None):
    with K.scope():
        _run_products(K, rounds, low_on, mods)


def _run_products(K, rounds, low_on, mods):
    nc = K.nc
    free_act, free_dve, tapped, finished, posted, vector_step = K.counts(6)
    w_hi, w_lo = K.take(PARTS, TPB * P, dtype=F32R), K.take(PARTS, TPB * P, dtype=F32R)
    items = [it for r in rounds for it in r]
    free = {"act": free_act, "dve": free_dve}
    rank, count = [], {"act": 0, "dve": 0}
    for it in items:
        count[it.on] += 1
        rank.append(count[it.on])
    convs = [e for e, it in enumerate(items) if it.conv]
    RAW, ACC, LAG = 3, 6, 2
    finishes = np.cumsum([items[e].conv.finish is not None for e in convs]).tolist()
    posts = np.cumsum([items[e].conv.post is not None for e in convs]).tolist()
    if convs:
        n = max(items[e].conv.n for e in convs)
        raw, acc = K.take(RAW, n), K.take(ACC, n)
    done0 = K.done.total
    first = items[0].products[0].tile // TPB
    last_of = [it.products[-1].tile // TPB - first for it in items]
    n_blocks = last_of[-1] + 1
    part0 = len(K.parts_ready)
    last_place = PLACE[first + n_blocks - 1] + 1
    mod_places = [(PLACE[b], b) for b in (mods[1] if mods else [])]

    for i in range(n_blocks):
        K.low_done[low_on].total += 1
        K.parts_ready.append(K.low_done[low_on].now())
        K.release[PLACE[first + i]] = K.low_done[low_on].now()
    if mods:
        mods[0].plan(mods[1])

    with nc.Block() as block:
        @block.tensor
        def _(pe):
            e, seen = 0, -1
            for r in rounds:
                for j in range(len(r)):
                    if e + j >= BANKS:
                        q = e + j - BANKS
                        pe.wait_ge(*free[items[q].on].at(rank[q]))
                for k in range(len(r[0].products)):
                    for j, it in enumerate(r):
                        p = it.products[k]
                        b = p.tile // TPB - first
                        if b != seen:
                            seen = b
                            pe.wait_ge(*K.parts_ready[part0 + b])
                        slot, at = (part0 + b) % PARTS, p.tile % TPB * P
                        wh, wl = (w[:, slot, at:at + int(p.n * P)] for w in (w_hi, w_lo))
                        out = p.out(K.bank[:, (e + j) % BANKS, :])
                        if p.moving:
                            passes = ((p.a[0], wh), (p.a[0], wl), (p.a[1], wh))
                        else:
                            passes = ((wh, p.a[0]), (wh, p.a[1]), (wl, p.a[0]))
                        for i, (lhsT, rhs) in enumerate(passes):
                            mm = pe.matmul(out, lhsT, rhs, start=p.start and i == 0, stop=p.stop and i == 2)
                        done = K.done if k == len(it.products) - 1 else K.used if p.ends else None
                        if done is not None:
                            mm.then_inc(*done.up())
                        if p.ends:
                            K.parts_used.append(done.now())
                e += len(r)

        @block.sync
        def _(sync):
            load_weights(K, sync, last_place)

        def high_part(act, i):
            wait_loaded(K, act, PLACE[first + i])
            if i >= PARTS:
                act.wait_ge(*K.parts_used[part0 + i - PARTS])
            act.activation(w_hi[:, (part0 + i) % PARTS, :], K.ring[:, PLACE[first + i] % RING, :],
                           ACT.Copy).then_inc(*K.high_done.up())

        def low_part(eng, i):
            slot = (part0 + i) % PARTS
            eng.wait_ge(K.high_done.sem, part0 + i + 1)
            eng.tensor_tensor(w_lo[:, slot, :], K.ring[:, PLACE[first + i] % RING, :], w_hi[:, slot, :].bitcast(F32),
                              ALU.subtract).then_inc(K.low_done[low_on].sem, 1)

        @block.scalar
        def _(act):
            def finish(i):
                c = items[convs[i]].conv
                if c.finish is None:
                    return
                act.wait_ge(*tapped.at(i + 1))
                c.finish(act, acc[:, i % ACC, 0:c.n]).then_inc(*finished.up())

            n_conv = n_high = 0
            for e, it in enumerate(items):
                while n_high < min(n_blocks, last_of[e] + PARTS):
                    high_part(act, n_high)
                    n_high += 1
                if it.on != "act":
                    continue
                act.wait_ge(K.done.sem, done0 + e + 1)
                bank = K.bank[:, e % BANKS, :]
                if not it.conv:
                    it.empty(act, bank).then_inc(*free_act.up())
                    continue
                c, i = it.conv, n_conv
                if i >= RAW:
                    act.wait_ge(*tapped.at(i - RAW + 1))
                if i >= ACC:
                    old = posts[i - ACC + 1] if items[convs[i - ACC + 1]].conv.post else posts[i - ACC]
                    if old:
                        act.wait_ge(*posted.at(old))
                    if finishes[i - ACC]:
                        act.wait_ge(*finished.at(finishes[i - ACC]))
                act.activation(acc[:, i % ACC, 0:c.n], bank[:, 0:c.n], ACT.Identity, bias=c.bias, scale=c.centre)
                act.activation(raw[:, i % RAW, 0:c.n], bank[:, 0:c.n], ACT.Copy).then_inc(*free_act.up())
                n_conv += 1
                if i >= LAG:
                    finish(i - LAG)
            for i in range(max(0, n_conv - LAG), n_conv):
                finish(i)

        @block.vector
        def _(dve):
            def post(i):
                c = items[convs[i]].conv
                if c.post is not None:
                    dve.wait_ge(*finished.at(finishes[i]))
                    c.post(dve, link, acc[:, (i - 1) % ACC, 0:c.n], acc[:, i % ACC, 0:c.n]).then_inc(*posted.up())

            link = Link(dve, vector_step)
            i = n_low = 0
            for e, it in enumerate(items):
                while mod_places and mod_places[0][0] < PLACE[first + min(n_blocks, last_of[e] + PARTS) - 1]:
                    mods[0].block(dve, *mod_places.pop(0))
                while low_on == "dve" and n_low < min(n_blocks, last_of[e] + PARTS):
                    low_part(dve, n_low)
                    n_low += 1
                if it.on == "dve":
                    dve.wait_ge(K.done.sem, done0 + e + 1)
                    it.empty(dve, link, K.bank[:, e % BANKS, :]).then_inc(*free_dve.up())
                    dve.wait_ge(*free_dve.now())
                if it.conv:
                    dve.wait_ge(*free_act.at(rank[e]))
                    for t, (region, shift, w) in enumerate(it.conv.taps):
                        o = region(acc[:, i % ACC, 0:it.conv.n])
                        ins = dve.scalar_tensor_tensor(o, shift(raw[:, i % RAW, 0:it.conv.n]), w, o, ALU.mult, ALU.add)
                        if t == len(it.conv.taps) - 1:
                            ins.then_inc(*tapped.up())
                        else:
                            link(ins)
                    if i >= LAG + 1:
                        post(i - LAG - 1)
                    i += 1
            for j in range(max(0, i - LAG - 1), i):
                post(j)
            if mods:
                mods[0].end(dve, mods[1])

        @block.gpsimd
        def _(pool):
            if low_on == "pool":
                for i in range(n_blocks):
                    low_part(pool, i)
    K.stage_end()


class Modulator:

    def __init__(self, K, cond):
        self.K, self.cond = K, cond
        self.unread = K.take(2, D, dtype=BF16)
        self.planned = K.mod_done.total

    def plan(self, blocks):
        for b in blocks:
            self.planned += 2
            self.K.release[PLACE[b]] = (self.K.mod_done.sem, self.planned)

    def block(self, dve, place, b):
        K = self.K
        layer, j = divmod(b - FIRST_TILE["mod0"] // TPB, 48)
        wait_loaded(K, dve, place)
        for c in range(2):
            if K.mod_done.total >= 2:
                dve.wait_ge(K.mod_done.sem, K.mod_done.total - 1)
            dve.scalar_tensor_tensor(self.unread[:, c, :], K.ring[:, place % RING, :], 1.0, self.cond[:, c, :],
                                     ALU.mult, ALU.mult, accum_out=K.mod[:, layer, j, c:c + 1]).then_inc(*K.mod_done.up())

    def end(self, dve, blocks):
        K = self.K
        dve.wait_ge(*K.mod_done.now())
        first = FIRST_TILE["mod0"] // TPB
        for layer in range(2):
            js = [b - first - 48 * layer for b in blocks if (b - first) // 48 == layer]
            if js:
                m = K.mod[:, layer, js[0]:js[-1] + 1, :]
                dve.tensor_tensor(m, m, last(K.col(f"mod_b{layer}", js[0], len(js)), 2), ALU.add)


def conv_taps_1d(w, n_regions=2):
    def view(a):
        return a.rearrange("p (r t) -> p r t", r=n_regions)
    n = 256
    return [(lambda o: view(o)[:, :, 1:n], lambda r: view(r)[:, :, 0:n - 1], w(0)),
            (lambda o: view(o)[:, :, 0:n - 1], lambda r: view(r)[:, :, 1:n], w(2))]


def conv_taps_ffn(w, with_ctx):
    taps = []
    lat0 = CTX if with_ctx else 0

    def grid(a, r0, r1, c0, c1):
        return a[:, lat0:lat0 + LAT].rearrange("p (r c) -> p r c", c=GRID_W)[:, r0:r1, c0:c1]

    for i in range(3):
        for j in range(3):
            if i == 1 and j == 1:
                continue
            di, dj = i - 1, j - 1
            r0, r1 = max(0, -di), ROWS - max(0, di)
            c0, c1 = max(0, -dj), GRID_W - max(0, dj)
            taps.append((lambda o, r0=r0, r1=r1, c0=c0, c1=c1: grid(o, r0, r1, c0, c1),
                         lambda a, r0=r0 + di, r1=r1 + di, c0=c0 + dj, c1=c1 + dj: grid(a, r0, r1, c0, c1),
                         w(3 * i + j)))
    if with_ctx:
        taps.append((lambda o: o[:, 1:CTX], lambda a: a[:, 0:CTX - 1], w(3)))
        taps.append((lambda o: o[:, 0:CTX - 1], lambda a: a[:, 1:CTX], w(5)))
    return taps


REGIONS = [(0, CTX, 1), (CTX, T, 0)]


def residual_items(K, segment, nk, a, t0, gate):
    items = []
    for n in range(KD):
        def empty(dve, link, bank, n=n):
            for a, b, which in REGIONS:
                if a < t0:
                    continue
                xs, ps = K.x[:, n, a:b], bank[:, a - t0:b - t0]
                if gate is None:
                    ins = dve.tensor_tensor(xs, ps, xs, ALU.add)
                else:
                    ins = dve.scalar_tensor_tensor(xs, ps, gate(n, which), xs, ALU.mult, ALU.add)
            return ins
        items.append([Item(tile_products(FIRST_TILE[segment] + n * nk, nk, a, T - t0), empty, "dve")])
    return items


def normalise(K, t0, gain, shift_scale=None, into_x=False):
    with K.scope():
        _normalise(K, t0, gain, shift_scale, into_x)


def _normalise(K, t0, gain, shift_scale, into_x):
    nc, n = K.nc, T - t0
    squared, summed, rooted, scaled, normed, whole, high, vector_step, scalar_step = K.counts(9)
    sq, std, rstd, amp = K.take(KD, n), K.take(n), K.take(n), K.take(2, KD)
    out = K.x[:, :, t0:T] if into_x else K.take(KD, n)

    with nc.Block() as block:
        @block.scalar
        def _(act):
            for k in range(KD):
                act.activation(sq[:, k, :], K.x[:, k, t0:T], ACT.Square).then_inc(*squared.up())
            act.wait_ge(*summed.at(1))
            act.activation(std, K.bank[:, 0, 0:n], ACT.Sqrt, bias=K.small[:, 0:1], scale=1.0 / D).then_inc(*rooted.up())
            if shift_scale:
                layer, shift, scale = shift_scale
                act.wait_ge(*scaled.at(1))
            if into_x:
                return

            def high_part(k):
                act.wait_ge(*(whole if shift_scale else normed).at(k + 1))
                act.activation(K.h_parts(n, k)[0], out[:, k, :], ACT.Copy).then_inc(*high.up())
            for k in range(KD):
                if shift_scale:
                    act.wait_ge(*normed.at(k + 1))
                    for a, b, which in REGIONS:
                        if a >= t0:
                            ins = act.activation(out[:, k, a - t0:b - t0], out[:, k, a - t0:b - t0], ACT.Identity,
                                                 bias=K.mod[:, layer, shift + k, which:which + 1],
                                                 scale=amp[:, which, k:k + 1])
                    ins.then_inc(*whole.up())
                    if k:
                        high_part(k - 1)
                else:
                    high_part(k)
            if shift_scale:
                high_part(KD - 1)

        @block.tensor
        def _(pe):
            for k in range(KD):
                pe.wait_ge(*squared.at(k + 1))
                mm = pe.matmul(K.bank[:, 0, 0:n], K.ones[:], sq[:, k, :], start=(k == 0), stop=(k == KD - 1))
            mm.then_inc(*summed.up())

        @block.vector
        def _(dve):
            link = Link(dve, vector_step)
            if shift_scale:
                layer, shift, scale = shift_scale
                for which in range(2):
                    ins = dve.scalar_tensor_tensor(amp[:, which, :], K.mod[:, layer, scale:scale + KD, which], 1.0,
                                                   K.col(gain, 0, KD), ALU.add, ALU.mult)
                ins.then_inc(*scaled.up())
            dve.wait_ge(*rooted.at(1))
            link(dve.reciprocal(rstd, std))
            for k in range(KD):
                if shift_scale:
                    dve.tensor_tensor(out[:, k, :], K.x[:, k, t0:T], rstd, ALU.mult).then_inc(*normed.up())
                else:
                    dve.scalar_tensor_tensor(out[:, k, :], K.x[:, k, t0:T], K.col(gain, k), rstd, ALU.mult,
                                             ALU.mult).then_inc(*normed.up())
            if into_x:
                return
            for k in range(KD):
                hi, lo = K.h_parts(n, k)
                dve.wait_ge(*high.at(k + 1))
                dve.tensor_tensor(lo, out[:, k, :], hi.bitcast(F32), ALU.subtract)
    K.stage_end()


def split(K, pairs):
    (high,) = K.counts(1)
    with K.nc.Block() as block:
        @block.scalar
        def _(act):
            for whole, hi, lo in pairs:
                act.activation(hi, whole, ACT.Copy).then_inc(*high.up())

        @block.vector
        def _(dve):
            for i, (whole, hi, lo) in enumerate(pairs):
                dve.wait_ge(*high.at(i + 1))
                dve.tensor_tensor(lo, whole, hi.bitcast(F32), ALU.subtract)
    K.stage_end()


def setup(K, cond, modulator):
    nc = K.nc
    filled, conds, loads, tokens, silued = K.counts(5)
    blocks = blocks_of("mod0")[:MOD_FIRST]
    modulator.plan(blocks)

    with nc.Block() as block:
        @block.gpsimd
        def _(pool):
            link = Link(pool, filled)
            for i, v in enumerate((EPS, 1.0, 0.0)):
                link(pool.memset(K.small[:, i:i + 1], v))
            for a, v in ((K.ones, 1.0), (K.ident, 0.0), (K.head_ones, 0.0), (K.tri_f, 1.0), (K.tri_b, 1.0)):
                link(pool.memset(a[:], v))
            link(pool.memset(K.head_ones[0:HD, 0:HD], 1.0))
            link(pool.memset(K.head_ones[HD:P, HD:P], 1.0))
            link(pool.affine_select(out=K.ident[:], in_=K.ident[:], compare_op=ALU.not_equal, fill=1.0, base=0,
                                    pattern=[[-1, P]], channel_multiplier=1))
            link(pool.affine_select(out=K.tri_f[:], in_=K.tri_f[:], compare_op=ALU.is_ge, fill=0.0, base=0,
                                    pattern=[[1, P]], channel_multiplier=-1))
            link(pool.affine_select(out=K.tri_b[:], in_=K.tri_b[:], compare_op=ALU.is_ge, fill=0.0, base=0,
                                    pattern=[[-1, P]], channel_multiplier=1))

        @block.sync
        def _(sync):
            for c in range(2):
                sync.dma_start(cond[:, c, :], K.dram["cond"][c].partition_broadcast(P)).then_inc(*conds.up(16))
            sync.dma_start(K.cols[:], K.dram["columns"]).then_inc(*loads.up(16))
            load_weights(K, sync, MOD_FIRST)
            sync.dma_start(K.x[:], K.dram["tokens"]).then_inc(*tokens.up(16))
            sync.wait_ge(*tokens.at(16))

        @block.scalar
        def _(act):
            act.wait_ge(*conds.at(32))
            act.activation(cond, cond, ACT.Silu).then_inc(*silued.up())

        @block.vector
        def _(dve):
            dve.wait_ge(*silued.at(1))
            for b in blocks:
                modulator.block(dve, PLACE[b], b)
            dve.wait_ge(*loads.at(16))
            modulator.end(dve, blocks)
    K.stage_end()


def feed_forward(K, layer, t0, mods=None):
    n = T - t0
    normalise(K, t0, f"ffn_g{layer}", (layer, 24, 32))
    with K.scope():
        gated_hi, gated_lo = K.take(KF, n, dtype=F32R), K.take(KF, n, dtype=F32R)
        rounds = []
        first = FIRST_TILE[f"up{layer}"]
        for j in range(KF):
            for half in range(2):
                c = half * KF + j

                def finish(act, acc):
                    return act.activation(acc, acc, ACT.Silu)

                def post(dve, link, a, g, j=j):
                    link(dve.tensor_tensor(g, a, g, ALU.mult))
                    link(dve.tensor_copy(gated_hi[:, j, :], g))
                    return dve.tensor_tensor(gated_lo[:, j, :], g, gated_hi[:, j, :].bitcast(F32), ALU.subtract)
                conv = Conv(n, K.col(f"conv_w{layer}", 4 * 44 + c), K.col(f"conv_b{layer}", c),
                            conv_taps_ffn(lambda tap, c=c: K.col(f"conv_w{layer}", tap * 44 + c), t0 == 0),
                            finish if half else None, post if half else None)
                rounds.append([Item(tile_products(first + (2 * j + half) * KD, KD, lambda k: K.h_parts(n, k), n),
                                    None, "act", conv)])
        run_products(K, rounds, "pool")
        rounds = residual_items(K, f"down{layer}", KF, lambda k: (gated_hi[:, k, :], gated_lo[:, k, :]), t0,
                                lambda m, which: K.mod[:, layer, 40 + m, which:which + 1])
        if not mods:
            run_products(K, rounds)
            return
        with K.scope():
            modulator = Modulator(K, K.take(2, D))
            conditions(K, modulator.cond)
            run_products(K, rounds, "pool", (modulator, mods))


def conditions(K, cond):
    (conds,) = K.counts(1)
    with K.nc.Block() as block:
        @block.sync
        def _(sync):
            for c in range(2):
                sync.dma_start(cond[:, c, :], K.dram["cond"][c].partition_broadcast(P)).then_inc(*conds.up(16))

        @block.scalar
        def _(act):
            act.wait_ge(*conds.at(32))
            act.activation(cond, cond, ACT.Silu)
    K.stage_end()


def even_mixer(K, cond_top):
    f, cum = cond_top
    with K.scope():
        gla(K, f, cum)
    with K.scope():
        mlstm(K, f)
    split(K, [(f[name][:, j, :], *K.h_parts(T, base + j)) for name, base in (("gg", 0), ("mq", 4)) for j in range(4)])
    run_products(K, residual_items(K, "even_out", KD, lambda k: K.h_parts(T, k), 0,
                                   lambda m, which: K.mod[:, 0, 16 + m, which:which + 1]))


def even_features(K):
    f = {}
    f["gq"], f["gk"], f["gg"] = K.take(2, T), K.take(2, T), K.take(4, T)
    f["mq"], f["mk"] = K.take(4, T), K.take(4, T)
    f["gv"], f["mv"], f["mo"] = K.take(TT, GW), K.take(TT, MH, MD + 1), K.take(TT, GW)
    f["low"], f["li"], f["lf"] = K.take(T), K.take(T), K.take(T)
    return f, K.take(4, T)


def even_projection(K, f, a2, modulator):
    first = FIRST_TILE["even_in"]
    rounds, tile = [], first

    def h(k):
        return K.h_parts(T, k)

    def put(dest, func, scale=1.0):
        return lambda act, bank: act.activation(dest, bank[0:dest.shape[0], :], func, scale=scale)

    for name, n, func, scale in (("gq", 2, ACT.Copy, GK ** -0.5), ("gk", 2, ACT.Copy, 1.0), ("gg", 4, ACT.Silu, 1.0)):
        for j in range(n):
            rounds.append([Item(tile_products(tile, KD, h, T), put(f[name][:, j, :], func, scale))])
            tile += KD
    for name, base in (("mq", 0), ("mk", 4)):
        for j in range(4):
            c = base + j

            def finish(act, acc, name=name, j=j):
                return act.activation(f[name][:, j, :], acc, ACT.Silu)
            conv = Conv(T, K.col("ml_conv_w", 8 + c), K.col("ml_conv_b", c),
                        conv_taps_1d(lambda tap, c=c: K.col("ml_conv_w", tap * 8 + c)), finish)
            rounds.append([Item(tile_products(tile, KD, h, T), None, "act", conv)])
            tile += KD
    for name in ("gv", "mv", "mo"):
        groups = token_products(K, tile, T, range(TT), GW)

        def empty(i, name=name):
            if name == "mv":
                return lambda act, bank: act.activation(f["mv"][:, i, :, 0:MD],
                                                        bank.rearrange("p (h v) -> p h v", v=MD), ACT.Copy)
            return put(f[name][:, i, :], ACT.Sigmoid if name == "mo" else ACT.Copy)
        rounds.append([Item(g, empty(i)) for i, g in enumerate(groups)])
        tile += 4 * KD
    for dest, m, bias in ((f["low"], 48, None), (f["li"], 36, "ml_li_b"), (f["lf"], 36, "ml_lf_b")):
        def empty(act, bank, dest=dest, m=m, bias=bias):
            if bias is None:
                return act.activation(dest[0:m, :], bank[0:m, :], ACT.Copy)
            return act.activation(dest[0:m, :], bank[0:m, :], ACT.Identity, bias=K.col(bias, rows=slice(0, m)), scale=1.0)
        rounds.append([Item(tile_products(tile, KD, h, T), empty)])
        tile += KD
    run_products(K, rounds, "pool", (modulator, blocks_of("mod0")[MOD_FIRST:] + blocks_of("mod1")[:MOD_EVEN]))
    (loads,) = K.counts(1)
    with K.nc.Block() as block:
        @block.sync
        def _(sync):
            sync.dma_start(a2[0:48, :], K.dram["gla_a2"]).then_inc(*loads.up(16))
            sync.wait_ge(*loads.at(16))

        @block.gpsimd
        def _(pool):
            pool.memset(f["mv"][:, :, :, MD:MD + 1], 1.0)
    K.stage_end()


def gla_decays(K, f, a2, la):
    nc = K.nc
    ready, biased, absed, logged, combined, vector_step, scalar_step = K.counts(7)
    e = K.take(4, T)
    z = la
    with nc.Block() as block:
        @block.tensor
        def _(pe):
            for d in range(2):
                for pair in range(2):
                    r = slice(32 * d, 32 * d + 16)
                    pe.matmul(K.bank[:, 2 * d + pair, :], a2[r, pair * P:pair * P + P], f["low"][r, :],
                              start=True, stop=True).then_inc(*ready.up())

        @block.scalar
        def _(act):
            link = Link(act, scalar_step)
            for i in range(4):
                act.wait_ge(*ready.at(i + 1))
                link(act.activation(z[:, i, :], K.bank[:, i, :], ACT.Identity, bias=K.col("gla_ab", i), scale=1.0))
            link(act.activation(e, z, ACT.Abs))
            link(act.activation(e, e, ACT.Exp, scale=-1.0))
            act.activation(e, e, ACT.Ln, bias=K.small[:, 1:2], scale=1.0).then_inc(*logged.up())

        @block.vector
        def _(dve):
            link = Link(dve, vector_step)
            dve.wait_ge(*logged.at(1))
            link(dve.tensor_scalar(z, z, 0.0, 1.0 / GTAU, ALU.min, ALU.mult))
            link(dve.scalar_tensor_tensor(e, e, -1.0 / GTAU, z, ALU.mult, ALU.add))
            for d in range(2):
                for pair in range(2):
                    for c in range(TT):
                        a, o = e[:, 2 * d + pair, c * P:c * P + P], z[:, 2 * d + pair, c * P:c * P + P]
                        if d:
                            a, o = a[:, ::-1], o[:, ::-1]
                        dve.tensor_tensor_scan(o, K.ones[:], a, 0.0, ALU.mult, ALU.add)
    K.stage_end()


CHUNK_ORDER = ([0, 1, 2, 3], [1, 0, 3, 2])


def gla(K, f, cum):
    nc = K.nc
    dp = 4
    factor = K.take(dp, T)
    qe, ke = K.take(dp, T), K.take(dp, T)
    att = K.take(2, TT, 2, P)
    masks = K.take(2 * GLEVELS, P)
    kend_t = factor.rearrange("p a (c t) -> p a c t", c=TT)
    state = K.take(dp, 3, P)
    cend = K.take(dp, TT)
    qv = lambda: f["gq"].unsqueeze(1).broadcast_to([P, 2, 2, T])
    kv = lambda: f["gk"].unsqueeze(1).broadcast_to([P, 2, 2, T])
    as4 = lambda a: a.rearrange("p (d q) t -> p d q t", q=2)

    (mask_step,) = K.counts(1)
    with nc.Block() as block:
        @block.gpsimd
        def _(pool):
            link = Link(pool, mask_step)
            link(pool.memset(masks, 0.0))
            for d in range(2):
                for l in range(1, GLEVELS + 1):
                    size, half = 1 << l, 1 << (l - 1)
                    m = masks[:, d * GLEVELS + l - 1, :].rearrange("p (b w) -> p b w", w=size)
                    t_half = m[:, :, half:size] if d == 0 else m[:, :, 0:half]
                    s_from = half if d else 0
                    n = P // size
                    link(pool.memset(t_half, 1.0))
                    link(pool.affine_select(out=t_half, in_=t_half, compare_op=ALU.is_ge, fill=0.0, base=-s_from,
                                            pattern=[[-size, n], [0, half]], channel_multiplier=1))
                    link(pool.affine_select(out=t_half, in_=t_half, compare_op=ALU.is_ge, fill=0.0,
                                            base=s_from + half - 1, pattern=[[size, n], [0, half]],
                                            channel_multiplier=-1))
    K.stage_end()

    differences, exps, qe_done, ke_done, read, scored, taken, vector_step, scalar_step = K.counts(9)
    done0 = [0]
    with nc.Block() as block:
        @block.vector
        def _(dve):
            link = Link(dve, vector_step)
            n_bank = 0

            def take_scores(l, d):
                nonlocal n_bank
                for i in range(4):
                    n_bank += 1
                    dve.wait_ge(*scored.at(n_bank))
                    if n_bank > 4:
                        dve.wait_ge(*taken.at(n_bank - 4))
                    b = K.bank[:, (n_bank - 1) % BANKS, :].rearrange("p (h t) -> p h t", t=P)
                    o = att[:, i % 2, 2 * (i // 2):2 * (i // 2) + 2, :, :].rearrange("p c h t -> p (c h) t")
                    if l == 0:
                        dve.tensor_scalar(o, b, 2.0, None, ALU.mult).then_inc(*taken.up())
                    else:
                        m = mid(masks[:, d * GLEVELS + l - 1, :].bitcast(I32), 4)
                        dve.copy_predicated(o, m, b).then_inc(*taken.up())

            for l in range(1, GLEVELS + 1):
                size, half = 1 << l, 1 << (l - 1)
                for d in range(2):
                    view = cum[:, 2 * d:2 * d + 2, :].rearrange("p a (b w) -> p (a b) w", w=size)
                    at = half if d else half - 1
                    o = factor[:, 2 * d:2 * d + 2, :].rearrange("p a (b w) -> p (a b) w", w=size)
                    ins = dve.tensor_tensor(o, view, view[:, :, at:at + 1].broadcast_to([P, 2 * T // size, size]),
                                            ALU.subtract)
                ins.then_inc(*differences.up())
                if l == 1:
                    take_scores(0, 0)
                else:
                    for d in range(2):
                        take_scores(l - 1, d)
                dve.wait_ge(*exps.at(l))
                dve.tensor_tensor(as4(qe), as4(factor), qv(), ALU.mult).then_inc(*qe_done.up())
                dve.tensor_tensor(as4(ke), as4(factor), kv(), ALU.mult).then_inc(*ke_done.up())
                dve.wait_ge(*ke_done.now())
            for d in range(2):
                take_scores(GLEVELS, d)
            for d in range(2):
                view = cum[:, 2 * d:2 * d + 2, :].rearrange("p a (b w) -> p (a b) w", w=P)
                at = 0 if d else P - 1
                o = factor[:, 2 * d:2 * d + 2, :].rearrange("p a (b w) -> p (a b) w", w=P)
                dve.tensor_copy(cend[:, 2 * d:2 * d + 2, :].rearrange("p a b -> p (a b)").unsqueeze(2),
                                view[:, :, at:at + 1])
                ins = dve.tensor_tensor(o, view, view[:, :, at:at + 1].broadcast_to([P, 2 * TT, P]), ALU.subtract)
            ins.then_inc(*differences.up())
            dve.wait_ge(*exps.at(GLEVELS + 1))
            dve.tensor_tensor(as4(ke), as4(factor), kv(), ALU.mult).then_inc(*qe_done.up())
            dve.wait_ge(*exps.at(GLEVELS + 2))
            dve.tensor_tensor(as4(qe), as4(cum), qv(), ALU.mult)

        @block.scalar
        def _(act):
            link = Link(act, scalar_step)
            for l in range(1, GLEVELS + 2):
                act.wait_ge(*differences.at(l))
                link(act.activation(factor, factor, ACT.Abs))
                act.activation(factor, factor, ACT.Exp, scale=-1.0).then_inc(*exps.up())
            act.activation(cend, cend, ACT.Exp)
            act.activation(cum, cum, ACT.Exp).then_inc(*exps.up())

        @block.tensor
        def _(pe):
            n = 0

            def scores(q, k):
                nonlocal n
                for i in range(4):
                    if n >= BANKS:
                        pe.wait_ge(*taken.at(n - BANKS + 1))
                    r = slice(GK * (i % 2), GK * (i % 2) + GK)
                    for j in range(4):
                        c, pair = 2 * (i // 2) + j // 2, j % 2
                        mm = pe.matmul(K.bank[:, n % BANKS, j * P:j * P + P], k[r, pair, c * P:c * P + P],
                                       q[r, pair, c * P:c * P + P], start=True, stop=True)
                    mm.then_inc(*scored.up())
                    n += 1
            scores(f["gq"], f["gk"])
            for l in range(1, GLEVELS + 1):
                pe.wait_ge(*ke_done.at(l))
                for d in range(2):
                    scores(qe[:, 2 * d:2 * d + 2, :], ke[:, 2 * d:2 * d + 2, :])
    K.stage_end()
    gla_states(K, f, ke, kend_t, cend, state)
    gla_outputs(K, f, att, qe, state, factor, ke)


def gla_states(K, f, ke, kend_t, cend, state):
    nc = K.nc
    turned, kept, summed, updated = K.counts(4)
    with nc.Block() as block:
        @block.tensor
        def _(pe):
            for i in range(4):
                for c in range(TT):
                    mm = pe.transpose(K.bank[:, i, c * P:c * P + P], ke[:, i, c * P:c * P + P], K.ident[:])
                mm.then_inc(*turned.up())
            for step in range(3):
                for i in range(4):
                    c = CHUNK_ORDER[i // 2][step]
                    if step == 0:
                        pe.wait_ge(*kept.at(i + 1))
                    if step:
                        pe.wait_ge(*updated.at(4 * (step - 1) + i + 1))
                    for h in range(2):
                        head = 2 * (i % 2) + h
                        mm = pe.matmul(K.bank[GK * h:GK * h + GK, 4 + i, 0:GV], kend_t[:, i, c, GK * h:GK * h + GK],
                                       f["gv"][:, c, head * GV:head * GV + GV], start=True, stop=True)
                    mm.then_inc(*summed.up())

        @block.scalar
        def _(act):
            for i in range(4):
                act.wait_ge(*turned.at(i + 1))
                act.activation(kend_t[:, i, :, :], K.bank[:, i, :].rearrange("p (c k) -> p c k", k=P),
                               ACT.Copy).then_inc(*kept.up())

        @block.vector
        def _(dve):
            for step in range(3):
                for i in range(4):
                    c = CHUNK_ORDER[i // 2][step]
                    dve.wait_ge(*summed.at(4 * step + i + 1))
                    if step == 0:
                        dve.tensor_copy(state[:, i, 0, :], K.bank[:, 4 + i, 0:GV]).then_inc(*updated.up())
                    else:
                        dve.wait_ge(*updated.at(4 * (step - 1) + i + 1))
                        dve.scalar_tensor_tensor(state[:, i, step, :], state[:, i, step - 1, :], cend[:, i, c:c + 1],
                                                 K.bank[:, 4 + i, 0:GV], ALU.mult, ALU.add).then_inc(*updated.up())
    K.stage_end()


def gla_outputs(K, f, att, qc, state, spare, unread):
    nc = K.nc
    made, squared, rooted, scaled, turned, gated, vector_step = K.counts(7)
    on = spare.rearrange("p a t -> p (a t)").rearrange("p (c v) -> p c v", v=GW)
    squares = unread.rearrange("p a t -> p (a t)").rearrange("p (i v) -> p i v", v=GV)
    ss, rt = K.take(TT, GH), K.take(TT, GH)

    def bank(c, h):
        return K.bank[:, 4 * (h % 2) + c, (h // 2) * GV:(h // 2) * GV + GV]

    with nc.Block() as block:
        @block.tensor
        def _(pe):
            for c in range(TT):
                for h in range(GH):
                    o = bank(c, h)
                    mms = [(att[:, h % 2, c, h // 2, :], f["gv"][:, c, h * GV:h * GV + GV])]
                    r = slice(GK * (h % 2), GK * (h % 2) + GK)
                    for d in range(2):
                        pos = CHUNK_ORDER[d].index(c)
                        if pos:
                            i = 2 * d + h // 2
                            mms.append((qc[r, i, c * P:c * P + P], state[r, i, pos - 1, :]))
                    for j, (a, b) in enumerate(mms):
                        mm = pe.matmul(o, a, b, start=(j == 0), stop=(j == len(mms) - 1))
                mm.then_inc(*made.up())
            for c in range(TT):
                pe.wait_ge(*scaled.at(c + 1))
                for h in range(GH):
                    mm = pe.transpose(K.bank[:, c, h * P:h * P + P], on[:, c, h * GV:h * GV + GV], K.ident[:])
                mm.then_inc(*turned.up())

        @block.scalar
        def _(act):
            for c in range(TT):
                act.wait_ge(*made.at(c + 1))
                for h in range(GH):
                    ins = act.activation(squares[:, GH * c + h, :], bank(c, h), ACT.Square,
                                         accum_out=ss[:, c, h:h + 1])
            ins.then_inc(*squared.up())
            act.wait_ge(*squared.at(1))
            act.activation(rt, ss, ACT.Sqrt, bias=K.small[:, 0:1], scale=1.0 / GV).then_inc(*rooted.up())

        @block.vector
        def _(dve):
            link = Link(dve, vector_step)
            dve.wait_ge(*rooted.at(1))
            link(dve.reciprocal(rt, rt))
            for c in range(TT):
                for e in range(2):
                    ins = dve.tensor_tensor(on[:, c, :].rearrange("p (h v) -> p h v", v=GV)[:, e:GH:2, :],
                                            K.bank[:, 4 * e + c, 0:2 * GV].rearrange("p (h v) -> p h v", v=GV),
                                            last(rt[:, c, e:GH:2], GV), ALU.mult)
                ins.then_inc(*scaled.up())
            for c in range(TT):
                dve.wait_ge(*turned.at(c + 1))
                for h in range(GH):
                    dve.scalar_tensor_tensor(f["gg"][:, h, c * P:c * P + P], K.bank[:, c, h * P:h * P + P],
                                             K.col("gla_norm", h), f["gg"][:, h, c * P:c * P + P], ALU.mult, ALU.mult)
    K.stage_end()


def mlstm_key_tiles(d):
    if d == 0:
        return [(s, [(s, TT)]) for s in range(TT)]
    return [(0, [(0, 1), (2, 4)]), (1, [(0, 4)]), (2, [(2, 3)]), (3, [(2, 4)])]


def mlstm(K, f):
    nc = K.nc
    R = 36
    li, lf = f["li"][0:R, :], f["lf"][0:R, :]
    e, run, peak, em = K.take(T)[0:R, :], K.take(T)[0:R, :], K.take(T)[0:R, :], K.take(T)[0:R, :]
    gcol, ecol = K.take(TT, R), K.take(TT, R)
    step_a, step_v, logged, peaks, ems = K.counts(5)
    ones_r = K.take(T)
    with nc.Block() as block:
        @block.gpsimd
        def _(pool):
            pool.memset(ones_r, 1.0).then_inc(*peaks.up())
            pool.memset(run, 0.0).then_inc(*peaks.up())
            pool.memset(peak, 0.0).then_inc(*peaks.up())

        @block.scalar
        def _(act):
            link = Link(act, step_a)
            link(act.activation(e, lf, ACT.Abs))
            link(act.activation(e, e, ACT.Exp, scale=-1.0))
            act.activation(e, e, ACT.Ln, bias=K.small[0:R, 1:2], scale=1.0).then_inc(*logged.up())
            act.wait_ge(*ems.at(1))
            act.activation(em, em, ACT.Exp, scale=-1.0)

        @block.vector
        def _(dve):
            link = Link(dve, step_v)
            dve.wait_ge(*logged.at(1))
            link(dve.scalar_tensor_tensor(e, lf, 0.0, e, ALU.min, ALU.subtract))
            dve.wait_ge(*peaks.at(3))

            def scans(out, data0, src, op0, op1):
                link(dve.tensor_tensor_scan(out[0:4, :], data0(0, slice(0, T)), src[0:4, :], 0.0, op0, op1))
                b = slice(32, 36)
                link(dve.tensor_tensor_scan(out[b, 0:CTX][:, ::-1], data0(32, slice(0, CTX))[:, ::-1],
                                            src[b, 0:CTX][:, ::-1], 0.0, op0, op1))
                link(dve.tensor_tensor_scan(out[b, CTX:T][:, ::-1], data0(32, slice(CTX, T))[:, ::-1],
                                            src[b, CTX:T][:, ::-1], out[b, 0:1], op0, op1))
            scans(run, lambda r, c: ones_r[r:r + 4, c], e, ALU.mult, ALU.add)
            link(dve.tensor_tensor(li, li, run, ALU.subtract))
            scans(peak, lambda r, c: li[r:r + 4, c], li, ALU.max, ALU.max)
            dve.tensor_tensor(em, run, peak, ALU.add).then_inc(*ems.up())
    K.stage_end()

    turned, = K.counts(1)
    with nc.Block() as block:
        @block.tensor
        def _(pe):
            for c in range(TT):
                pe.transpose(K.bank[:, 0, c * R:c * R + R], li[:, c * P:c * P + P], K.ident[0:R, 0:R])
                mm = pe.transpose(K.bank[:, 1, c * R:c * R + R], em[:, c * P:c * P + P], K.ident[0:R, 0:R])
            mm.then_inc(*turned.up())

        @block.scalar
        def _(act):
            act.wait_ge(*turned.at(1))
            act.activation(gcol.rearrange("p c r -> p (c r)"), K.bank[:, 0, 0:TT * R], ACT.Copy)
            act.activation(ecol.rearrange("p c r -> p (c r)"), K.bank[:, 1, 0:TT * R], ACT.Copy)
    K.stage_end()

    W = K.take(2, TT, T)
    hacc = K.take(TT, GW)
    den = K.take(2, TT)
    raised, qk_done, bounded, exped, weighted, used, made, unit_done, vector_step = K.counts(9)
    PEAK, QK, OUT = 0, 1, 5
    with nc.Block() as block:
        @block.tensor
        def _(pe):
            def scores(h):
                if h:
                    pe.wait_ge(*weighted.at(2 * h))
                for s in range(TT):
                    mm = pe.matmul(K.bank[:, QK + s, :], f["mk"][:, h, s * P:s * P + P], f["mq"][:, h, :],
                                   start=True, stop=True)
                mm.then_inc(*qk_done.up())

            def spread(u):
                h, d = u // 2, u % 2
                if u:
                    pe.wait_ge(*bounded.at(u))
                r = h + 32 * d
                pe.matmul(K.bank[:, PEAK, :], K.ident[0:R, r:r + 1].broadcast_to([R, P]), peak,
                          start=True, stop=True).then_inc(*raised.up())

            spread(0)
            for u in range(2 * MH):
                h, d = u // 2, u % 2
                if d == 0:
                    scores(h)
                if u + 1 < 2 * MH:
                    spread(u + 1)
                pe.wait_ge(*weighted.at(u + 1))
                if u:
                    pe.wait_ge(*unit_done.at(u))
                tiles = mlstm_key_tiles(d)
                for t in range(TT):
                    seen = [s for s, ranges in tiles if any(a <= t < b for a, b in ranges)]
                    o = K.bank[:, OUT + t // 2, (t % 2) * 256:(t % 2) * 256 + MD + 1]
                    for j, s in enumerate(seen):
                        mm = pe.matmul(o, W[:, u % 2, s, t * P:t * P + P], f["mv"][:, s, h, :],
                                       start=(j == 0), stop=(j == len(seen) - 1))
                mm.then_inc(*made.up())

        @block.vector
        def _(dve):
            link = Link(dve, vector_step)

            def bound(u):
                h, d = u // 2, u % 2
                r = h + 32 * d
                dve.wait_ge(*raised.at(u + 1))
                if u >= 2:
                    dve.wait_ge(*made.at(u - 1))
                tiles = mlstm_key_tiles(d)
                for s, ranges in tiles:
                    for a, b in ranges:
                        ins = dve.tensor_scalar(W[:, u % 2, s, a * P:b * P], K.bank[:, PEAK, a * P:b * P],
                                                gcol[:, s, r:r + 1], 0.0, ALU.subtract, ALU.max)
                ins.then_inc(*bounded.up())

            def weigh(u):
                h, d = u // 2, u % 2
                dve.wait_ge(*exped.at(u + 1))
                dve.wait_ge(*qk_done.at(h + 1))
                tiles = mlstm_key_tiles(d)
                for s, ranges in tiles:
                    for a, b in ranges:
                        ins = dve.scalar_tensor_tensor(W[:, u % 2, s, a * P:b * P], K.bank[:, QK + s, a * P:b * P],
                                                       MD ** -0.5, W[:, u % 2, s, a * P:b * P], ALU.mult, ALU.mult)
                link(ins)
                tri = K.tri_b if d else K.tri_f
                for s in range(TT):
                    diag = W[:, u % 2, s, s * P:s * P + P]
                    ins = dve.tensor_tensor(diag, diag, tri[:], ALU.mult)
                ins.then_inc(*weighted.up())

            def divide(u):
                h, d = u // 2, u % 2
                r = h + 32 * d
                dve.wait_ge(*made.at(u + 1))
                dn = den[:, u % 2, :]
                total = K.bank[:, OUT:OUT + 2, :].rearrange("p b (u x) -> p b u x", x=256)[:, :, :, MD]
                floor = ecol[:, :, r].rearrange("p (b u) -> p b u", u=2)
                dn2 = dn.rearrange("p (b u) -> p b u", u=2)
                link(dve.scalar_tensor_tensor(dn2, total, -1.0, floor, ALU.mult, ALU.max))
                link(dve.tensor_tensor(dn2, total, dn2, ALU.max))
                link(dve.reciprocal(dn, dn))
                for t in range(TT):
                    o = K.bank[:, OUT + t // 2, (t % 2) * 256:(t % 2) * 256 + MD]
                    acc = hacc[:, t, h * MD:h * MD + MD]
                    if d == 0:
                        ins = dve.tensor_scalar(acc, o, dn[:, t:t + 1], None, ALU.mult)
                    else:
                        ins = dve.scalar_tensor_tensor(acc, o, dn[:, t:t + 1], acc, ALU.mult, ALU.add)
                ins.then_inc(*unit_done.up())
                dve.wait_ge(*unit_done.now())

            bound(0)
            for u in range(2 * MH):
                if u + 1 < 2 * MH:
                    bound(u + 1)
                weigh(u)
                if u:
                    divide(u - 1)
            divide(2 * MH - 1)

        @block.scalar
        def _(act):
            for u in range(2 * MH):
                d = u % 2
                act.wait_ge(*bounded.at(u + 1))
                tiles = mlstm_key_tiles(d)
                for s, ranges in tiles:
                    for a, b in ranges:
                        w = W[:, u % 2, s, a * P:b * P]
                        ins = act.activation(w, w, ACT.Exp, scale=-1.0)
                ins.then_inc(*exped.up())
    K.stage_end()

    gatedh, squared, rooted, scaled, turned, vector_step = K.counts(6)
    squares = W.rearrange("p u s t -> p (u s t)").rearrange("p (i v) -> p i v", v=MD)
    ss, rt = K.take(TT, MH), K.take(TT, MH)
    with nc.Block() as block:
        @block.vector
        def _(dve):
            link = Link(dve, vector_step)
            dve.tensor_tensor(hacc, hacc, f["mo"], ALU.mult).then_inc(*gatedh.up())
            dve.wait_ge(*rooted.at(1))
            link(dve.reciprocal(rt, rt))
            for c in range(TT):
                v = hacc[:, c, :].rearrange("p (h v) -> p h v", v=MD)
                dve.tensor_tensor(v, v, last(rt[:, c, :], MD), ALU.mult).then_inc(*scaled.up())
            for c in range(TT):
                dve.wait_ge(*turned.at(c + 1))
                for h in range(MH):
                    dve.tensor_scalar(f["mq"][:, h, c * P:c * P + P], K.bank[:, c, h * P:h * P + P],
                                      K.col("ml_norm", h), None, ALU.mult)

        @block.scalar
        def _(act):
            act.wait_ge(*gatedh.at(1))
            for c in range(TT):
                for h in range(MH):
                    ins = act.activation(squares[:, MH * c + h, :], hacc[:, c, h * MD:h * MD + MD], ACT.Square,
                                         accum_out=ss[:, c, h:h + 1])
            ins.then_inc(*squared.up())
            act.wait_ge(*squared.at(1))
            act.activation(rt, ss, ACT.Sqrt, bias=K.small[:, 0:1], scale=1.0 / MD).then_inc(*rooted.up())

        @block.tensor
        def _(pe):
            for c in range(TT):
                pe.wait_ge(*scaled.at(c + 1))
                for h in range(MH):
                    mm = pe.transpose(K.bank[:, c, h * P:h * P + P], hacc[:, c, h * MD:h * MD + MD], K.ident[:])
                mm.then_inc(*turned.up())
    K.stage_end()

def log1p_small(link, dve, e, t, w, w2):
    link(dve.tensor_scalar(t, e, 2.0, None, ALU.add))
    link(dve.reciprocal(t, t))
    link(dve.tensor_tensor(w, e, t, ALU.mult))
    link(dve.tensor_tensor(w2, w, w, ALU.mult))
    link(dve.tensor_scalar(t, w2, 1.0 / 17.0, None, ALU.mult))
    for n in (15, 13, 11, 9, 7, 5, 3):
        link(dve.scalar_tensor_tensor(t, t, 1.0 / n, w2, ALU.add, ALU.mult))
    link(dve.scalar_tensor_tensor(t, t, 1.0, w, ALU.add, ALU.mult))
    link(dve.tensor_scalar(e, t, 2.0, None, ALU.mult))


def odd_mixer(K):
    with K.scope():
        zs, xl, xc = K.take(KI, LAT), K.take(KI, LAT), K.take(KI, CTX)
        bt, ct, dt = K.take(SG, T), K.take(SG, LAT), K.take(T)[0:64, :]
        ssd_projection(K, zs, xl, xc, bt, ct, dt)
        cum, dcol = K.take(T)[0:64, :], K.take(8, 64)
        with K.scope():
            ssd_steps(K, dt, cum, dcol)
        xt, bs, state = K.take(TT, SI), K.take(LT, SG, SN), K.take(2, SI)
        ssd_turn(K, xc, xl, bt, xt, bs)
        wx = xc.rearrange("p a t -> p (a t)").rearrange("p (c x) -> p c x", c=2)
        ssd_context(K, wx, xt, bs, dcol, state)
        y = xt[:, 0:2, :]
        ssd_entering(K, y, ct, state, dcol, wx)
        cb = state.rearrange("p d x -> p (d x)")[:, 0:2 * SG * 3 * P]
        ssd_inside(K, y, xt, bt, ct, cb.rearrange("p (d g b t) -> p d g b t", d=2, g=SG, b=3), cum, dcol)
        ssd_combine(K, y, xl, zs, xc)
        split(K, [(xl[:, c, :], *K.h_parts(LAT, c)) for c in range(KI)])
    run_products(K, residual_items(K, "ssd_out", KI, lambda k: K.h_parts(LAT, k), CTX,
                                   lambda m, which: K.mod[:, 1, 16 + m, which:which + 1]))


def ssd_projection(K, zs, xl, xc, bt, ct, dt):
    first = FIRST_TILE["ssd_in"]
    rounds, tile = [], first
    for c in range(24):
        n = T if c < 20 else LAT

        def finish(act, acc, c=c):
            if c < 16:
                act.activation(xc[:, c, :], acc[:, 0:CTX], ACT.Silu)
                return act.activation(xl[:, c, :], acc[:, CTX:T], ACT.Silu)
            return act.activation(bt[:, c - 16, :] if c < 20 else ct[:, c - 20, :], acc, ACT.Silu)
        conv = Conv(n, K.col("ssd_conv_w", 24 + c), K.col("ssd_conv_b", c),
                    conv_taps_1d(lambda tap, c=c: K.col("ssd_conv_w", tap * 24 + c), n // 256), finish)
        rounds.append([Item(tile_products(tile, KD, lambda k, n=n: K.h_parts(T, k, T - n, T), n), None, "act", conv)])
        tile += KD
    for c in range(KI):
        rounds.append([Item(tile_products(tile, KD, lambda k: K.h_parts(T, k, CTX, T), LAT),
                            lambda act, bank, c=c: act.activation(zs[:, c, :], bank[:, 0:LAT], ACT.Silu))])
        tile += KD
    rounds.append([Item(tile_products(tile, KD, lambda k: K.h_parts(T, k), T),
                        lambda act, bank: act.activation(dt, bank[0:64, :], ACT.Identity,
                                                         bias=K.col("ssd_dt_b", rows=slice(0, 64)), scale=1.0))])
    run_products(K, rounds)


def ssd_steps(K, dt, cum, dcol):
    nc = K.nc
    flat = K.take(8, T)
    R = slice(0, 64)
    e, t, w, w2, la, wend, ecum = (flat[R, i, :] for i in range(7))
    acol = K.take(2)[R, :]
    step_a, step_v, exped, summed, decayed, ready, turned = K.counts(7)
    with nc.Block() as block:
        @block.scalar
        def _(act):
            link = Link(act, step_a)
            link(act.activation(acol[:, 0:1], K.col("ssd_a_log", rows=R), ACT.Exp))
            link(act.activation(e, dt, ACT.Abs))
            act.activation(e, e, ACT.Exp, scale=-1.0).then_inc(*exped.up())
            act.wait_ge(*summed.at(1))
            act.activation(ecum[:, 0:LAT], cum[:, CTX:T], ACT.Exp)
            act.activation(wend[:, 0:CTX], wend[:, 0:CTX], ACT.Exp, scale=-1.0).then_inc(*decayed.up())

        @block.vector
        def _(dve):
            link = Link(dve, step_v)
            dve.wait_ge(*exped.at(1))
            log1p_small(link, dve, e, t, w, w2)
            link(dve.scalar_tensor_tensor(dt, dt, 0.0, e, ALU.max, ALU.add))
            link(dve.tensor_scalar(la, dt, acol[:, 0:1], -1.0, ALU.mult, ALU.mult))
            one = w
            link(dve.memset(one, 1.0))
            for a, b in ((0, CTX), (CTX, T)):
                link(dve.tensor_tensor_scan(cum[0:32, a:b], one[0:32, a:b], la[0:32, a:b], 0.0, ALU.mult, ALU.add))
                link(dve.tensor_tensor_scan(cum[32:64, a:b][:, ::-1], one[32:64, a:b], la[32:64, a:b][:, ::-1], 0.0,
                                            ALU.mult, ALU.add))
            dve.tensor_scalar(wend[0:32, 0:CTX], cum[0:32, 0:CTX], cum[0:32, CTX - 1:CTX], None, ALU.subtract)
            dve.tensor_scalar(wend[32:64, 0:CTX], cum[32:64, 0:CTX], cum[32:64, 0:1], None,
                              ALU.subtract).then_inc(*summed.up())
            dve.wait_ge(*decayed.at(1))
            dve.tensor_tensor(wend[:, 0:CTX], wend[:, 0:CTX], dt[:, 0:CTX], ALU.mult).then_inc(*ready.up())
            dve.wait_ge(*turned.at(1))
            dve.tensor_copy(dcol.rearrange("p i h -> p (i h)"), K.bank[:, 0, :])

        @block.tensor
        def _(pe):
            pe.wait_ge(*ready.at(1))
            for i, src in enumerate((wend[:, 0:CTX], dt[:, CTX:T], cum[:, CTX:T], ecum[:, 0:LAT])):
                for c in range(LT):
                    mm = pe.transpose(K.bank[:, 0, (2 * i + c) * 64:(2 * i + c) * 64 + 64], src[:, c * P:c * P + P],
                                      K.ident[R, 0:64])
            mm.then_inc(*turned.up())
    K.stage_end()


WEND, DT, CUM, ECUM = 0, 2, 4, 6


def ssd_turn(K, xc, xl, bt, xt, bs):
    nc = K.nc
    turned, kept = K.counts(2)
    jobs = []
    for c in range(TT):
        for q in range(KI // 4):
            src = [(xc if c < LT else xl)[:, 4 * q + i, (c % LT) * P:(c % LT) * P + P] for i in range(4)]
            jobs.append((src, xt[:, c, q * 512:q * 512 + 512]))
    for c in range(LT):
        jobs.append(([bt[:, g, c * P:c * P + P] for g in range(SG)], bs[:, c, :, :].rearrange("p g n -> p (g n)")))
    with nc.Block() as block:
        @block.tensor
        def _(pe):
            for j, (src, _d) in enumerate(jobs):
                if j >= BANKS:
                    pe.wait_ge(*kept.at(j - BANKS + 1))
                for i, a in enumerate(src):
                    mm = pe.transpose(K.bank[:, j % BANKS, i * P:i * P + P], a, K.ident[:])
                mm.then_inc(*turned.up())

        @block.scalar
        def _(act):
            for j, (_s, dest) in enumerate(jobs):
                act.wait_ge(*turned.at(j + 1))
                act.activation(dest, K.bank[:, j % BANKS, :], ACT.Copy).then_inc(*kept.up())
    K.stage_end()


def ssd_context(K, wx, xt, bs, dcol, state):
    nc = K.nc
    weighted, summed = K.counts(2)
    with nc.Block() as block:
        @block.vector
        def _(dve):
            for d in range(2):
                if d:
                    dve.wait_ge(*summed.at(SG))
                for c in range(LT):
                    dve.tensor_tensor(wx[:, c, :].rearrange("p (h x) -> p h x", x=SP),
                                      xt[:, c, :].rearrange("p (h x) -> p h x", x=SP),
                                      last(dcol[:, WEND + c, 32 * d:32 * d + 32], SP), ALU.mult).then_inc(*weighted.up())

        @block.tensor
        def _(pe):
            for d in range(2):
                pe.wait_ge(*weighted.at(2 * d + 2))
                for g in range(SG):
                    for c in range(LT):
                        mm = pe.matmul(K.bank[:, SG * d + g, :], bs[:, c, g, :], wx[:, c, g * 512:g * 512 + 512],
                                       start=(c == 0), stop=(c == LT - 1))
                    mm.then_inc(*summed.up())

        @block.scalar
        def _(act):
            for i in range(2 * SG):
                act.wait_ge(*summed.at(i + 1))
                act.activation(state[:, i // SG, (i % SG) * 512:(i % SG) * 512 + 512], K.bank[:, i, :], ACT.Copy)
    K.stage_end()


def ssd_entering(K, y, ct, state, dcol, tmp):
    nc = K.nc
    made, taken, vector_step = K.counts(3)
    units = [(d, t, g) for d in range(2) for t in range(LT) for g in range(SG)]
    with nc.Block() as block:
        @block.tensor
        def _(pe):
            for u, (d, t, g) in enumerate(units):
                if u >= BANKS:
                    pe.wait_ge(*taken.at(u - BANKS + 1))
                pe.matmul(K.bank[:, u % BANKS, :], ct[:, g, t * P:t * P + P], state[:, d, g * 512:g * 512 + 512],
                          start=True, stop=True).then_inc(*made.up())

        @block.vector
        def _(dve):
            link = Link(dve, vector_step)
            for u, (d, t, g) in enumerate(units):
                dve.wait_ge(*made.at(u + 1))
                yv = y[:, t, g * 512:g * 512 + 512]
                o = tmp[:, 0, 0:512] if d else yv
                ins = dve.tensor_tensor(o.rearrange("p (h x) -> p h x", x=SP),
                                        K.bank[:, u % BANKS, :].rearrange("p (h x) -> p h x", x=SP),
                                        last(dcol[:, ECUM + t, 32 * d + 8 * g:32 * d + 8 * g + 8], SP), ALU.mult)
                ins.then_inc(*taken.up())
                if d:
                    dve.wait_ge(*taken.now())
                    link(dve.tensor_tensor(yv, yv, o, ALU.add))
    K.stage_end()


def ssd_inside(K, y, xt, bt, ct, cb, cum, dcol):
    nc = K.nc
    blocks = (((0, 0, True), (0, 1, False), (1, 1, True)), ((1, 0, False), (1, 1, True), (0, 0, True)))
    made, = K.counts(1)
    with nc.Block() as block:
        @block.tensor
        def _(pe):
            for g in range(SG):
                for s in range(LT):
                    mm = pe.matmul(K.bank[:, g, s * LAT:s * LAT + LAT], bt[:, g, CTX + s * P:CTX + s * P + P],
                                   ct[:, g, :], start=True, stop=True)
                mm.then_inc(*made.up())

        @block.vector
        def _(dve):
            for g in range(SG):
                dve.wait_ge(*made.at(g + 1))
                for d in range(2):
                    for b, (s, t, diag) in enumerate(blocks[d]):
                        src = K.bank[:, g, s * LAT + t * P:s * LAT + t * P + P]
                        if diag:
                            dve.tensor_tensor(cb[:, d, g, b, :], src, (K.tri_b if d else K.tri_f)[:], ALU.mult)
                        else:
                            dve.tensor_copy(cb[:, d, g, b, :], src)
    K.stage_end()

    NW, NX = 4, 4
    W = K.take(NW, 3, P)
    units = [(g, h, d) for g in range(SG) for h in range(8) for d in range(2)]
    raised, bounded, exped, weighted, used, finished, added = K.counts(7)
    with nc.Block() as block:
        @block.tensor
        def _(pe):
            def spread(u):
                g, h, d = units[u]
                if u >= NX:
                    pe.wait_ge(*bounded.at(u - NX + 1))
                r = 32 * d + 8 * g + h
                pe.matmul(K.bank[:, u % NX, 0:LAT], K.ident[0:64, r:r + 1].broadcast_to([64, P]), cum[:, CTX:T],
                          start=True, stop=True).then_inc(*raised.up())

            for u in range(NX - 1):
                spread(u)
            for u, (g, h, d) in enumerate(units):
                if u + NX - 1 < len(units):
                    spread(u + NX - 1)
                pe.wait_ge(*weighted.at(u + 1))
                if h == 0 and d == 0 and g >= 2:
                    pe.wait_ge(*added.at(g - 1))
                head = 8 * g + h
                for b, (s, t, diag) in enumerate(blocks[d]):
                    first = (d == 0 and b == 0) if t == 0 else (d == 0 and b == 1)
                    stop = (d == 1 and b == 2) if t == 0 else (d == 1 and b == 1)
                    mm = pe.matmul(K.bank[:, NX + 2 * (g % 2) + t, h * SP:h * SP + SP], W[:, u % NW, b, :],
                                   xt[:, LT + s, head * SP:head * SP + SP], start=first, stop=stop)
                mm.then_inc(*used.up())

        @block.vector
        def _(dve):
            def bound(u):
                g, h, d = units[u]
                r = 32 * d + 8 * g + h
                dve.wait_ge(*raised.at(u + 1))
                if u >= NW:
                    dve.wait_ge(*used.at(u - NW + 1))
                sa, sb = blocks[d][0][0], blocks[d][2][0]
                tb = blocks[d][2][1]
                w = W[:, u % NW, :, :].rearrange("p b t -> p (b t)")
                dve.tensor_scalar(w[:, 0:LAT], K.bank[:, u % NX, 0:LAT], dcol[:, CUM + sa, r:r + 1], 0.0,
                                  ALU.subtract, ALU.min)
                dve.tensor_scalar(w[:, LAT:LAT + P], K.bank[:, u % NX, tb * P:tb * P + P], dcol[:, CUM + sb, r:r + 1],
                                  0.0, ALU.subtract, ALU.min).then_inc(*bounded.up())

            def weigh(u):
                g, h, d = units[u]
                r = 32 * d + 8 * g + h
                sa, sb = blocks[d][0][0], blocks[d][2][0]
                w = W[:, u % NW, :, :].rearrange("p b t -> p (b t)")
                c = cb[:, d, g, :, :].rearrange("p b t -> p (b t)")
                dve.wait_ge(*exped.at(u + 1))
                dve.scalar_tensor_tensor(w[:, 0:LAT], w[:, 0:LAT], dcol[:, DT + sa, r:r + 1], c[:, 0:LAT],
                                         ALU.mult, ALU.mult)
                dve.scalar_tensor_tensor(w[:, LAT:LAT + P], w[:, LAT:LAT + P], dcol[:, DT + sb, r:r + 1],
                                         c[:, LAT:LAT + P], ALU.mult, ALU.mult).then_inc(*weighted.up())

            def add(g):
                dve.wait_ge(*used.at(16 * g + 16))
                for t in range(LT):
                    yv = y[:, t, g * 512:g * 512 + 512]
                    ins = dve.tensor_tensor(yv, yv, K.bank[:, NX + 2 * (g % 2) + t, :], ALU.add)
                ins.then_inc(*added.up())

            AHEAD = 2
            for u in range(AHEAD):
                bound(u)
            for u in range(len(units)):
                if u + AHEAD < len(units):
                    bound(u + AHEAD)
                weigh(u)
                if u % 16 == 4 and u > 16:
                    add(u // 16 - 1)
            add(SG - 1)

        @block.scalar
        def _(act):
            for u in range(len(units)):
                act.wait_ge(*bounded.at(u + 1))
                w = W[:, u % NW, :, :]
                act.activation(w, w, ACT.Exp).then_inc(*exped.up())
    K.stage_end()


def ssd_combine(K, y, xl, zs, sq):
    nc = K.nc
    turned, gated, squared, summed, rooted, vector_step, scalar_step = K.counts(7)
    rstd = K.take(SG, LAT)
    with nc.Block() as block:
        @block.tensor
        def _(pe):
            for c in range(KI):
                for t in range(LT):
                    mm = pe.transpose(K.bank[:, c // 2, (c % 2) * LAT + t * P:(c % 2) * LAT + t * P + P],
                                      y[:, t, c * P:c * P + P], K.ident[:])
                mm.then_inc(*turned.up())
            for g in range(SG):
                pe.wait_ge(*squared.at(4 * g + 4))
                for c in range(4):
                    mm = pe.matmul(K.bank[:, 2 * g, 0:LAT], K.ones[:], sq[:, 4 * g + c, :], start=(c == 0), stop=(c == 3))
                mm.then_inc(*summed.up())

        @block.vector
        def _(dve):
            link = Link(dve, vector_step)
            for c in range(KI):
                dve.wait_ge(*turned.at(c // 2 * 2 + 2))
                link(dve.scalar_tensor_tensor(xl[:, c, :], xl[:, c, :], K.col("ssd_d", c),
                                              K.bank[:, c // 2, (c % 2) * LAT:(c % 2) * LAT + LAT], ALU.mult, ALU.add))
                dve.tensor_tensor(xl[:, c, :], xl[:, c, :], zs[:, c, :], ALU.mult).then_inc(*gated.up())
            for g in range(SG):
                dve.wait_ge(*rooted.at(g + 1))
                link(dve.reciprocal(rstd[:, g, :], rstd[:, g, :]))
                for c in range(4 * g, 4 * g + 4):
                    dve.scalar_tensor_tensor(xl[:, c, :], xl[:, c, :], K.col("ssd_norm", c), rstd[:, g, :],
                                             ALU.mult, ALU.mult)

        @block.scalar
        def _(act):
            for c in range(KI):
                act.wait_ge(*gated.at(c + 1))
                act.activation(sq[:, c, :], xl[:, c, :], ACT.Square).then_inc(*squared.up())
            for g in range(SG):
                act.wait_ge(*summed.at(g + 1))
                act.activation(rstd[:, g, :], K.bank[:, 2 * g, 0:LAT], ACT.Sqrt, bias=K.small[:, 0:1],
                               scale=1.0 / 512).then_inc(*rooted.up())
    K.stage_end()


IN2 = [("qa", 4, "Copy"), ("ka", 4, "Copy"), ("qc", 4, "Copy"), ("kd", 4, "Copy"), ("xb", 4, "Copy"), ("kc", 1, "Copy"),
       ("vc", 1, "Copy"), ("ud", 4, "Gelu"), ("ga", 4, "Silu"), ("gb", 4, "Silu"), ("gc", 4, "Silu"), ("gd", 4, "Silu"),
       ("mg", 32, "Sigmoid")]


def hybrid_layer(K, out):
    normalise(K, CTX, "final_g", into_x=True)
    normalise(K, CTX, "norm2")
    with K.scope():
        f = {name: K.take(n, LAT) for name, n, _func in IN2}
        f["va"], f["vd"], f["vs"] = K.take(LT, BW), K.take(LT, BW), K.take(LT, 256)
        f["gate"], f["fa"] = K.take(LT, 24), K.take(LAT)
        project2(K, f)
        with K.scope():
            qk_norms(K, f)
        with K.scope():
            forget_sums(K, f)
        with K.scope():
            attentions(K, f)
        with K.scope():
            recurrence(K, f)
        with K.scope():
            spatial_gating(K, f)
        merge(K, f, out)


def attentions(K, f):
    addmask, sums = K.take(2 * P), K.take(LT, NH)
    attention_mask(K, addmask)

    def head_rows(h):
        return slice(HD * (h % 2), HD * (h % 2) + HD)

    with K.scope():
        o = K.take(LT, BW)
        attention(K, lambda h: f["qa"][head_rows(h), h // 2, :], lambda h: f["ka"][head_rows(h), h // 2, :],
                  lambda s, h: f["va"][:, s, h * HD:h * HD + HD], addmask, f["fa"], o, sums, None, False)
        turn_gate(K, o, f["ga"])
    o = f["va"]
    with K.scope():
        compressed_attention(K, f, o, sums)
    for branch, (kt, vt) in ((1, (0, 0)), (2, (2, 128))):
        with K.scope():
            attention(K, lambda h: f["qc"][head_rows(h), h // 2, :],
                      lambda h, kt=kt: f["kd"][head_rows(h), kt + h // 4, :],
                      lambda s, h, vt=vt: f["vs"][:, s, vt + (h // 4) * HD:vt + (h // 4) * HD + HD],
                      addmask, None, o, sums, lambda t, b=branch: f["gate"][:, t, NH * b:NH * b + NH], True)
    turn_gate(K, o, f["gc"])


def project2(K, f):
    first = FIRST_TILE["in2"]
    rounds, tile = [], first
    func_of = {"Copy": ACT.Copy, "Gelu": ACT.Gelu, "Silu": ACT.Silu, "Sigmoid": ACT.Sigmoid}

    def h(k):
        return K.h_parts(LAT, k)

    def token_round(name, width, func):
        groups = token_products(K, tile, LAT, range(LT), width)
        rounds.append([Item(g, lambda act, bank, i=i: act.activation(f[name][:, i, :], bank[:, 0:width], func))
                       for i, g in enumerate(groups)])

    for name, n, func in IN2:
        if name == "ud":
            token_round("va", BW, ACT.Copy)
            tile += 4 * KD
            token_round("vs", 256, ACT.Copy)
            tile += 2 * KD
            rounds.append([Item(tile_products(tile, KD, h, LAT),
                                lambda act, bank: act.activation(f["fa"][0:8, :], bank[0:8, 0:LAT], ACT.Identity,
                                                                 bias=K.col("b_forget", rows=slice(0, 8)), scale=1.0))])
            tile += KD
            token_round("vd", BW, ACT.Gelu)
            tile += 4 * KD
        for j in range(n):
            dest = f[name][:, j, :]
            rounds.append([Item(tile_products(tile, KD, h, LAT),
                                lambda act, bank, dest=dest, func=func: act.activation(dest, bank[:, 0:LAT], func_of[func]))])
            tile += KD
    token_round("gate", 24, ACT.Sigmoid)
    run_products(K, rounds)


def qk_norms(K, f):
    nc = K.nc
    squared, summed, rooted, vector_step = K.counts(4)
    sets = (("qa", "qn_a"), ("ka", "kn_a"), ("qc", "qn_c"), ("kd", "kn_c"))
    sq, rt = K.take(4, 4, LAT), K.take(4, 4, LAT)
    with nc.Block() as block:
        @block.scalar
        def _(act):
            for i, (name, _g) in enumerate(sets):
                act.activation(sq[:, i, :, :], f[name], ACT.Square).then_inc(*squared.up())
            for i in range(4):
                act.wait_ge(*summed.at(i + 1))
                act.activation(rt[:, i, :, :].rearrange("p (b a) t -> p b (a t)", a=2), K.bank[:, 2 * i:2 * i + 2, :],
                               ACT.Sqrt, bias=K.small[:, 0:1], scale=1.0 / HD).then_inc(*rooted.up())

        @block.tensor
        def _(pe):
            for i in range(4):
                pe.wait_ge(*squared.at(i + 1))
                for half in range(2):
                    mm = pe.matmul(K.bank[:, 2 * i + half, :], K.head_ones[:],
                                   sq[:, i, 2 * half:2 * half + 2, :].rearrange("p a t -> p (a t)"), start=True, stop=True)
                mm.then_inc(*summed.up())

        @block.vector
        def _(dve):
            link = Link(dve, vector_step)
            for i, (name, gain) in enumerate(sets):
                dve.wait_ge(*rooted.at(i + 1))
                link(dve.reciprocal(rt[:, i, :, :], rt[:, i, :, :]))
                dve.scalar_tensor_tensor(f[name], f[name], K.col(gain), rt[:, i, :, :], ALU.mult, ALU.mult)
    K.stage_end()


def forget_sums(K, f):
    nc = K.nc
    logged, vector_step, scalar_step = K.counts(3)
    e, one = K.take(LAT)[0:8, :], K.take(LAT)[0:8, :]
    z = f["fa"][0:8, :]
    with nc.Block() as block:
        @block.scalar
        def _(act):
            link = Link(act, scalar_step)
            link(act.activation(e, z, ACT.Abs))
            link(act.activation(e, e, ACT.Exp, scale=-1.0))
            act.activation(e, e, ACT.Ln, bias=K.small[0:8, 1:2], scale=1.0).then_inc(*logged.up())

        @block.vector
        def _(dve):
            link = Link(dve, vector_step)
            link(dve.memset(one, 1.0))
            dve.wait_ge(*logged.at(1))
            link(dve.scalar_tensor_tensor(e, z, 0.0, e, ALU.min, ALU.subtract))
            link(dve.tensor_tensor_scan(z, one, e, 0.0, ALU.mult, ALU.add))
            dve.tensor_scalar(z, z, -float(HD) ** 0.5, None, ALU.mult)
    K.stage_end()


NEG = 1e30


def attention_mask(K, addmask):
    with K.nc.Block() as block:
        @block.vector
        def _(dve):
            dve.memset(addmask[:, 0:P], 0.0)
            dve.tensor_scalar(addmask[:, P:2 * P], K.tri_b[:], 1.0, NEG, ALU.subtract, ALU.mult)


def attention(K, q, k, v, addmask, row_bias, o, sums, gate, add):
    nc = K.nc
    NS = 4
    s = K.take(NS, LAT)
    pt = K.take(NS, LT, P)
    top = K.take(NS, 2)
    tmp = K.take(BW)
    units = [(t, h) for t in range(LT) for h in range(NH)]
    scored, masked, negated, exped, turned, kept, used, finished, vector_step = K.counts(9)
    SCORE, TURN, OUT = 0, 2, 4
    with nc.Block() as block:
        @block.tensor
        def _(pe):
            def score(u):
                t, h = units[u]
                n = (t + 1) * P
                if u >= 2:
                    pe.wait_ge(*masked.at(u - 1))
                b = K.bank[:, SCORE + u % 2, 0:n]
                mm = pe.matmul(b, q(h)[:, t * P:t * P + P], k(h)[:, 0:n], start=True, stop=row_bias is None)
                if row_bias is not None:
                    mm = pe.matmul(b, K.ident[0:NH, h:h + 1].broadcast_to([NH, P]), row_bias[0:NH, 0:n],
                                   start=False, stop=True)
                mm.then_inc(*scored.up())

            def turn(u):
                t, h = units[u]
                pe.wait_ge(*exped.at(u + 1))
                if u >= 2:
                    pe.wait_ge(*kept.at(u - 1))
                for c in range(t + 1):
                    mm = pe.transpose(K.bank[:, TURN + u % 2, c * P:c * P + P], s[:, u % NS, c * P:c * P + P], K.ident[:])
                mm.then_inc(*turned.up())

            def weigh(u):
                t, h = units[u]
                pe.wait_ge(*kept.at(u + 1))
                for c in range(t + 1):
                    mm = pe.matmul(K.bank[:, OUT + t, h * HD:h * HD + HD], pt[:, u % NS, c, :], v(c, h),
                                   start=(c == 0), stop=(c == t))
                mm.then_inc(*used.up())

            n = len(units)
            for u in range(n + 3):
                if u < n:
                    score(u)
                if 1 <= u <= n:
                    turn(u - 1)
                if 2 <= u <= n + 1:
                    weigh(u - 2)

        @block.vector
        def _(dve):
            link = Link(dve, vector_step)
            for u, (t, h) in enumerate(units):
                n = (t + 1) * P
                w = s[:, u % NS, 0:n]
                dve.wait_ge(*scored.at(u + 1))
                if u >= NS:
                    dve.wait_ge(*turned.at(u - NS + 1))
                dve.scalar_tensor_tensor(w, K.bank[:, SCORE + u % 2, 0:n], HD ** -0.5, addmask[:, 2 * P - n:2 * P],
                                         ALU.mult, ALU.add).then_inc(*masked.up())
                dve.wait_ge(*masked.now())
                m = top[:, u % NS, :]
                link(dve.reduce_max(m[:, 0:1], w, AX.X))
                dve.tensor_scalar(m[:, 1:2], m[:, 0:1], -1.0, None, ALU.mult).then_inc(*negated.up())
            for t in range(LT):
                dve.wait_ge(*used.at(NH * t + NH))
                link(dve.reciprocal(sums[:, t, :], sums[:, t, :]))
                if gate is not None:
                    link(dve.tensor_tensor(sums[:, t, :], sums[:, t, :], gate(t), ALU.mult))
                dest = tmp if add else o[:, t, :]
                link(dve.tensor_tensor(dest.rearrange("p (h v) -> p h v", v=HD),
                                       K.bank[:, OUT + t, :].rearrange("p (h v) -> p h v", v=HD),
                                       last(sums[:, t, :], HD), ALU.mult))
                if add:
                    link(dve.tensor_tensor(o[:, t, :], o[:, t, :], tmp, ALU.add))

        @block.scalar
        def _(act):
            n = len(units)

            def keep(u):
                t, h = units[u]
                act.wait_ge(*turned.at(u + 1))
                if u >= NS:
                    act.wait_ge(*used.at(u - NS + 1))
                act.activation(pt[:, u % NS, 0:t + 1, :].rearrange("p c t -> p (c t)"),
                               K.bank[:, TURN + u % 2, 0:(t + 1) * P], ACT.Copy).then_inc(*kept.up())
            for u, (t, h) in enumerate(units):
                act.wait_ge(*negated.at(u + 1))
                w = s[:, u % NS, 0:(t + 1) * P]
                act.activation(w, w, ACT.Exp, bias=top[:, u % NS, 1:2], scale=1.0,
                               accum_out=sums[:, t, h:h + 1]).then_inc(*exped.up())
                if u:
                    keep(u - 1)
            keep(n - 1)
    K.stage_end()


def turn_gate(K, o, gate):
    nc = K.nc
    (turned,) = K.counts(1)
    with nc.Block() as block:
        @block.tensor
        def _(pe):
            for j in range(KB):
                for t in range(LT):
                    mm = pe.transpose(K.bank[:, j, t * P:t * P + P], o[:, t, j * P:j * P + P], K.ident[:])
                mm.then_inc(*turned.up())

        @block.vector
        def _(dve):
            for j in range(KB):
                dve.wait_ge(*turned.at(j + 1))
                dve.tensor_tensor(gate[:, j, :], gate[:, j, :], K.bank[:, j, 0:LAT], ALU.mult)
    K.stage_end()


def compressed_attention(K, f, o, sums):
    nc = K.nc
    S = 32
    w1 = (K.take(CB, P), K.take(CB, P))
    w2 = K.take(2, P)
    tb = K.take(2, CB, NC)
    hid = K.take(4, NC)
    kn, rt, sq = K.take(2, NC), K.take(2, NC), K.take(2, NC)
    vblk = K.take(2, 4, HD)
    mask, neg = K.take(LT, NC), K.take(LT, NC)
    prob = K.take(LT, NH, S)
    peak = K.take(LT, NH)
    turned_p = K.take(LT, 2, P)
    loads, cleared, masks, posed, hidden, silued, keyed, squared, summed, rooted, normed, valued = K.counts(12)
    pool_step, vector_step = K.counts(2)
    with nc.Block() as block:
        @block.sync
        def _(sync):
            for i in range(2):
                sync.dma_start(w1[i], K.dram["cmp_w1"][:, i, :, :]).then_inc(*loads.up(16))
            sync.dma_start(w2, K.dram["cmp_w2"]).then_inc(*loads.up(16))

        @block.gpsimd
        def _(pool):
            link = Link(pool, pool_step)
            pool.memset(vblk, 0.0).then_inc(*cleared.up())
            pool.memset(prob, 0.0).then_inc(*cleared.up())
            link(pool.memset(mask, 1.0))
            for t in range(LT):
                pool.affine_select(out=mask[:, t, :], in_=mask[:, t, :], compare_op=ALU.is_ge, fill=0.0,
                                   base=t * P - (CB - 1), pattern=[[-CS, NC]], channel_multiplier=1).then_inc(*masks.up())

        @block.vector
        def _(dve):
            link = Link(dve, vector_step)
            for i, name in enumerate(("kc", "vc")):
                src = f[name][:, 0, :].rearrange("p (c b) -> p b c", b=CS)
                for a in range(CB // CS):
                    dve.tensor_tensor(tb[:, i, a * CS:a * CS + CS, :], src[:, :, a:a + NC],
                                      last(K.col("cmp_pos", a * CS, CS), NC), ALU.add).then_inc(*posed.up())
            dve.wait_ge(*masks.at(2))
            dve.tensor_scalar(neg, mask, 1.0, NEG, ALU.subtract, ALU.mult)
            dve.wait_ge(*rooted.at(1))
            link(dve.reciprocal(rt, rt))
            dve.scalar_tensor_tensor(kn, K.bank[:, 1, 0:2 * NC].rearrange("p (g c) -> p g c", c=NC), K.col("kn_c"), rt,
                                     ALU.mult, ALU.mult).then_inc(*normed.up())
            dve.wait_ge(*valued.at(1))
            dve.wait_ge(*cleared.at(2))
            for g in range(2):
                for j in range(4):
                    r = slice(S * j, S * j + NC)
                    dve.tensor_copy(vblk[r, g, j, :], K.bank[r, 3, g * HD:g * HD + HD])

        @block.tensor
        def _(pe):
            pe.wait_ge(*loads.at(48))
            pe.wait_ge(*posed.at(4))
            for i in range(2):
                for g in range(2):
                    r = slice(HD * g, HD * g + HD)
                    for c in range(CB):
                        mm = pe.matmul(K.bank[:, 4 * g, i * NC:i * NC + NC], w1[i][r, c, :],
                                       tb[r, i, c, :], start=(c == 0), stop=(c == CB - 1))
            mm.then_inc(*hidden.up())
            pe.wait_ge(*silued.at(1))
            for g in range(2):
                mm = pe.matmul(K.bank[:, 1, g * NC:g * NC + NC], w2[:, 0, :], hid[:, g, :], start=True, stop=True)
            mm.then_inc(*keyed.up())
            for g in range(2):
                for j in range(4):
                    mm = pe.matmul(K.bank[S * j:S * j + NC, 3, g * HD:g * HD + HD], hid[:, 2 + g, :], w2[:, 1, 0:HD],
                                   start=True, stop=True)
            mm.then_inc(*valued.up())
            pe.wait_ge(*squared.at(1))
            pe.matmul(K.bank[:, 2, 0:2 * NC], K.head_ones[:], sq.rearrange("p g c -> p (g c)"), start=True,
                      stop=True).then_inc(*summed.up())

        @block.scalar
        def _(act):
            act.wait_ge(*hidden.at(1))
            for g in range(2):
                ins = act.activation(hid[:, g:g + 3:2, :], K.bank[:, 4 * g, 0:2 * NC].rearrange("p (i c) -> p i c", c=NC),
                                     ACT.Silu)
            ins.then_inc(*silued.up())
            act.wait_ge(*keyed.at(1))
            act.activation(sq.rearrange("p g c -> p (g c)"), K.bank[:, 1, 0:2 * NC], ACT.Square).then_inc(*squared.up())
            act.wait_ge(*summed.at(1))
            act.activation(rt.rearrange("p g c -> p (g c)"), K.bank[:, 2, 0:2 * NC], ACT.Sqrt, bias=K.small[:, 0:1],
                           scale=1.0 / HD).then_inc(*rooted.up())
    K.stage_end()

    scored, shifted, exped, ready, turned, kept, made, vector_step = K.counts(8)
    live = prob[:, :, :, 0:NC]
    with nc.Block() as block:
        @block.tensor
        def _(pe):
            for t in range(LT):
                for h in range(NH):
                    r = slice(HD * (h % 2), HD * (h % 2) + HD)
                    mm = pe.matmul(K.bank[:, 2 * t + h % 2, (h // 2) * S:(h // 2) * S + NC], f["qc"][r, h // 2, t * P:t * P + P], kn[r, h // 4, :],
                                   start=True, stop=True)
                mm.then_inc(*scored.up())
            for t in range(LT):
                pe.wait_ge(*ready.at(t + 1))
                for g in range(2):
                    mm = pe.transpose(K.bank[:, 4 + t, g * P:g * P + P],
                                      prob[:, t, 4 * g:4 * g + 4, :].rearrange("p h s -> p (h s)"), K.ident[:])
                mm.then_inc(*turned.up())
            for t in range(LT):
                pe.wait_ge(*kept.at(t + 1))
                for g in range(2):
                    mm = pe.matmul(K.bank[:, 6 + t, g * 256:g * 256 + 256], turned_p[:, t, g, :],
                                   vblk[:, g, :, :].rearrange("p j v -> p (j v)"), start=True, stop=True)
                mm.then_inc(*made.up())

        @block.vector
        def _(dve):
            link = Link(dve, vector_step)
            for t in range(LT):
                dve.wait_ge(*scored.at(t + 1))
                for e in range(2):
                    sv = K.bank[:, 2 * t + e, 0:4 * S].rearrange("p (h s) -> p h s", s=S)[:, :, 0:NC]
                    link(dve.scalar_tensor_tensor(live[:, t, e:NH:2, :], sv, HD ** -0.5, mid(neg[:, t, :], 4), ALU.mult,
                                                  ALU.add))
                link(dve.tensor_reduce(peak[:, t, :], live[:, t, :, :], AX.X, ALU.max))
                dve.tensor_tensor(live[:, t, :, :], live[:, t, :, :], last(peak[:, t, :], NC),
                                  ALU.subtract).then_inc(*shifted.up())
            for t in range(LT):
                dve.wait_ge(*exped.at(t + 1))
                link(dve.tensor_reduce(sums[:, t, :], live[:, t, :, :], AX.X, ALU.add))
                dve.tensor_tensor(live[:, t, :, :], live[:, t, :, :], mid(mask[:, t, :], NH), ALU.mult).then_inc(*ready.up())
            for t in range(LT):
                dve.wait_ge(*made.at(t + 1))
                link(dve.reciprocal(sums[:, t, :], sums[:, t, :]))
                link(dve.tensor_tensor(sums[:, t, :], sums[:, t, :], f["gate"][:, t, 0:NH], ALU.mult))
                dve.tensor_tensor(o[:, t, :].rearrange("p (h v) -> p h v", v=HD),
                                  K.bank[:, 6 + t, :].rearrange("p (h v) -> p h v", v=HD),
                                  last(sums[:, t, :], HD), ALU.mult)

        @block.scalar
        def _(act):
            for t in range(LT):
                act.wait_ge(*shifted.at(t + 1))
                act.activation(live[:, t, :, :], live[:, t, :, :], ACT.Exp).then_inc(*exped.up())
            for t in range(LT):
                act.wait_ge(*turned.at(t + 1))
                act.activation(turned_p[:, t, :, :].rearrange("p g t -> p (g t)"), K.bank[:, 4 + t, 0:2 * P],
                               ACT.Copy).then_inc(*kept.up())
    K.stage_end()


def recurrence(K, f):
    nc = K.nc
    W = 4
    xc, r, ig, a, m = (K.take(KB, LAT) for _ in range(5))
    wg = K.take(2, KB, P)
    sp = K.take(5, KB)
    loads, centred, conved, gated, sigmoided, absed, logged, decays, exped, tanhed, scaled, rooted = K.counts(12)
    vector_step, scalar_step = K.counts(2)
    with nc.Block() as block:
        @block.sync
        def _(sync):
            sync.dma_start(wg, K.dram["rg_w"]).then_inc(*loads.up(16))

        @block.scalar
        def _(act):
            link = Link(act, scalar_step)
            for j in range(KB):
                ins = act.activation(xc[:, j, :], f["xb"][:, j, :], ACT.Identity, bias=K.col("lru_conv_b", j),
                                     scale=K.col("lru_conv_w", 3 * KB + j))
            ins.then_inc(*centred.up())
            link(act.activation(sp[:, 0, :], K.col("lam", 0, KB), ACT.Abs))
            act.activation(sp[:, 0, :], sp[:, 0, :], ACT.Exp, scale=-1.0).then_inc(*absed.up())
            act.wait_ge(*gated.at(1))
            for j in range(KB):
                act.activation(r[:, j, :], K.bank[:, j, 0:LAT], ACT.Sigmoid, bias=K.col("b_rg_a", j), scale=1.0)
                ins = act.activation(ig[:, j, :], K.bank[:, j, LAT:2 * LAT], ACT.Sigmoid, bias=K.col("b_rg_x", j), scale=1.0)
            ins.then_inc(*sigmoided.up())
            act.wait_ge(*decays.at(1))
            act.activation(a, r, ACT.Exp, scale=-1.0).then_inc(*exped.up())
            act.activation(m, r, ACT.Tanh).then_inc(*tanhed.up())
            act.wait_ge(*scaled.at(1))
            act.activation(m, m, ACT.Sqrt).then_inc(*rooted.up())

        @block.vector
        def _(dve):
            link = Link(dve, vector_step)
            dve.wait_ge(*centred.at(1))
            for j in range(KB):
                for tap in range(W - 1):
                    s = W - 1 - tap
                    ins = dve.scalar_tensor_tensor(xc[:, j, s:LAT], f["xb"][:, j, 0:LAT - s],
                                                   K.col("lru_conv_w", tap * KB + j), xc[:, j, s:LAT], ALU.mult, ALU.add)
                    if j == KB - 1 and tap == W - 2:
                        ins.then_inc(*conved.up())
                    else:
                        link(ins)
            dve.wait_ge(*absed.at(1))
            log1p_small(link, dve, sp[:, 0, :], sp[:, 1, :], sp[:, 2, :], sp[:, 3, :])
            link(dve.tensor_scalar(sp[:, 4, :], K.col("lam", 0, KB), -1.0, 0.0, ALU.mult, ALU.max))
            link(dve.tensor_tensor(sp[:, 0, :], sp[:, 0, :], sp[:, 4, :], ALU.add))
            dve.wait_ge(*sigmoided.at(1))
            for j in range(KB):
                ins = dve.tensor_scalar(r[:, j, :], r[:, j, :], sp[:, 0, j:j + 1], 8.0, ALU.mult, ALU.mult)
            ins.then_inc(*decays.up())
            link(dve.tensor_tensor(ig, ig, xc, ALU.mult))
            dve.wait_ge(*tanhed.at(1))
            link(dve.tensor_tensor(xc, a, a, ALU.mult))
            dve.scalar_tensor_tensor(m, xc, 1.0, m, ALU.add, ALU.mult).then_inc(*scaled.up())
            dve.wait_ge(*rooted.at(1))
            link(dve.tensor_tensor(m, m, ig, ALU.mult))
            for j in range(KB):
                link(dve.tensor_tensor_scan(xc[:, j, :], a[:, j, :], m[:, j, :], 0.0, ALU.mult, ALU.add))
            dve.tensor_tensor(f["gb"], f["gb"], xc, ALU.mult)

        @block.tensor
        def _(pe):
            pe.wait_ge(*loads.at(16))
            pe.wait_ge(*conved.at(1))
            for j in range(KB):
                for gate in range(2):
                    mm = pe.matmul(K.bank[:, j, gate * LAT:gate * LAT + LAT], wg[:, gate, j, :], xc[:, j, :],
                                   start=True, stop=True)
            mm.then_inc(*gated.up())
    K.stage_end()


def spatial_gating(K, f):
    nc = K.nc
    ws, bs, ln = K.take(8, P), K.take(P), K.take(BW)
    mean, var = K.take(LT), K.take(LT)
    squares = K.take(LT, BW)
    loads, masked, centred, squared, rooted, normed, mixed, vector_step = K.counts(8)
    with nc.Block() as block:
        @block.sync
        def _(sync):
            sync.dma_start(ws, K.dram["spatial_w"]).then_inc(*loads.up(16))
            sync.dma_start(bs[0:8, :], K.dram["spatial_b"]).then_inc(*loads.up(16))
            sync.dma_start(ln, K.dram["ln_v_g"].partition_broadcast(P)).then_inc(*loads.up(16))

        @block.vector
        def _(dve):
            link = Link(dve, vector_step)
            for t in range(LT):
                link(dve.reduce_sum(mean[:, t:t + 1], f["vd"][:, t, :], AX.X))
                link(dve.tensor_scalar(mean[:, t:t + 1], mean[:, t:t + 1], 1.0 / BW, None, ALU.mult))
                dve.tensor_scalar(f["vd"][:, t, :], f["vd"][:, t, :], mean[:, t:t + 1], None,
                                  ALU.subtract).then_inc(*centred.up())
            dve.wait_ge(*loads.at(48))
            link(dve.tensor_tensor(ws, ws, mid(K.tri_f[:], 8), ALU.mult))
            dve.wait_ge(*rooted.at(1))
            link(dve.reciprocal(var, var))
            for t in range(LT):
                dve.scalar_tensor_tensor(f["vd"][:, t, :], f["vd"][:, t, :], var[:, t:t + 1], ln, ALU.mult,
                                         ALU.mult).then_inc(*normed.up())
            for j in range(KB):
                dve.wait_ge(*mixed.at(j + 1))
                link(dve.tensor_tensor(f["ud"][:, j, :], f["ud"][:, j, :], K.bank[:, j, 0:LAT], ALU.mult))
                dve.tensor_tensor(f["gd"][:, j, :], f["gd"][:, j, :], f["ud"][:, j, :], ALU.mult)

        @block.scalar
        def _(act):
            for t in range(LT):
                act.wait_ge(*centred.at(t + 1))
                ins = act.activation(squares[:, t, :], f["vd"][:, t, :], ACT.Square, accum_out=var[:, t:t + 1])
            ins.then_inc(*squared.up())
            act.wait_ge(*squared.at(1))
            act.activation(var, var, ACT.Sqrt, bias=K.small[:, 0:1], scale=1.0 / BW).then_inc(*rooted.up())

        @block.tensor
        def _(pe):
            pe.wait_ge(*normed.at(LT))
            for j in range(KB):
                for c in range(LT):
                    for e in range(2):
                        g = 2 * j + e
                        b = K.bank[HD * e:HD * e + HD, j, c * P:c * P + P]
                        pe.matmul(b, f["vd"][:, c, g * HD:g * HD + HD], ws[:, g, :], start=True, stop=False)
                        mm = pe.matmul(b, K.ident[0:8, g:g + 1].broadcast_to([8, HD]), bs[0:8, :], start=False, stop=True)
                mm.then_inc(*mixed.up())
    K.stage_end()


def merge(K, f, out):
    nc = K.nc
    branches = ("ga", "gb", "gc", "gd")
    split(K, [(f[name][:, j, :], *K.h_parts(LAT, 4 * b + j)) for b, name in enumerate(branches) for j in range(KB)])
    with K.scope():
        tmp, total = K.take(LAT), K.take(LAT)
        merged_hi, merged_lo = K.take(KD, LAT, dtype=F32R), K.take(KD, LAT, dtype=F32R)
        first = FIRST_TILE["branch2"]
        rounds = []
        for n in range(KD):
            for b in range(4):
                def empty(dve, link, bank, n=n, b=b):
                    if b == 0:
                        return dve.tensor_tensor(total, bank[:, 0:LAT], f["mg"][:, b * KD + n, :], ALU.mult)
                    link(dve.tensor_tensor(tmp, bank[:, 0:LAT], f["mg"][:, b * KD + n, :], ALU.mult))
                    ins = dve.tensor_tensor(total, total, tmp, ALU.add)
                    if b == 3:
                        link(ins)
                        link(dve.tensor_copy(merged_hi[:, n, :], total))
                        ins = dve.tensor_tensor(merged_lo[:, n, :], total, merged_hi[:, n, :].bitcast(F32), ALU.subtract)
                    return ins
                rounds.append([Item(tile_products(first + (n * 4 + b) * KB, KB,
                                                  lambda k, b=b: K.h_parts(LAT, 4 * b + k), LAT), empty, "dve")])
        run_products(K, rounds)
        run_products(K, residual_items(K, "out2", KD, lambda k: (merged_hi[:, k, :], merged_lo[:, k, :]), CTX, None))
    (stored,) = K.counts(1)
    with nc.Block() as block:
        @block.sync
        def _(sync):
            sync.dma_start(out, K.x[:, :, CTX:T]).then_inc(*stored.up(16))
            sync.wait_ge(*stored.at(16))
    K.stage_end()


def build(nc, dram, out):
    with ExitStack() as ctx:
        K = Kit(nc, ctx, dram)
        with K.scope():
            features = even_features(K)
            a2 = K.take(256)
            with K.scope():
                cond = K.take(2, D)
                modulator = Modulator(K, cond)
                setup(K, cond, modulator)
                normalise(K, 0, "mix_g0", (0, 0, 8))
                even_projection(K, features[0], a2, modulator)
            gla_decays(K, features[0], a2, features[1])
            even_mixer(K, features)
        feed_forward(K, 0, 0, blocks_of("mod1")[MOD_EVEN:])
        normalise(K, 0, "mix_g1", (1, 0, 8))
        odd_mixer(K)
        feed_forward(K, 1, CTX)
        hybrid_layer(K, out)


def feature_columns(a):
    return a.reshape(-1, P).T


def feature_tiles(w):
    k, n = w.shape
    return w.reshape(k // P, P, n // P, P).transpose(2, 0, 1, 3).reshape(-1, P, P)


def token_tiles(w):
    k, n = w.shape
    return w.reshape(k // P, P, n // P, P).transpose(0, 2, 1, 3).reshape(-1, P, P)


def widened(w):
    return np.concatenate([w, np.zeros((w.shape[0], P - w.shape[1]), w.dtype)], axis=1)


def rows_to_partitions(w):
    return w.reshape(-1, P, w.shape[1]).transpose(1, 0, 2)


def lay_out(v):
    f32 = np.float32
    parts = {}
    for l in range(2):
        parts[f"mod{l}"] = [v["mod_w"][l].reshape(KD, P, 48, P).transpose(2, 0, 3, 1).reshape(-1, P, P)]
        up = v["ffn_w_up"][l]
        pair = np.concatenate([up[:, :FF].reshape(D, KF, 1, P), up[:, FF:].reshape(D, KF, 1, P)], axis=2)
        parts[f"up{l}"] = [feature_tiles(pair.reshape(D, 2 * FF))]
        parts[f"down{l}"] = [feature_tiles(v["ffn_w_down"][l])]
    w = v["even_w_in"][0]
    gq, gk, gv, gg, mq, mk, mv, mo, mg = np.split(w, np.cumsum([256, 256, 512, 512, 512, 512, 512, 512]), axis=1)
    small = np.zeros((D, 3, P), f32)
    small[:, 0, 0:16], small[:, 0, 32:48] = v["gla_a1"][0, 0], v["gla_a1"][0, 1]
    small[:, 1, 0:4], small[:, 1, 32:36] = mg[:, 0:4], mg[:, 8:12]
    small[:, 2, 0:4], small[:, 2, 32:36] = mg[:, 4:8], mg[:, 12:16]
    parts["even_in"] = [feature_tiles(x) for x in (gq, gk, gg, mq, mk)] + [token_tiles(x) for x in (gv, mv, mo)] + \
                       [feature_tiles(small.reshape(D, 3 * P))]
    parts["even_out"] = [feature_tiles(v["even_w_out"][0])]
    a2 = np.zeros((48, 256), f32)
    a2[0:16], a2[32:48] = v["gla_a2"][0, 0], v["gla_a2"][0, 1]

    w = v["ssd_w_in"][0]
    parts["ssd_in"] = [feature_tiles(w[:, SI:SI + 3072]), feature_tiles(w[:, 0:SI]), feature_tiles(widened(w[:, SI + 3072:]))]
    parts["ssd_out"] = [feature_tiles(v["ssd_w_out"][0])]

    w = v["w_in_2"][0]
    names = ["qa", "ka", "va", "fa", "ga", "xb", "gb", "qc", "kc", "vc", "ks", "vs", "kw", "vw", "gate", "gc", "ud", "vd",
             "gd", "mg"]
    sizes = [BW, BW, BW, NH, BW, BW, BW, BW] + [128] * 6 + [24] + [BW] * 4 + [4096]
    z = dict(zip(names, np.split(w, np.cumsum(sizes)[:-1], axis=1)))
    z["kd"] = np.concatenate([z[n][:, g * HD:g * HD + HD] for n in ("ks", "kw") for g in (0, 0, 1, 1)], axis=1)
    parts["in2"] = []
    for name, n, _func in IN2:
        if name == "ud":
            parts["in2"] += [token_tiles(z["va"]), token_tiles(np.concatenate([z["vs"], z["vw"]], axis=1)),
                             feature_tiles(widened(z["fa"])), token_tiles(z["vd"])]
        parts["in2"].append(feature_tiles(z[name]))
    parts["in2"].append(token_tiles(widened(z["gate"])))
    wb = v["w_branch_2"][0].reshape(4, KB, P, KD, P).transpose(3, 0, 1, 2, 4)
    parts["branch2"] = [wb.reshape(-1, P, P)]
    parts["out2"] = [feature_tiles(v["w_out_2"][0])]
    tiles = np.concatenate([t for name, _n in SEGMENTS for t in parts[name]], axis=0)
    weights = tiles.reshape(N_BLOCKS, TPB, P, P)[STREAM].transpose(0, 2, 1, 3).reshape(N_BLOCKS, P, TPB * P)

    cols = np.zeros((P, N_COLS), f32)

    def put(name, a):
        a = np.asarray(a)
        cols[0:a.shape[0], COL[name]:COL[name] + a.shape[1]] = a

    def taps(w):
        return np.concatenate([feature_columns(t) for t in w], axis=1)

    for l in range(2):
        put(f"mod_b{l}", feature_columns(v["mod_b"][l]))
        put(f"mix_g{l}", feature_columns(v["norm_mix_g"][l]))
        put(f"ffn_g{l}", feature_columns(v["norm_ffn_g"][l]))
        put(f"conv_w{l}", taps(v["ffn_conv_w"][l].reshape(9, 2 * FF)))
        put(f"conv_b{l}", feature_columns(v["ffn_conv_b"][l]))
    put("final_g", feature_columns(v["final_norm_g"]))
    put("gla_ab", feature_columns(v["gla_ab"][0].reshape(-1)))
    put("ml_conv_w", taps(v["ml_conv_w"][0]))
    put("ml_conv_b", feature_columns(v["ml_conv_b"][0]))
    put("gla_norm", feature_columns(v["gla_norm_g"][0]))
    put("ml_norm", feature_columns(v["ml_norm_g"][0]))
    gb = v["ml_gate_b"][0]
    for name, a in (("ml_li_b", 0), ("ml_lf_b", 4)):
        cols[0:4, COL[name]], cols[32:36, COL[name]] = gb[a:a + 4], gb[8 + a:12 + a]
    put("ssd_conv_w", taps(v["ssd_conv_w"][0]))
    put("ssd_conv_b", feature_columns(v["ssd_conv_b"][0]))
    put("ssd_d", feature_columns(np.repeat(v["ssd_d"][0], SP)))
    put("ssd_norm", feature_columns(v["ssd_norm_g"][0]))
    put("ssd_dt_b", v["ssd_dt_bias"][0].reshape(64, 1))
    put("ssd_a_log", v["ssd_a_log"][0].reshape(64, 1))
    put("norm2", feature_columns(v["norm_g_2"][0]))
    for name in ("qn_a", "kn_a", "qn_c", "kn_c"):
        put(name, np.tile(v[name + "_2"][0], 2).reshape(P, 1))
    put("b_forget", v["b_forget_2"][0].reshape(NH, 1))
    put("lru_conv_w", taps(v["conv_w_2"][0]))
    put("lru_conv_b", feature_columns(v["conv_b_2"][0]))
    put("b_rg_a", feature_columns(v["b_rg_a_2"][0]))
    put("b_rg_x", feature_columns(v["b_rg_x_2"][0]))
    put("lam", feature_columns(v["lru_lambda_2"][0]))
    put("cmp_pos", np.tile(v["cmp_pos_2"][0].T, (2, 1)))

    tokens = np.concatenate([v["ctx"][0], v["x"][0]], axis=0)
    w1 = np.stack([v["cmp_k_w1_2"][0], v["cmp_v_w1_2"][0]]).reshape(2, CB, HD, P).transpose(2, 0, 1, 3)
    w2 = np.stack([np.tile(v[n][0], (1, 2)) for n in ("cmp_k_w2_2", "cmp_v_w2_2")], axis=1)
    rg = np.zeros((2, HD, 2, KB, 2, HD), f32)
    for gate, name in enumerate(("w_rg_a_2", "w_rg_x_2")):
        for e in range(2):
            rg[e, :, gate, :, e, :] = v[name][0][e::2].transpose(1, 0, 2)
    return {
        "weights": weights,
        "columns": cols,
        "tokens": rows_to_partitions(tokens.T),
        "cond": np.stack([v["c"][0], v["c_ctx"]]),
        "gla_a2": a2,
        "cmp_w1": np.concatenate([w1, w1], axis=0),
        "cmp_w2": w2,
        "rg_w": rg.reshape(P, 2, KB, P),
        "spatial_w": v["w_spatial_2"][0].transpose(2, 0, 1),
        "spatial_b": v["b_spatial_2"][0],
        "ln_v_g": v["ln_v_g_2"][0],
    }


def kernel(**inputs):
    import concourse.bacc as bacc
    from concourse.bass_utils import run_bass_kernel_spmd

    laid = {name: np.ascontiguousarray(a) for name, a in lay_out({k: np.asarray(a) for k, a in inputs.items()}).items()}
    nc = bacc.Bacc("TRN2", target_bir_lowering=False, num_devices=1)
    dram = {name: nc.dram_tensor("in_" + name, a.shape, F32, kind="ExternalInput").ap() for name, a in laid.items()}
    out = nc.dram_tensor("out", (P, KD, LAT), F32, kind="ExternalOutput").ap()
    build(nc, dram, out)
    r = run_bass_kernel_spmd(nc, [{"in_" + name: a for name, a in laid.items()}], core_ids=[0])
    y = r.results[0]["out"]
    return y.transpose(2, 1, 0).reshape(1, LAT, D)
```

```python
from contextlib import ExitStack, contextmanager

import numpy as np

import concourse.bass as bass
from concourse import mybir

F32 = mybir.dt.float32
F32R = mybir.dt.float32r
BF16 = mybir.dt.bfloat16
I32 = mybir.dt.int32
ALU = mybir.AluOpType
ACT = mybir.ActivationFunctionType
AX = mybir.AxisListType

P = 128
D = 1024
KD = D // P
CTX, LAT = 256, 256
T = CTX + LAT
TT = T // P
LT = LAT // P
GRID_W = 64
ROWS = LAT // GRID_W
EPS = 1e-6
FF = 2816
KF = FF // P
GH, GK, GV = 4, 64, 128
GW = GH * GV
GLEVELS = 7
GTAU = 16.0
MH, MD = 4, 128
SH, SP, SN, SG = 32, 64, 128, 4
SI = SH * SP
KI = SI // P
HD = 64
NH = 8
BW = 512
KB = BW // P
CB, CS = 32, 16
NC = (LAT - CB) // CS + 1
BANKS = 8
TPB = 8
RING = 5
PARTS = 3
AHEAD = 2

SEGMENTS = [
    ("mod0", 48 * KD), ("mod1", 48 * KD), ("even_in", 31 * KD), ("even_out", 8 * 8), ("up0", 2 * KF * KD),
    ("down0", 8 * KF), ("ssd_in", 41 * KD), ("ssd_out", 8 * KI), ("up1", 2 * KF * KD), ("down1", 8 * KF),
    ("in2", 86 * KD), ("branch2", 8 * 4 * KB), ("out2", 8 * KD),
]
FIRST_TILE, N_TILES = {}, {}
_n = 0
for _name, _count in SEGMENTS:
    FIRST_TILE[_name], N_TILES[_name] = _n, _count
    _n += _count
    assert _count % TPB == 0
N_BLOCKS = _n // TPB


def blocks_of(name):
    first = FIRST_TILE[name] // TPB
    return list(range(first, first + N_TILES[name] // TPB))


def spread_among(few, many):
    out, placed = [], 0
    for i, b in enumerate(many):
        while placed < len(few) * (i + 1) // len(many):
            out.append(few[placed])
            placed += 1
        out.append(b)
    return out


MOD_FIRST = 16
MOD_EVEN = 16
STREAM = blocks_of("mod0")[:MOD_FIRST] \
    + spread_among(blocks_of("mod0")[MOD_FIRST:] + blocks_of("mod1")[:MOD_EVEN], blocks_of("even_in")) \
    + blocks_of("even_out") + blocks_of("up0") + spread_among(blocks_of("mod1")[MOD_EVEN:], blocks_of("down0"))
for _name in ("ssd_in", "ssd_out", "up1", "down1", "in2", "branch2", "out2"):
    STREAM += blocks_of(_name)
PLACE = {b: i for i, b in enumerate(STREAM)}
assert sorted(STREAM) == list(range(N_BLOCKS))

COLUMNS = [
    ("mod_b0", 48), ("mod_b1", 48), ("mix_g0", 8), ("mix_g1", 8), ("ffn_g0", 8), ("ffn_g1", 8), ("final_g", 8),
    ("conv_w0", 9 * 44), ("conv_w1", 9 * 44), ("conv_b0", 44), ("conv_b1", 44), ("gla_ab", 4),
    ("ml_conv_w", 24), ("ml_conv_b", 8), ("gla_norm", 4), ("ml_norm", 4), ("ml_li_b", 1), ("ml_lf_b", 1),
    ("ssd_conv_w", 72), ("ssd_conv_b", 24), ("ssd_d", 16), ("ssd_norm", 16), ("ssd_dt_b", 1), ("ssd_a_log", 1),
    ("norm2", 8), ("qn_a", 1), ("kn_a", 1), ("qn_c", 1), ("kn_c", 1), ("b_forget", 1), ("lru_conv_w", 16),
    ("lru_conv_b", 4), ("b_rg_a", 4), ("b_rg_x", 4), ("lam", 4), ("cmp_pos", 32),
]
COL = {}
_n = 0
for _name, _count in COLUMNS:
    COL[_name] = _n
    _n += _count
N_COLS = _n


class Count:

    def __init__(self, sem):
        self.sem, self.base, self.total = sem, 0, 0

    def up(self, n=1):
        self.total += n
        return self.sem, n

    def at(self, n):
        return self.sem, self.base + n

    def now(self):
        return self.sem, self.total


class Kit:

    def __init__(self, nc, ctx, dram):
        self.nc, self.dram = nc, dram
        self.scopes = [ctx]
        self.n_taken = 0

        def sb(name, shape, dtype=F32):
            return ctx.enter_context(nc.sbuf_tensor(name, shape, dtype))

        self.ring = sb("weight_ring", [P, RING, TPB * P])
        self.x = sb("x", [P, KD, T])
        self.h_hi = self.h_lo = None
        self.cols = sb("columns", [P, N_COLS])
        self.mod = sb("modulation", [P, 2, 48, 2])
        self.ident = sb("identity", [P, P])
        self.ones = sb("ones", [P, P])
        self.tri_f = sb("tri_f", [P, P])
        self.tri_b = sb("tri_b", [P, P])
        self.small = sb("small", [P, 8])
        self.bank = ctx.enter_context(nc.psum_tensor("banks", [P, BANKS, 512], F32))

        def count(name):
            return Count(ctx.enter_context(nc.semaphore(name)))

        self.loaded = [count(f"weights_loaded{i}") for i in range(RING)]
        self.mod_done = count("modulation_steps")
        self.high_done = count("weights_high_done")
        self.low_done = {"dve": count("weights_low_done_dve"), "pool": count("weights_low_done_pool")}
        self.used = count("weights_used")
        self.done = count("products_done")
        self.cmp_loaded, self.rg_loaded = count("compression_loaded"), count("recurrence_loaded")
        self.spatial_loaded = count("spatial_loaded")
        self.conds, self.silued = count("conditions_loaded"), count("conditions_ready")
        self.release = {}
        self.parts_ready = []
        self.parts_used = []
        self.pool = [count(f"stage_signal{i}") for i in range(48)]
        self.free = list(self.pool)
        self.issued = 0

    def col(self, name, i=0, n=1, rows=slice(0, P)):
        return self.cols[rows, COL[name] + i:COL[name] + i + n]

    def counts(self, n):
        return [self.free.pop() for _ in range(n)]

    def stage_end(self):
        for s in self.pool:
            s.base = s.total
        self.free = list(self.pool)

    @contextmanager
    def scope(self):
        with ExitStack() as ctx:
            self.scopes.append(ctx)
            yield
            self.scopes.pop()

    @contextmanager
    def activations(self, size):
        with self.scope():
            self.h_hi, self.h_lo = self.take(size, dtype=F32R), self.take(size, dtype=F32R)
            yield

    def take(self, *shape, dtype=F32):
        self.n_taken += 1
        t = self.scopes[-1].enter_context(self.nc.sbuf_tensor(f"m{self.n_taken}", [P, int(np.prod(shape))], dtype))
        names = "abcde"[:len(shape)]
        if len(shape) == 1:
            return t[:]
        return t[:].rearrange(f"p ({' '.join(names)}) -> p {' '.join(names)}", **dict(zip(names[1:], shape[1:])))

    def sum_squares(self, t0):
        return self.bank[:, BANKS - 1, 0:T - t0]

    def h_parts(self, width, k, a=0, b=None):
        b = width if b is None else b
        return self.h_hi[:, k * width + a:k * width + b], self.h_lo[:, k * width + a:k * width + b]


def load_weights(K, sync, last_place):
    last = min(N_BLOCKS, last_place + RING)
    while K.issued < last:
        i = K.issued
        if i >= RING:
            sync.wait_ge(*K.release[i - RING])
        sync.dma_start(K.ring[:, i % RING, :], K.dram["weights"][i]).then_inc(*K.loaded[i % RING].up(16))
        K.issued += 1


def wait_loaded(K, eng, place):
    eng.wait_ge(K.loaded[place % RING].sem, 16 * (place // RING + 1))


class Link:

    def __init__(self, eng, step):
        self.eng, self.step = eng, step

    def __call__(self, ins):
        ins.then_inc(*self.step.up())
        self.eng.wait_ge(*self.step.now())


def rsqrt(act, link, out, total, eps, scale):
    link(act.activation(out, total, ACT.Ln, bias=eps, scale=scale))
    return act.activation(out, out, ACT.Exp, scale=-0.5)


def mid(ap, n):
    return ap.unsqueeze(1).broadcast_to([ap.shape[0], n, ap.shape[1]])


def last(ap, n):
    return ap.unsqueeze(2).broadcast_to([ap.shape[0], ap.shape[1], n])



class Product:

    def __init__(self, out, tile, a, start, stop, ends, n=1, moving=False):
        self.out, self.tile, self.a, self.start, self.stop, self.ends = out, tile, a, start, stop, ends
        self.n, self.moving = n, moving


class Item:

    def __init__(self, products, empty, on="act", conv=None):
        self.products, self.empty, self.on, self.conv, self.of_posts = products, empty, on, conv, False


class Conv:

    def __init__(self, n, centre, bias, taps, finish, post=None):
        self.n, self.centre, self.bias, self.taps, self.finish, self.post = n, centre, bias, taps, finish, post


def tile_products(tile, nk, a, n):
    return [Product(lambda o: o[:, 0:n], tile + k, a(k), k == 0, k == nk - 1, (tile + k) % TPB == TPB - 1)
            for k in range(nk)]


def token_products(K, tile, width_h, tokens, width, cols=None):
    n = -(-width // P)
    groups = [[] for _ in tokens]
    for k in range(KD):
        t = tile + k * n
        for i, tok in enumerate(tokens):
            ends = i == len(tokens) - 1 and (t + n) % TPB == 0
            groups[i].append(Product(lambda o: o[:, 0:width], t, K.h_parts(width_h, k, tok * P, tok * P + P),
                                     k == 0, k == KD - 1, ends, width / P, True))
    return groups


def run_products(K, rounds, low_on="dve", mods=None, prepare=None, beside=None, banks=BANKS):
    with K.scope():
        _run_products(K, rounds, low_on, mods, prepare, beside, banks)


def _run_products(K, rounds, low_on, mods, prepare, beside, banks):
    nc = K.nc
    free_act, free_dve, tapped, finished, posted, vector_step = K.counts(6)
    w_hi, w_lo = K.take(PARTS, TPB * P, dtype=F32R), K.take(PARTS, TPB * P, dtype=F32R)
    items = [it for r in rounds for it in r]
    free = {"act": free_act, "dve": free_dve}
    rank, count = [], {"act": 0, "dve": 0}
    for it in items:
        count[it.on] += 1
        rank.append(count[it.on])
    convs = [e for e, it in enumerate(items) if it.conv]
    RAW, ACC, LAG = 4, 6, 3
    finishes = np.cumsum([items[e].conv.finish is not None for e in convs]).tolist()
    posts = np.cumsum([items[e].conv.post is not None for e in convs]).tolist()
    if convs:
        n = max(items[e].conv.n for e in convs)
        raw, acc = K.take(RAW, n), K.take(ACC, n)
    done0 = K.done.total
    first = items[0].products[0].tile // TPB
    last_of = [it.products[-1].tile // TPB - first for it in items]
    n_blocks = last_of[-1] + 1
    part0 = len(K.parts_ready)
    last_place = PLACE[first + n_blocks - 1] + 1
    mod_places = [(PLACE[b], b) for b in (mods[1] if mods else [])]

    n_ahead = sum(PLACE[first + i] < K.issued for i in range(min(AHEAD, n_blocks))) if prepare else 0
    if prepare:
        prepare.take([a[:, i, :] for a, m in ((acc, ACC), (raw, RAW)) for i in range(m)] if convs else None)
    for i in range(n_blocks):
        low = K.low_done["pool" if i < n_ahead else low_on]
        low.total += 1
        K.parts_ready.append(low.now())
        K.release[PLACE[first + i]] = low.now()
    if mods:
        mods[0].plan(mods[1])

    with nc.Block() as block:
        @block.tensor
        def _(pe):
            e, seen, posts_seen = 0, -1, False
            for r in rounds:
                for j in range(len(r)):
                    if e + j >= banks:
                        q = e + j - banks
                        pe.wait_ge(*free[items[q].on].at(rank[q]))
                for k in range(len(r[0].products)):
                    for j, it in enumerate(r):
                        p = it.products[k]
                        if prepare and j == 0 and e * len(it.products) + k < prepare.n:
                            pe.wait_ge(*prepare.ready.at(e * len(it.products) + k + 1))
                        if it.of_posts and not posts_seen:
                            pe.wait_ge(*posted.at(k + 1))
                        b = p.tile // TPB - first
                        if b != seen:
                            seen = b
                            pe.wait_ge(*K.parts_ready[part0 + b])
                        slot, at = (part0 + b) % PARTS, p.tile % TPB * P
                        wh, wl = (w[:, slot, at:at + int(p.n * P)] for w in (w_hi, w_lo))
                        out = p.out(K.bank[:, (e + j) % banks, :])
                        if p.moving:
                            passes = ((p.a[0], wh), (p.a[0], wl), (p.a[1], wh))
                        else:
                            passes = ((wh, p.a[0]), (wh, p.a[1]), (wl, p.a[0]))
                        for i, (lhsT, rhs) in enumerate(passes):
                            mm = pe.matmul(out, lhsT, rhs, start=p.start and i == 0, stop=p.stop and i == 2)
                        done = K.done if k == len(it.products) - 1 else K.used if p.ends else None
                        if done is not None:
                            mm.then_inc(*done.up())
                        if p.ends:
                            K.parts_used.append(done.now())
                posts_seen = posts_seen or r[0].of_posts
                for j in range(len(r)):
                    if beside:
                        beside.tensor(pe, e + j)
                e += len(r)

        @block.sync
        def _(sync):
            if beside:
                beside.sync(sync)
            if mods and not mods[0].loaded:
                mods[0].load(sync)
            load_weights(K, sync, last_place)

        def high_part(act, i):
            wait_loaded(K, act, PLACE[first + i])
            if i >= PARTS:
                act.wait_ge(*K.parts_used[part0 + i - PARTS])
            act.activation(w_hi[:, (part0 + i) % PARTS, :], K.ring[:, PLACE[first + i] % RING, :],
                           ACT.Copy).then_inc(*K.high_done.up())

        def low_part(eng, i, by=low_on):
            slot = (part0 + i) % PARTS
            eng.wait_ge(K.high_done.sem, part0 + i + 1)
            eng.tensor_tensor(w_lo[:, slot, :], K.ring[:, PLACE[first + i] % RING, :], w_hi[:, slot, :].bitcast(F32),
                              ALU.subtract).then_inc(K.low_done[by].sem, 1)

        @block.scalar
        def _(act):
            def finish(i):
                c = items[convs[i]].conv
                if c.finish is None:
                    return
                act.wait_ge(*tapped.at(i + 1))
                c.finish(act, acc[:, i % ACC, 0:c.n]).then_inc(*finished.up())

            if prepare:
                prepare.scalar_first(act)
            for i in range(n_ahead):
                high_part(act, i)
            if prepare:
                prepare.scalar(act)
            n_conv, n_finish, n_high = 0, 0, n_ahead
            if mods and not mods[0].loaded:
                while n_high < AHEAD:
                    high_part(act, n_high)
                    n_high += 1
                mods[0].silu(act)
            for e, it in enumerate(items):
                while n_high < min(n_blocks, last_of[e] + PARTS):
                    high_part(act, n_high)
                    n_high += 1
                if it.on != "act":
                    while n_finish < n_conv:
                        finish(n_finish)
                        n_finish += 1
                    if beside:
                        beside.scalar(act, e, free_dve.at(rank[e]))
                    continue
                act.wait_ge(K.done.sem, done0 + e + 1)
                bank = K.bank[:, e % banks, :]
                if not it.conv:
                    it.empty(act, bank).then_inc(*free_act.up())
                    if beside:
                        beside.scalar(act, e, free_act.now())
                    continue
                c, i = it.conv, n_conv
                if i >= RAW:
                    act.wait_ge(*tapped.at(i - RAW + 1))
                if i >= ACC:
                    old = posts[i - ACC + 1] if items[convs[i - ACC + 1]].conv.post else posts[i - ACC]
                    if old:
                        act.wait_ge(*posted.at(old))
                    if finishes[i - ACC]:
                        act.wait_ge(*finished.at(finishes[i - ACC]))
                act.activation(acc[:, i % ACC, 0:c.n], bank[:, 0:c.n], ACT.Identity, bias=c.bias, scale=c.centre)
                act.activation(raw[:, i % RAW, 0:c.n], bank[:, 0:c.n], ACT.Copy).then_inc(*free_act.up())
                n_conv += 1
                if i >= LAG:
                    finish(i - LAG)
                    n_finish += 1
            for i in range(n_finish, n_conv):
                finish(i)

        @block.vector
        def _(dve):
            def post(i):
                c = items[convs[i]].conv
                if c.post is not None:
                    dve.wait_ge(*finished.at(finishes[i]))
                    c.post(dve, link, acc[:, (i - 1) % ACC, 0:c.n], acc[:, i % ACC, 0:c.n]).then_inc(*posted.up())

            def convolve(group):
                nonlocal n_post
                dve.wait_ge(*free_act.at(rank[convs[group[-1]]]))
                while n_post < group[-1] - LAG:
                    post(n_post)
                    n_post += 1
                last_tap = {}
                for t in range(len(items[convs[group[0]]].conv.taps)):
                    for i in group:
                        c = items[convs[i]].conv
                        region, shift, w = c.taps[t]
                        o = region(acc[:, i % ACC, 0:c.n])
                        if t:
                            dve.wait_ge(*last_tap[i])
                        ins = dve.scalar_tensor_tensor(o, shift(raw[:, i % RAW, 0:c.n]), w, o, ALU.mult, ALU.add)
                        if t == len(c.taps) - 1:
                            ins.then_inc(*tapped.up())
                        else:
                            ins.then_inc(*vector_step.up())
                            last_tap[i] = vector_step.now()

            if prepare:
                prepare.vector(dve)
            link = Link(dve, vector_step)
            i, n_low, n_post = 0, n_ahead, 0
            group = []
            for e, it in enumerate(items):
                while mod_places and mod_places[0][0] < PLACE[first + min(n_blocks, last_of[e] + PARTS) - 1]:
                    mods[0].block(dve, *mod_places.pop(0))
                while low_on == "dve" and n_low < min(n_blocks, last_of[e] + PARTS):
                    low_part(dve, n_low)
                    n_low += 1
                if it.on == "dve":
                    while n_post < i:
                        post(n_post)
                        n_post += 1
                    dve.wait_ge(K.done.sem, done0 + e + 1)
                    it.empty(dve, link, K.bank[:, e % banks, :]).then_inc(*free_dve.up())
                    dve.wait_ge(*free_dve.now())
                if it.conv:
                    group.append(i)
                    i += 1
                    if len(group) == 2 or i == len(convs):
                        convolve(group)
                        group = []
                if beside:
                    beside.vector(dve, e, free_act.at(rank[e]))
            while n_post < i:
                post(n_post)
                n_post += 1
            if mods:
                mods[0].end(dve, mods[1])

        @block.gpsimd
        def _(pool):
            for i in range(n_ahead):
                low_part(pool, i, "pool")
            if beside:
                beside.gpsimd(pool)
            if low_on == "pool":
                for i in range(n_ahead, n_blocks):
                    low_part(pool, i)
    K.stage_end()


class Modulator:

    def __init__(self, K, cond):
        self.K, self.cond = K, cond
        self.unread = K.take(2, D, dtype=BF16)
        self.planned, self.loaded = K.mod_done.total, False

    def plan(self, blocks):
        for b in blocks:
            self.planned += 2
            self.K.release[PLACE[b]] = (self.K.mod_done.sem, self.planned)

    def load(self, sync):
        for c in range(2):
            sync.dma_start(self.cond[:, c, :], self.K.dram["cond"][c].partition_broadcast(P)).then_inc(*self.K.conds.up(16))

    def silu(self, act):
        act.wait_ge(*self.K.conds.now())
        act.activation(self.cond, self.cond, ACT.Silu).then_inc(*self.K.silued.up())
        self.loaded = True

    def block(self, dve, place, b):
        K = self.K
        dve.wait_ge(*K.silued.now())
        layer, j = divmod(b - FIRST_TILE["mod0"] // TPB, 48)
        wait_loaded(K, dve, place)
        for c in range(2):
            if K.mod_done.total >= 2:
                dve.wait_ge(K.mod_done.sem, K.mod_done.total - 1)
            dve.scalar_tensor_tensor(self.unread[:, c, :], K.ring[:, place % RING, :], 1.0, self.cond[:, c, :],
                                     ALU.mult, ALU.mult, accum_out=K.mod[:, layer, j, c:c + 1]).then_inc(*K.mod_done.up())

    def end(self, dve, blocks):
        K = self.K
        dve.wait_ge(*K.mod_done.now())
        first = FIRST_TILE["mod0"] // TPB
        for layer in range(2):
            js = [b - first - 48 * layer for b in blocks if (b - first) // 48 == layer]
            if js:
                m = K.mod[:, layer, js[0]:js[-1] + 1, :]
                dve.tensor_tensor(m, m, last(K.col(f"mod_b{layer}", js[0], len(js)), 2), ALU.add)


def conv_taps_1d(w, n_regions=2):
    def view(a):
        return a.rearrange("p (r t) -> p r t", r=n_regions)
    n = 256
    return [(lambda o: view(o)[:, :, 1:n], lambda r: view(r)[:, :, 0:n - 1], w(0)),
            (lambda o: view(o)[:, :, 0:n - 1], lambda r: view(r)[:, :, 1:n], w(2))]


def conv_taps_ffn(w, with_ctx):
    taps = []
    lat0 = CTX if with_ctx else 0

    def grid(a, r0, r1, c0, c1):
        return a[:, lat0:lat0 + LAT].rearrange("p (r c) -> p r c", c=GRID_W)[:, r0:r1, c0:c1]

    for i in range(3):
        for j in range(3):
            if i == 1 and j == 1:
                continue
            di, dj = i - 1, j - 1
            r0, r1 = max(0, -di), ROWS - max(0, di)
            c0, c1 = max(0, -dj), GRID_W - max(0, dj)
            taps.append((lambda o, r0=r0, r1=r1, c0=c0, c1=c1: grid(o, r0, r1, c0, c1),
                         lambda a, r0=r0 + di, r1=r1 + di, c0=c0 + dj, c1=c1 + dj: grid(a, r0, r1, c0, c1),
                         w(3 * i + j)))
    if with_ctx:
        taps.append((lambda o: o[:, 1:CTX], lambda a: a[:, 0:CTX - 1], w(3)))
        taps.append((lambda o: o[:, 0:CTX - 1], lambda a: a[:, 1:CTX], w(5)))
    return taps


REGIONS = [(0, CTX, 1), (CTX, T, 0)]


def residual_items(K, segment, nk, a, t0, gate):
    items = []
    for n in range(KD):
        def empty(dve, link, bank, n=n):
            for a, b, which in REGIONS:
                if a < t0:
                    continue
                xs, ps = K.x[:, n, a:b], bank[:, a - t0:b - t0]
                if gate is None:
                    ins = dve.tensor_tensor(xs, ps, xs, ALU.add)
                else:
                    ins = dve.scalar_tensor_tensor(xs, ps, gate(n, which), xs, ALU.mult, ALU.add)
            return ins
        items.append([Item(tile_products(FIRST_TILE[segment] + n * nk, nk, a, T - t0), empty, "dve")])
    return items


class Normalise:

    def __init__(self, K, t0, gain, shift_scale=None, rows=None):
        self.rows = rows
        self.K, self.t0, self.gain, self.shift_scale, self.n = K, t0, gain, shift_scale, KD

    def take(self, rows):
        K, self.width = self.K, T - self.t0
        *self.place, self.rstd, amp = (self.rows or rows)[:KD + 2]
        self.amp = amp[:, 0:2 * KD].rearrange("p (w k) -> p w k", k=KD)
        self.rooted, self.scaled, self.normed, self.whole, self.high, self.ready, self.scalar_step = K.counts(7)
        self.parts = [K.h_parts(self.width, k) for k in range(KD)]

    def scalar_first(self, act):
        K = self.K
        rsqrt(act, Link(act, self.scalar_step), self.rstd, K.sum_squares(self.t0), K.small[:, 0:1],
              1.0 / D).then_inc(*self.rooted.up())

    def scalar(self, act):
        K, t0 = self.K, self.t0

        def high_part(k):
            act.wait_ge(*(self.whole if self.shift_scale else self.normed).at(k + 1))
            act.activation(self.parts[k][0], self.place[k], ACT.Copy).then_inc(*self.high.up())

        if not self.shift_scale:
            for k in range(KD):
                high_part(k)
            return
        layer, shift, _scale = self.shift_scale
        act.wait_ge(*self.scaled.at(1))
        for k in range(KD):
            act.wait_ge(*self.normed.at(k + 1))
            for a, b, which in REGIONS:
                if a >= t0:
                    part = self.place[k][:, a - t0:b - t0]
                    ins = act.activation(part, part, ACT.Identity, bias=K.mod[:, layer, shift + k, which:which + 1],
                                         scale=self.amp[:, which, k:k + 1])
            ins.then_inc(*self.whole.up())
            if k:
                high_part(k - 1)
        high_part(KD - 1)

    def vector(self, dve):
        K, t0 = self.K, self.t0
        if self.shift_scale:
            layer, _shift, scale = self.shift_scale
            for which in range(2):
                ins = dve.scalar_tensor_tensor(self.amp[:, which, :], K.mod[:, layer, scale:scale + KD, which], 1.0,
                                               K.col(self.gain, 0, KD), ALU.add, ALU.mult)
            ins.then_inc(*self.scaled.up())

        def norm(k):
            x = K.x[:, k, t0:T]
            if self.shift_scale:
                ins = dve.tensor_tensor(self.place[k], x, self.rstd, ALU.mult)
            else:
                ins = dve.scalar_tensor_tensor(self.place[k], x, K.col(self.gain, k), self.rstd, ALU.mult, ALU.mult)
            ins.then_inc(*self.normed.up())

        dve.wait_ge(*self.rooted.at(1))
        lead = 3
        for k in range(lead):
            norm(k)
        for k in range(KD):
            if k + lead < KD:
                norm(k + lead)
            hi, lo = self.parts[k]
            dve.wait_ge(*self.high.at(k + 1))
            dve.tensor_tensor(lo, self.place[k], hi.bitcast(F32), ALU.subtract).then_inc(*self.ready.up())


class SumSquares:

    def __init__(self, K, t0, beside=True, first=0):
        self.first = first
        self.K, self.t0, self.sq = K, t0, K.take(2, T - t0)
        self.squared, self.added, self.summed = K.counts(3)
        self.beside, self.acc = beside, K.take(T - t0) if beside else None

    def square(self, act, k, made):
        act.wait_ge(*made)
        if self.beside and k >= 3:
            act.wait_ge(*self.added.at(k - 2))
        if not self.beside and k >= 2:
            act.wait_ge(*self.summed.at(k - 1))
        out = self.acc if self.beside and k == 0 else self.sq[:, k % 2, :]
        act.activation(out, self.K.x[:, k, self.t0:T], ACT.Square).then_inc(*self.squared.up())

    def total(self, pe, squares, start, stop):
        return pe.matmul(self.K.sum_squares(self.t0), self.K.ones[:], squares, start=start, stop=stop)

    def add(self, pe, k):
        pe.wait_ge(*self.squared.at(k + 1))
        self.total(pe, self.sq[:, k % 2, :], k == 0, k == KD - 1).then_inc(*self.summed.up())

    def scalar(self, act, item, emptied):
        item -= self.first
        if item:
            self.square(act, item - 1, self.before)
        self.before = emptied
        if item == KD - 1:
            self.square(act, item, emptied)

    def vector(self, dve, item, emptied):
        k = item - self.first - 1
        if 1 <= k < KD - 2:
            dve.wait_ge(*self.squared.at(k + 1))
            if k >= 2:
                dve.wait_ge(*self.added.at(k - 1))
            dve.tensor_tensor(self.acc, self.acc, self.sq[:, k % 2, :], ALU.add).then_inc(*self.added.up())

    def tensor(self, pe, item):
        if item - self.first != KD - 1:
            return
        pe.wait_ge(*self.added.at(KD - 3))
        self.total(pe, self.acc, True, False)
        for k in (KD - 2, KD - 1):
            pe.wait_ge(*self.squared.at(k + 1))
            self.total(pe, self.sq[:, k % 2, :], False, k == KD - 1)

    def sync(self, sync):
        pass

    def gpsimd(self, pool):
        pass


class Split:
    LEAD = 3

    def __init__(self, K, pairs, make=None):
        self.K, self.pairs, self.make, self.n = K, pairs, make, len(pairs)

    def take(self, rows):
        self.made, self.high, self.ready = self.K.counts(3)

    def scalar_first(self, act):
        pass

    def scalar(self, act):
        for i, (whole, hi, _lo) in enumerate(self.pairs):
            if self.make:
                act.wait_ge(*self.made.at(i + 1))
            act.activation(hi, whole, ACT.Copy).then_inc(*self.high.up())

    def vector(self, dve):
        def make(i):
            if self.make and i < self.n:
                self.make(dve, i).then_inc(*self.made.up())

        for i in range(self.LEAD):
            make(i)
        for i, (whole, hi, lo) in enumerate(self.pairs):
            make(i + self.LEAD)
            dve.wait_ge(*self.high.at(i + 1))
            dve.tensor_tensor(lo, whole, hi.bitcast(F32), ALU.subtract).then_inc(*self.ready.up())


def normalise_in_place(K, t0, gain):
    nc = K.nc
    rooted, scalar_step, normed = K.counts(3)
    with K.scope():
        rstd = K.take(T - t0)
        sums = SumSquares(K, t0, False)
        with nc.Block() as block:
            @block.scalar
            def _(act):
                rsqrt(act, Link(act, scalar_step), rstd, K.sum_squares(t0), K.small[:, 0:1],
                      1.0 / D).then_inc(*rooted.up())
                for k in range(KD):
                    sums.square(act, k, normed.at(k + 1))

            @block.vector
            def _(dve):
                dve.wait_ge(*rooted.at(1))
                for k in range(KD):
                    dve.scalar_tensor_tensor(K.x[:, k, t0:T], K.x[:, k, t0:T], K.col(gain, k), rstd, ALU.mult,
                                             ALU.mult).then_inc(*normed.up())

            @block.tensor
            def _(pe):
                for k in range(KD):
                    sums.add(pe, k)
    K.stage_end()


def setup(K, modulator, f, a2):
    nc = K.nc
    filled, loads, tokens, ones = K.counts(4)
    sums = SumSquares(K, 0, False)
    blocks = blocks_of("mod0")[:MOD_FIRST]
    modulator.plan(blocks)

    with nc.Block() as block:
        @block.gpsimd
        def _(pool):
            link = Link(pool, filled)
            for i, v in enumerate((EPS, 1.0, 0.0)):
                link(pool.memset(K.small[:, i:i + 1], v))
            pool.memset(K.ones[:], 1.0).then_inc(*ones.up())
            pool.memset(f["mv"][:, :, :, MD:MD + 1], 1.0)
            for a, v in ((K.ident, 0.0), (K.tri_f, 1.0), (K.tri_b, 1.0)):
                link(pool.memset(a[:], v))
            link(pool.affine_select(out=K.ident[:], in_=K.ident[:], compare_op=ALU.not_equal, fill=1.0, base=0,
                                    pattern=[[-1, P]], channel_multiplier=1))
            link(pool.affine_select(out=K.tri_f[:], in_=K.tri_f[:], compare_op=ALU.is_ge, fill=0.0, base=0,
                                    pattern=[[1, P]], channel_multiplier=-1))
            link(pool.affine_select(out=K.tri_b[:], in_=K.tri_b[:], compare_op=ALU.is_ge, fill=0.0, base=0,
                                    pattern=[[-1, P]], channel_multiplier=1))

        @block.sync
        def _(sync):
            modulator.load(sync)
            sync.dma_start(K.cols[:], K.dram["columns"]).then_inc(*loads.up(16))
            load_weights(K, sync, 0)
            sync.dma_start(K.x[:], K.dram["tokens"]).then_inc(*tokens.up(16))
            load_weights(K, sync, MOD_FIRST)
            sync.dma_start(a2[0:48, :], K.dram["gla_a2"]).then_inc(*loads.up(16))
            sync.wait_ge(*tokens.at(16))
            sync.wait_ge(*loads.at(32))

        @block.scalar
        def _(act):
            modulator.silu(act)
            for k in range(KD):
                sums.square(act, k, tokens.at(16))

        @block.tensor
        def _(pe):
            pe.wait_ge(*ones.at(1))
            for k in range(KD):
                sums.add(pe, k)

        @block.vector
        def _(dve):
            for b in blocks:
                modulator.block(dve, PLACE[b], b)
            dve.wait_ge(*loads.at(16))
            modulator.end(dve, blocks)
    K.stage_end()


def feed_forward(K, layer, t0, mods=None):
    n = T - t0
    with K.scope():
        gated_hi, gated_lo = K.take(KF, n, dtype=F32R), K.take(KF, n, dtype=F32R)
        with K.activations(KD * n):
            rounds = []
            first = FIRST_TILE[f"up{layer}"]
            for j in range(KF):
                for half in range(2):
                    c = half * KF + j

                    def finish(act, acc):
                        return act.activation(acc, acc, ACT.Silu)

                    def post(dve, link, a, g, j=j):
                        link(dve.tensor_tensor(g, a, g, ALU.mult))
                        link(dve.tensor_copy(gated_hi[:, j, :], g))
                        return dve.tensor_tensor(gated_lo[:, j, :], g, gated_hi[:, j, :].bitcast(F32), ALU.subtract)
                    conv = Conv(n, K.col(f"conv_w{layer}", 4 * 44 + c), K.col(f"conv_b{layer}", c),
                                conv_taps_ffn(lambda tap, c=c: K.col(f"conv_w{layer}", tap * 44 + c), t0 == 0),
                                finish if half else None, post if half else None)
                    rounds.append([Item(tile_products(first + (2 * j + half) * KD, KD, lambda k: K.h_parts(n, k), n), None, "act", conv)])
            down = residual_items(K, f"down{layer}", KF, lambda k: (gated_hi[:, k, :], gated_lo[:, k, :]), t0,
                                  lambda m, which: K.mod[:, layer, 40 + m, which:which + 1])
            prepare = Normalise(K, t0, f"ffn_g{layer}", (layer, 24, 32))
            if not mods:
                for r in down:
                    r[0].of_posts = True
                run_products(K, rounds + down, "pool", prepare=prepare, beside=SumSquares(K, t0, first=len(rounds)),
                             banks=BANKS - 1)
                return
            run_products(K, rounds, "pool", prepare=prepare)
        with K.scope():
            modulator = Modulator(K, K.take(2, D))
            run_products(K, down, "pool", (modulator, mods), beside=SumSquares(K, t0), banks=BANKS - 1)


def even_mixer(K, cond_top, a2):
    f, cum = cond_top
    with K.scope():
        R = MlstmGates.R
        parts, gcol, ecol = K.take(T, dtype=F32R), K.take(TT, R), K.take(TT, R)
        with K.scope():
            masks = K.take(GLEVELS, P)
            with K.scope():
                gla_decays(K, f, a2, cum, masks)
            gla(K, f, cum, masks, (parts, gcol, ecol))
        with K.scope():
            mlstm(K, f, parts, gcol, ecol)
    with K.activations(KD * T):
        parts = Split(K, [(f[name][:, j, :], *K.h_parts(T, base + j))
                          for name, base in (("gg", 0), ("mq", 4)) for j in range(4)])
        run_products(K, residual_items(K, "even_out", KD, lambda k: K.h_parts(T, k), 0,
                                       lambda m, which: K.mod[:, 0, 16 + m, which:which + 1]), prepare=parts,
                     beside=SumSquares(K, 0), banks=BANKS - 1)


def even_features(K):
    f = {}
    f["gq"], f["gk"], f["gg"] = K.take(2, T), K.take(2, T), K.take(4, T)
    f["mq"], f["mk"] = K.take(4, T), K.take(4, T)
    f["gv"], f["mv"], f["mo"] = K.take(TT, GW), K.take(TT, MH, MD + 1), K.take(TT, GW)
    f["low"], f["li"], f["lf"] = K.take(T), K.take(T), K.take(T)
    return f, K.take(4, T)


def even_projection(K, f, modulator):
    first = FIRST_TILE["even_in"]
    rounds, tile = [], first

    def h(k):
        return K.h_parts(T, k)

    def put(dest, func, scale=1.0):
        return lambda act, bank: act.activation(dest, bank[0:dest.shape[0], :], func, scale=scale)

    for name, n, func, scale in (("gq", 2, ACT.Copy, GK ** -0.5), ("gk", 2, ACT.Copy, 1.0), ("gg", 4, ACT.Silu, 1.0)):
        for j in range(n):
            rounds.append([Item(tile_products(tile, KD, h, T), put(f[name][:, j, :], func, scale))])
            tile += KD
    for name, base in (("mq", 0), ("mk", 4)):
        for j in range(4):
            c = base + j

            def finish(act, acc, name=name, j=j):
                return act.activation(f[name][:, j, :], acc, ACT.Silu)
            conv = Conv(T, K.col("ml_conv_w", 8 + c), K.col("ml_conv_b", c),
                        conv_taps_1d(lambda tap, c=c: K.col("ml_conv_w", tap * 8 + c)), finish)
            rounds.append([Item(tile_products(tile, KD, h, T), None, "act", conv)])
            tile += KD
    for name in ("gv", "mv", "mo"):
        groups = token_products(K, tile, T, range(TT), GW)

        def empty(i, name=name):
            if name == "mv":
                return lambda act, bank: act.activation(f["mv"][:, i, :, 0:MD],
                                                        bank.rearrange("p (h v) -> p h v", v=MD), ACT.Copy)
            return put(f[name][:, i, :], ACT.Sigmoid if name == "mo" else ACT.Copy)
        rounds.append([Item(g, empty(i)) for i, g in enumerate(groups)])
        tile += 4 * KD
    for dest, m, bias in ((f["low"], 48, None), (f["li"], 36, "ml_li_b"), (f["lf"], 36, "ml_lf_b")):
        def empty(act, bank, dest=dest, m=m, bias=bias):
            if bias is None:
                return act.activation(dest[0:m, :], bank[0:m, :], ACT.Copy)
            return act.activation(dest[0:m, :], bank[0:m, :], ACT.Identity, bias=K.col(bias, rows=slice(0, m)), scale=1.0)
        rounds.append([Item(tile_products(tile, KD, h, T), empty)])
        tile += KD
    run_products(K, rounds, "pool", (modulator, blocks_of("mod0")[MOD_FIRST:] + blocks_of("mod1")[:MOD_EVEN]),
                 Normalise(K, 0, "mix_g0", (0, 0, 8)))


def gla_decays(K, f, a2, la, masks):
    nc = K.nc
    ready, logged, vector_step, scalar_step, pool_step = K.counts(5)
    e = K.take(4, T)
    z = la
    with nc.Block() as block:
        @block.gpsimd
        def _(pool):
            link = Link(pool, pool_step)
            for l in range(1, GLEVELS + 1):
                size, half = 1 << l, 1 << (l - 1)
                n = P // size
                for s_from in (half, 0):
                    m = masks[:, l - 1, :].rearrange("p (b w) -> p b w", w=size)[:, :, half - s_from:size - s_from]
                    link(pool.memset(m, 1.0))
                    link(pool.affine_select(out=m, in_=m, compare_op=ALU.is_ge, fill=0.0, base=-s_from,
                                            pattern=[[-size, n], [0, half]], channel_multiplier=1))
                    link(pool.affine_select(out=m, in_=m, compare_op=ALU.is_ge, fill=0.0, base=s_from + half - 1,
                                            pattern=[[size, n], [0, half]], channel_multiplier=-1))

        @block.tensor
        def _(pe):
            for d in range(2):
                for pair in range(2):
                    r = slice(32 * d, 32 * d + 16)
                    pe.matmul(K.bank[:, 2 * d + pair, :], a2[r, pair * P:pair * P + P], f["low"][r, :],
                              start=True, stop=True).then_inc(*ready.up())

        @block.scalar
        def _(act):
            link = Link(act, scalar_step)
            for i in range(4):
                act.wait_ge(*ready.at(i + 1))
                link(act.activation(z[:, i, :], K.bank[:, i, :], ACT.Identity, bias=K.col("gla_ab", i), scale=1.0))
            link(act.activation(e, z, ACT.Abs))
            link(act.activation(e, e, ACT.Exp, scale=-1.0))
            act.activation(e, e, ACT.Ln, bias=K.small[:, 1:2], scale=1.0).then_inc(*logged.up())

        @block.vector
        def _(dve):
            link = Link(dve, vector_step)
            dve.wait_ge(*logged.at(1))
            link(dve.tensor_scalar(z, z, 0.0, 1.0 / GTAU, ALU.min, ALU.mult))
            link(dve.scalar_tensor_tensor(e, e, -1.0 / GTAU, z, ALU.mult, ALU.add))
            for d in range(2):
                for pair in range(2):
                    for c in range(TT):
                        a, o = e[:, 2 * d + pair, c * P:c * P + P], z[:, 2 * d + pair, c * P:c * P + P]
                        if d:
                            a, o = a[:, ::-1], o[:, ::-1]
                        dve.tensor_tensor_scan(o, K.ones[:], a, 0.0, ALU.mult, ALU.add)
    K.stage_end()


CHUNK_ORDER = ([0, 1, 2, 3], [1, 0, 3, 2])


def gla(K, f, cum, masks, gate_buffers):
    nc = K.nc
    dp = 4
    NF = 3
    factor = K.take(NF, 2, 2, T)
    att = K.take(2, TT, 2, P)
    state = K.take(dp, 3, P)
    cend = K.take(dp, TT)
    kend = factor[:, (GLEVELS + 1) % NF, :, :, :].rearrange("p i a t -> p (i a) t")
    kend_t = factor[:, GLEVELS % NF, :, :, :].rearrange("p i a (c t) -> p (i a) c t", c=TT)
    distances, exps, made, scored, taken, scalar_step = K.counts(6)
    gates = MlstmGates(K, f, *gate_buffers)
    n_scores = 4 * (GLEVELS + 1)
    gate_banks = [K.bank[:, (n_scores + i) % BANKS, :] for i in range(2)]
    with nc.Block() as block:
        @block.gpsimd
        def _(pool):
            for l in range(1, GLEVELS + 1):
                size, half = 1 << l, 1 << (l - 1)
                if l > NF:
                    pool.wait_ge(*scored.at(4 * (l - NF + 1)))
                fwd, bwd = (cum[:, 2 * d:2 * d + 2, :].rearrange("p a (b w) -> p (a b) w", w=size) for d in range(2))
                q, k = (factor[:, l % NF, i, :, :].rearrange("p a (b w) -> p (a b) w", w=size) for i in range(2))
                n = 2 * T // size
                early, late = slice(0, half), slice(half, size)
                f_mid, b_mid = (v.broadcast_to([P, n, half]) for v in (fwd[:, :, half - 1:half], bwd[:, :, half:half + 1]))
                pool.tensor_tensor(q[:, :, late], fwd[:, :, late], f_mid, ALU.subtract)
                pool.tensor_tensor(k[:, :, early], f_mid, fwd[:, :, early], ALU.subtract)
                pool.tensor_tensor(q[:, :, early], bwd[:, :, early], b_mid, ALU.subtract)
                pool.tensor_tensor(k[:, :, late], b_mid, bwd[:, :, late], ALU.subtract).then_inc(*distances.up())
                if l == 1:
                    gates.clear(pool)
            pool.wait_ge(*scored.at(4 * (GLEVELS - NF + 2)))
            for d in range(2):
                view = cum[:, 2 * d:2 * d + 2, :].rearrange("p a (b w) -> p (a b) w", w=P)
                at = 0 if d else P - 1
                o = kend[:, 2 * d:2 * d + 2, :].rearrange("p a (b w) -> p (a b) w", w=P)
                ins = pool.tensor_tensor(o, view[:, :, at:at + 1].broadcast_to([P, 2 * TT, P]), view, ALU.subtract)
            ins.then_inc(*distances.up())

        @block.vector
        def _(dve):
            n_bank = 0

            def take_scores(l):
                nonlocal n_bank
                for i in range(4):
                    n_bank += 1
                    dve.wait_ge(*scored.at(n_bank))
                    if n_bank > 4:
                        dve.wait_ge(*taken.at(n_bank - 4))
                    b = K.bank[:, (n_bank - 1) % BANKS, :].rearrange("p (h t) -> p h t", t=P)
                    o = att[:, i % 2, 2 * (i // 2):2 * (i // 2) + 2, :, :].rearrange("p c h t -> p (c h) t")
                    if l == 0:
                        dve.tensor_scalar(o, b, 2.0, None, ALU.mult).then_inc(*taken.up())
                    else:
                        m = mid(masks[:, l - 1, :].bitcast(I32), 4)
                        dve.copy_predicated(o, m, b).then_inc(*taken.up())

            for l in range(1, GLEVELS + 1):
                dve.wait_ge(*exps.at(l))
                for i, src in enumerate((f["gq"], f["gk"])):
                    a = factor[:, l % NF, i, :, :]
                    ins = dve.tensor_tensor(a, a, src, ALU.mult)
                ins.then_inc(*made.up())
                take_scores(l - 1)
                if l == 2:
                    gates.sums(dve)
                if l == 4:
                    gates.peaks(dve)
            take_scores(GLEVELS)
            dve.wait_ge(*exps.at(GLEVELS + 1))
            for d in range(2):
                dve.tensor_tensor(kend[:, 2 * d:2 * d + 2, :], kend[:, 2 * d:2 * d + 2, :], f["gk"], ALU.mult)
                dve.tensor_tensor(cum[:, 2 * d:2 * d + 2, :], cum[:, 2 * d:2 * d + 2, :], f["gq"], ALU.mult)

        @block.scalar
        def _(act):
            gates.logarithms(act)
            for l in range(1, GLEVELS + 1):
                act.wait_ge(*distances.at(l))
                a = factor[:, l % NF, :, :, :]
                act.activation(a, a, ACT.Exp).then_inc(*exps.up())
                if l == 6:
                    gates.floors(act)
            act.wait_ge(*distances.at(GLEVELS + 1))
            for d in range(2):
                at = 0 if d else P - 1
                act.activation(cend[:, 2 * d:2 * d + 2, :].rearrange("p a b -> p (a b)").unsqueeze(2),
                               cum[:, 2 * d:2 * d + 2, :].rearrange("p a (b w) -> p (a b) w", w=P)[:, :, at:at + 1],
                               ACT.Exp).then_inc(*scalar_step.up())
            act.wait_ge(*scalar_step.at(2))
            act.activation(kend, kend, ACT.Exp)
            act.activation(cum, cum, ACT.Exp).then_inc(*exps.up())
            gates.keep(act, *gate_banks)

        @block.tensor
        def _(pe):
            n = 0

            def scores(q, k):
                nonlocal n
                for i in range(4):
                    if n >= BANKS:
                        pe.wait_ge(*taken.at(n - BANKS + 1))
                    r = slice(GK * (i % 2), GK * (i % 2) + GK)
                    for j in range(4):
                        c, pair = 2 * (i // 2) + j // 2, j % 2
                        mm = pe.matmul(K.bank[:, n % BANKS, j * P:j * P + P], k[r, pair, c * P:c * P + P],
                                       q[r, pair, c * P:c * P + P], start=True, stop=True)
                    mm.then_inc(*scored.up())
                    n += 1
            scores(f["gq"], f["gk"])
            for l in range(1, GLEVELS + 1):
                pe.wait_ge(*made.at(l))
                scores(factor[:, l % NF, 0, :, :], factor[:, l % NF, 1, :, :])
            for i in range(2):
                pe.wait_ge(*taken.at(n_scores - BANKS + 1 + i))
            gates.turn(pe, *gate_banks)
    K.stage_end()
    gla_states(K, f, kend, kend_t, cend, state)
    gla_outputs(K, f, att, cum, state, factor[:, (GLEVELS + 1) % NF, :, :, :],
                factor[:, GLEVELS % NF, :, :, :])


def gla_states(K, f, ke, kend_t, cend, state):
    nc = K.nc
    turned, kept, summed, updated = K.counts(4)
    with nc.Block() as block:
        @block.tensor
        def _(pe):
            for i in range(4):
                for c in range(TT):
                    mm = pe.transpose(K.bank[:, i, c * P:c * P + P], ke[:, i, c * P:c * P + P], K.ident[:])
                mm.then_inc(*turned.up())
            for step in range(3):
                for i in range(4):
                    c = CHUNK_ORDER[i // 2][step]
                    if step == 0:
                        pe.wait_ge(*kept.at(i + 1))
                    if step:
                        pe.wait_ge(*updated.at(4 * (step - 1) + i + 1))
                    for h in range(2):
                        head = 2 * (i % 2) + h
                        mm = pe.matmul(K.bank[GK * h:GK * h + GK, 4 + i, 0:GV], kend_t[:, i, c, GK * h:GK * h + GK],
                                       f["gv"][:, c, head * GV:head * GV + GV], start=True, stop=True)
                    mm.then_inc(*summed.up())

        @block.scalar
        def _(act):
            for i in range(4):
                act.wait_ge(*turned.at(i + 1))
                act.activation(kend_t[:, i, :, :], K.bank[:, i, :].rearrange("p (c k) -> p c k", k=P),
                               ACT.Copy).then_inc(*kept.up())

        @block.vector
        def _(dve):
            for step in range(3):
                for i in range(4):
                    c = CHUNK_ORDER[i // 2][step]
                    dve.wait_ge(*summed.at(4 * step + i + 1))
                    if step == 0:
                        dve.tensor_copy(state[:, i, 0, :], K.bank[:, 4 + i, 0:GV]).then_inc(*updated.up())
                    else:
                        dve.wait_ge(*updated.at(4 * (step - 1) + i + 1))
                        dve.scalar_tensor_tensor(state[:, i, step, :], state[:, i, step - 1, :], cend[:, i, c:c + 1],
                                                 K.bank[:, 4 + i, 0:GV], ALU.mult, ALU.add).then_inc(*updated.up())
    K.stage_end()


def gla_outputs(K, f, att, qc, state, spare, unread):
    nc = K.nc
    made, squared, rooted, scaled, turned, gated, vector_step = K.counts(7)
    on = spare.rearrange("p i a t -> p (i a t)").rearrange("p (c v) -> p c v", v=GW)
    squares = unread.rearrange("p i a t -> p (i a t)").rearrange("p (i v) -> p i v", v=GV)
    ss, rt = K.take(TT, GH), K.take(TT, GH)

    def bank(c, h):
        return K.bank[:, 4 * (h % 2) + c, (h // 2) * GV:(h // 2) * GV + GV]

    with nc.Block() as block:
        @block.tensor
        def _(pe):
            for c in range(TT):
                for h in range(GH):
                    o = bank(c, h)
                    mms = [(att[:, h % 2, c, h // 2, :], f["gv"][:, c, h * GV:h * GV + GV])]
                    r = slice(GK * (h % 2), GK * (h % 2) + GK)
                    for d in range(2):
                        pos = CHUNK_ORDER[d].index(c)
                        if pos:
                            i = 2 * d + h // 2
                            mms.append((qc[r, i, c * P:c * P + P], state[r, i, pos - 1, :]))
                    for j, (a, b) in enumerate(mms):
                        mm = pe.matmul(o, a, b, start=(j == 0), stop=(j == len(mms) - 1))
                mm.then_inc(*made.up())
            for c in range(TT):
                pe.wait_ge(*scaled.at(c + 1))
                for h in range(GH):
                    mm = pe.transpose(K.bank[:, c, h * P:h * P + P], on[:, c, h * GV:h * GV + GV], K.ident[:])
                mm.then_inc(*turned.up())

        @block.scalar
        def _(act):
            for c in range(TT):
                act.wait_ge(*made.at(c + 1))
                for h in range(GH):
                    ins = act.activation(squares[:, GH * c + h, :], bank(c, h), ACT.Square,
                                         accum_out=ss[:, c, h:h + 1])
            ins.then_inc(*squared.up())
            act.wait_ge(*squared.at(1))
            act.activation(rt, ss, ACT.Sqrt, bias=K.small[:, 0:1], scale=1.0 / GV).then_inc(*rooted.up())

        @block.vector
        def _(dve):
            link = Link(dve, vector_step)
            dve.wait_ge(*rooted.at(1))
            link(dve.reciprocal(rt, rt))
            for c in range(TT):
                for e in range(2):
                    ins = dve.tensor_tensor(on[:, c, :].rearrange("p (h v) -> p h v", v=GV)[:, e:GH:2, :],
                                            K.bank[:, 4 * e + c, 0:2 * GV].rearrange("p (h v) -> p h v", v=GV),
                                            last(rt[:, c, e:GH:2], GV), ALU.mult)
                ins.then_inc(*scaled.up())
            for c in range(TT):
                dve.wait_ge(*turned.at(c + 1))
                for h in range(GH):
                    dve.scalar_tensor_tensor(f["gg"][:, h, c * P:c * P + P], K.bank[:, c, h * P:h * P + P],
                                             K.col("gla_norm", h), f["gg"][:, h, c * P:c * P + P], ALU.mult, ALU.mult)
    K.stage_end()


def mlstm_key_tiles(d):
    if d == 0:
        return [(s, [(s, TT)]) for s in range(TT)]
    return [(0, [(0, 1), (2, 4)]), (1, [(0, 4)]), (2, [(2, 3)]), (3, [(2, 4)])]


class MlstmGates:
    R = 36

    def __init__(self, K, f, parts, gcol, ecol):
        self.K, self.parts, self.gcol, self.ecol = K, parts, gcol, ecol
        R = self.R
        self.li, self.lf = f["li"][0:R, :], f["lf"][0:R, :]
        self.e, self.run, self.em, self.peak = (K.take(T)[0:R, :] for _ in range(4))
        self.ones, self.nothing = K.take(T), K.take(T)
        self.step_a, self.step_v, self.logged, self.cleared, self.ems, self.floored, self.turned = K.counts(7)

    def clear(self, pool):
        for a, v in ((self.ones, 1.0), (self.run, 0.0), (self.peak, 0.0), (self.nothing, 0.0)):
            pool.memset(a, v).then_inc(*self.cleared.up())

    def logarithms(self, act):
        link, e = Link(act, self.step_a), self.e
        link(act.activation(e, self.lf, ACT.Abs))
        link(act.activation(e, e, ACT.Exp, scale=-1.0))
        act.activation(e, e, ACT.Ln, bias=self.K.small[0:self.R, 1:2], scale=1.0).then_inc(*self.logged.up())

    def scans(self, link, dve, out, data0, src, op0, op1):
        b = slice(32, 36)
        link(dve.tensor_tensor_scan(out[0:4, :], data0[0:4, :], src[0:4, :], 0.0, op0, op1))
        link(dve.tensor_tensor_scan(out[b, 0:CTX][:, ::-1], data0[b, 0:CTX][:, ::-1], src[b, 0:CTX][:, ::-1], 0.0, op0, op1))
        link(dve.tensor_tensor_scan(out[b, CTX:T][:, ::-1], data0[b, CTX:T][:, ::-1], src[b, CTX:T][:, ::-1], out[b, 0:1],
                                    op0, op1))

    def sums(self, dve):
        link = Link(dve, self.step_v)
        dve.wait_ge(*self.logged.at(1))
        link(dve.scalar_tensor_tensor(self.e, self.lf, 0.0, self.e, ALU.min, ALU.subtract))
        dve.wait_ge(*self.cleared.at(4))
        self.scans(link, dve, self.run, self.ones, self.e, ALU.mult, ALU.add)
        link(dve.tensor_tensor(self.li, self.li, self.run, ALU.subtract))

    def peaks(self, dve):
        link = Link(dve, self.step_v)
        self.scans(link, dve, self.peak, self.li, self.li, ALU.max, ALU.max)
        dve.tensor_tensor(self.em, self.run, self.peak, ALU.add).then_inc(*self.ems.up())
        link(dve.tensor_copy(self.parts, self.nothing))
        link(dve.tensor_copy(self.parts[0:self.R, :], self.peak))
        dve.tensor_tensor(self.parts[64:64 + self.R, :], self.peak, self.parts[0:self.R, :].bitcast(F32), ALU.subtract)

    def floors(self, act):
        act.wait_ge(*self.ems.at(1))
        act.activation(self.em, self.em, ACT.Exp, scale=-1.0).then_inc(*self.floored.up())

    def turn(self, pe, g_bank, e_bank):
        pe.wait_ge(*self.floored.at(1))
        R = self.R
        for c in range(TT):
            pe.transpose(g_bank[:, c * R:c * R + R], self.li[:, c * P:c * P + P], self.K.ident[0:R, 0:R])
            mm = pe.transpose(e_bank[:, c * R:c * R + R], self.em[:, c * P:c * P + P], self.K.ident[0:R, 0:R])
        mm.then_inc(*self.turned.up())

    def keep(self, act, g_bank, e_bank):
        act.wait_ge(*self.turned.at(1))
        act.activation(self.gcol.rearrange("p c r -> p (c r)"), g_bank[:, 0:TT * self.R], ACT.Copy, scale=-1.0)
        act.activation(self.ecol.rearrange("p c r -> p (c r)"), e_bank[:, 0:TT * self.R], ACT.Copy)


def mlstm(K, f, parts, gcol, ecol):
    nc = K.nc
    pick = K.take(64, dtype=F32R)
    NW = 3
    W = K.take(NW, TT, T)
    qk = K.take(2, TT, T)
    hacc = K.take(TT, GW)
    den = K.take(2, TT)
    raised, scored, kept, eased, exped, weighted, made, unit_done, picks, vector_step = K.counts(10)
    PEAK, QK, OUT = (0, 7), 1, (3, 5)
    UNITS = 2 * MH
    with nc.Block() as block:
        @block.tensor
        def _(pe):
            def scores(h, half):
                if h or half:
                    pe.wait_ge(*kept.at(2 * h + half))
                for i in range(2):
                    s = 2 * half + i
                    mm = pe.matmul(K.bank[:, QK + i, :], f["mk"][:, h, s * P:s * P + P], f["mq"][:, h, :],
                                   start=True, stop=True)
                mm.then_inc(*scored.up())

            def spread(u):
                h, d = u // 2, u % 2
                if u >= 2:
                    pe.wait_ge(*eased.at(u - 1))
                r = h + 32 * d
                pe.matmul(K.bank[:, PEAK[u % 2], :], pick[:, r:r + 1].broadcast_to([P, P]), parts,
                          start=True, stop=True).then_inc(*raised.up())

            scores(0, 0)
            scores(0, 1)
            pe.wait_ge(*picks.at(1))
            spread(0)
            spread(1)
            for u in range(UNITS):
                h, d = u // 2, u % 2
                if u + 2 < UNITS:
                    spread(u + 2)
                if d == 1 and h + 1 < MH:
                    scores(h + 1, 1)
                pe.wait_ge(*weighted.at(u + 1))
                if u >= 2:
                    pe.wait_ge(*unit_done.at(u - 1))
                tiles = mlstm_key_tiles(d)
                for t in range(TT):
                    seen = [s for s, ranges in tiles if any(a <= t < b for a, b in ranges)]
                    o = K.bank[:, OUT[u % 2] + t // 2, (t % 2) * 256:(t % 2) * 256 + MD + 1]
                    for j, s in enumerate(seen):
                        mm = pe.matmul(o, W[:, u % NW, s, t * P:t * P + P], f["mv"][:, s, h, :],
                                       start=(j == 0), stop=(j == len(seen) - 1))
                mm.then_inc(*made.up())
                if d == 0 and h + 1 < MH:
                    scores(h + 1, 0)

        @block.vector
        def _(dve):
            link = Link(dve, vector_step)

            def weigh(u):
                h, d = u // 2, u % 2
                dve.wait_ge(*kept.at(2 * h + 2))
                dve.wait_ge(*exped.at(u + 1))
                tiles = mlstm_key_tiles(d)
                for s, ranges in tiles:
                    for a, b in ranges:
                        w = W[:, u % NW, s, a * P:b * P]
                        ins = dve.tensor_tensor(w, w, qk[:, h % 2, s, a * P:b * P], ALU.mult)
                link(ins)
                diagonal = W[:, u % NW, :, :].rearrange("p s (c t) -> p (s c) t", t=P)[:, 0:TT * TT:TT + 1, :]
                tri = K.tri_b if d else K.tri_f
                dve.tensor_tensor(diagonal, diagonal, mid(tri[:], TT), ALU.mult).then_inc(*weighted.up())

            def divide(u):
                h, d = u // 2, u % 2
                r = h + 32 * d
                dve.wait_ge(*made.at(u + 1))
                dn = den[:, u % 2, :]
                total = K.bank[:, OUT[u % 2]:OUT[u % 2] + 2, :].rearrange("p b (u x) -> p b u x", x=256)[:, :, :, MD]
                floor = ecol[:, :, r].rearrange("p (b u) -> p b u", u=2)
                dn2 = dn.rearrange("p (b u) -> p b u", u=2)
                link(dve.scalar_tensor_tensor(dn2, total, -1.0, floor, ALU.mult, ALU.max))
                link(dve.tensor_tensor(dn2, total, dn2, ALU.max))
                link(dve.reciprocal(dn, dn))
                for t in range(TT):
                    o = K.bank[:, OUT[u % 2] + t // 2, (t % 2) * 256:(t % 2) * 256 + MD]
                    acc = hacc[:, t, h * MD:h * MD + MD]
                    if d == 0:
                        ins = dve.tensor_scalar(acc, o, dn[:, t:t + 1], None, ALU.mult)
                    else:
                        ins = dve.scalar_tensor_tensor(acc, o, dn[:, t:t + 1], acc, ALU.mult, ALU.add)
                ins.then_inc(*unit_done.up())
                dve.wait_ge(*unit_done.now())

            dve.tensor_copy(pick[0:64, :], K.ident[0:64, 0:64])
            dve.tensor_copy(pick[64:P, :], K.ident[64:P, 64:P]).then_inc(*picks.up())
            for u in range(UNITS):
                weigh(u)
                if u:
                    divide(u - 1)
            divide(UNITS - 1)

        @block.scalar
        def _(act):
            def keep(h, half):
                act.wait_ge(*scored.at(2 * h + half + 1))
                if h >= 2:
                    act.wait_ge(*weighted.at(2 * h - 2))
                act.activation(qk[:, h % 2, 2 * half:2 * half + 2, :], K.bank[:, QK:QK + 2, :], ACT.Copy,
                               scale=MD ** -0.5).then_inc(*kept.up())

            def ease(u):
                h, d = u // 2, u % 2
                r = h + 32 * d
                act.wait_ge(*raised.at(u + 1))
                if u >= NW:
                    act.wait_ge(*made.at(u - NW + 1))
                tiles = mlstm_key_tiles(d)
                for s, ranges in tiles:
                    for a, b in ranges:
                        ins = act.activation(W[:, u % NW, s, a * P:b * P], K.bank[:, PEAK[u % 2], a * P:b * P], ACT.Relu,
                                             bias=gcol[:, s, r:r + 1], scale=1.0)
                ins.then_inc(*eased.up())

            keep(0, 0)
            keep(0, 1)
            ease(0)
            ease(1)
            for u in range(UNITS):
                h, d = u // 2, u % 2
                act.wait_ge(*eased.at(u + 1))
                tiles = mlstm_key_tiles(d)
                for s, ranges in tiles:
                    for a, b in ranges:
                        w = W[:, u % NW, s, a * P:b * P]
                        ins = act.activation(w, w, ACT.Exp, scale=-1.0)
                ins.then_inc(*exped.up())
                if d == 1 and h + 1 < MH:
                    keep(h + 1, 0)
                if u + 2 < UNITS:
                    ease(u + 2)
                if d == 1 and h + 1 < MH:
                    keep(h + 1, 1)
    K.stage_end()

    gatedh, squared, rooted, scaled, turned, vector_step = K.counts(6)
    squares = W[:, 0:2, :, :].rearrange("p u s t -> p (u s t)").rearrange("p (i v) -> p i v", v=MD)
    ss, rt = K.take(TT, MH), K.take(TT, MH)
    with nc.Block() as block:
        @block.vector
        def _(dve):
            link = Link(dve, vector_step)
            dve.tensor_tensor(hacc, hacc, f["mo"], ALU.mult).then_inc(*gatedh.up())
            dve.wait_ge(*rooted.at(1))
            link(dve.reciprocal(rt, rt))
            for c in range(TT):
                v = hacc[:, c, :].rearrange("p (h v) -> p h v", v=MD)
                dve.tensor_tensor(v, v, last(rt[:, c, :], MD), ALU.mult).then_inc(*scaled.up())
            for c in range(TT):
                dve.wait_ge(*turned.at(c + 1))
                for h in range(MH):
                    dve.tensor_scalar(f["mq"][:, h, c * P:c * P + P], K.bank[:, c, h * P:h * P + P],
                                      K.col("ml_norm", h), None, ALU.mult)

        @block.scalar
        def _(act):
            act.wait_ge(*gatedh.at(1))
            for c in range(TT):
                for h in range(MH):
                    ins = act.activation(squares[:, MH * c + h, :], hacc[:, c, h * MD:h * MD + MD], ACT.Square,
                                         accum_out=ss[:, c, h:h + 1])
            ins.then_inc(*squared.up())
            act.wait_ge(*squared.at(1))
            act.activation(rt, ss, ACT.Sqrt, bias=K.small[:, 0:1], scale=1.0 / MD).then_inc(*rooted.up())

        @block.tensor
        def _(pe):
            for c in range(TT):
                pe.wait_ge(*scaled.at(c + 1))
                for h in range(MH):
                    mm = pe.transpose(K.bank[:, c, h * P:h * P + P], hacc[:, c, h * MD:h * MD + MD], K.ident[:])
                mm.then_inc(*turned.up())
    K.stage_end()

def log1p_small(link, dve, e, t, w, w2):
    link(dve.tensor_scalar(t, e, 2.0, None, ALU.add))
    link(dve.reciprocal(t, t))
    link(dve.tensor_tensor(w, e, t, ALU.mult))
    link(dve.tensor_tensor(w2, w, w, ALU.mult))
    link(dve.tensor_scalar(t, w2, 1.0 / 17.0, None, ALU.mult))
    for n in (15, 13, 11, 9, 7, 5, 3):
        link(dve.scalar_tensor_tensor(t, t, 1.0 / n, w2, ALU.add, ALU.mult))
    link(dve.scalar_tensor_tensor(t, t, 1.0, w, ALU.add, ALU.mult))
    link(dve.tensor_scalar(e, t, 2.0, None, ALU.mult))


def odd_mixer(K):
    with K.scope():
        zs, xl, xc = K.take(KI, LAT), K.take(KI, LAT), K.take(KI, CTX)
        bt, ct, dt = K.take(SG, T), K.take(SG, LAT), K.take(T)[0:64, :]
        cum, dcol = K.take(T)[0:64, :], K.take(6, 64)
        with K.activations(KD * T):
            ssd_projection(K, zs, xl, xc, bt, ct, dt, cum, dcol)
        with K.scope():
            xt, bs, state = K.take(TT, SI), K.take(LT, SG, SN), K.take(2, SI)
            ssd_turn(K, xc, xl, bt, xt, bs)
            back_x = K.take(LT, SI)
            wx = xc.rearrange("p a t -> p (a t)").rearrange("p (c x) -> p c x", c=2)
            ssd_context(K, wx, xt, back_x, bs, dcol, state)
            cb = xt[:, 0:2, :].rearrange("p c x -> p (c x)")[:, 0:2 * SG * 3 * P]
            spare = (bs.rearrange("p c g n -> p (c g n)"), xt[:, 0:2, :].rearrange("p c x -> p (c x)")[:, 2 * SG * 3 * P:])
            cb = cb.rearrange("p (d g b t) -> p d g b t", d=2, g=SG, b=3)
            with K.scope():
                ssd_latent(K, xl, xt[:, LT:TT, :], back_x, bt, ct, cb, state, cum, dcol, spare)
            normed = ssd_combine(K, xl, zs, xc)
        with K.activations(KI * LAT):
            parts = Split(K, [(xl[:, c, :], *K.h_parts(LAT, c)) for c in range(KI)], normed)
            run_products(K, residual_items(K, "ssd_out", KI, lambda k: K.h_parts(LAT, k), CTX,
                                           lambda m, which: K.mod[:, 1, 16 + m, which:which + 1]), prepare=parts,
                         beside=SumSquares(K, CTX), banks=BANKS - 1)


def ssd_projection(K, zs, xl, xc, bt, ct, dt, cum, dcol):
    first = FIRST_TILE["ssd_in"]
    rounds, tile = [], first
    for c in range(24):
        n = T if c < 20 else LAT

        def finish(act, acc, c=c):
            if c < 16:
                act.activation(xc[:, c, :], acc[:, 0:CTX], ACT.Silu)
                return act.activation(xl[:, c, :], acc[:, CTX:T], ACT.Silu)
            return act.activation(bt[:, c - 16, :] if c < 20 else ct[:, c - 20, :], acc, ACT.Silu)
        conv = Conv(n, K.col("ssd_conv_w", 24 + c), K.col("ssd_conv_b", c),
                    conv_taps_1d(lambda tap, c=c: K.col("ssd_conv_w", tap * 24 + c), n // 256), finish)
        rounds.append([Item(tile_products(tile, KD, lambda k, n=n: K.h_parts(T, k, T - n, T), n), None, "act", conv)])
        tile += KD
    rounds.append([Item(tile_products(tile, KD, lambda k: K.h_parts(T, k), T),
                        lambda act, bank: act.activation(dt, bank[0:64, :], ACT.Identity,
                                                         bias=K.col("ssd_dt_b", rows=slice(0, 64)), scale=1.0))])
    tile += KD
    for c in range(KI):
        rounds.append([Item(tile_products(tile, KD, lambda k: K.h_parts(T, k, CTX, T), LAT),
                            lambda act, bank, c=c: act.activation(zs[:, c, :], bank[:, 0:LAT], ACT.Silu))])
        tile += KD
    run_products(K, rounds, "pool", prepare=Normalise(K, 0, "mix_g1", (1, 0, 8)), beside=SsdSteps(K, dt, cum, dcol),
                 banks=BANKS - 1)


class SsdSteps:
    FIRST, SECOND, LAST = 25, 36, 40

    def __init__(self, K, dt, cum, dcol):
        self.K, self.dt, self.cum, self.dcol, self.R = K, dt, cum, dcol, slice(0, 64)
        self.e, self.t, self.w, self.w2, self.la = (K.take(T)[self.R, :] for _ in range(5))
        self.wend, self.acol = K.take(CTX)[self.R, :], K.take(2)[self.R, :]
        self.step_a, self.step_v, self.exped, self.summed, self.decayed, self.ready, self.turned = K.counts(7)

    def scalar(self, act, item, emptied):
        K, e = self.K, self.e
        link = Link(act, self.step_a)
        if item == self.FIRST:
            act.wait_ge(*emptied)
            link(act.activation(self.acol[:, 0:1], K.col("ssd_a_log", rows=self.R), ACT.Exp))
            link(act.activation(e, self.dt, ACT.Abs))
            act.activation(e, e, ACT.Exp, scale=-1.0).then_inc(*self.exped.up())
        if item == self.SECOND:
            act.wait_ge(*self.summed.at(1))
            act.activation(self.wend, self.wend, ACT.Exp, scale=-1.0).then_inc(*self.decayed.up())

    def sync(self, sync):
        pass

    def gpsimd(self, pool):
        pass

    def vector(self, dve, item, emptied):
        if item != self.LAST:
            return
        e, w, la, dt, cum, wend = self.e, self.w, self.la, self.dt, self.cum, self.wend
        link = Link(dve, self.step_v)
        dve.wait_ge(*self.exped.at(1))
        log1p_small(link, dve, e, self.t, w, self.w2)
        link(dve.scalar_tensor_tensor(dt, dt, 0.0, e, ALU.max, ALU.add))
        link(dve.tensor_scalar(la, dt, self.acol[:, 0:1], -1.0, ALU.mult, ALU.mult))
        one = w
        link(dve.memset(one, 1.0))
        for a, b in ((0, CTX), (CTX, T)):
            link(dve.tensor_tensor_scan(cum[0:32, a:b], one[0:32, a:b], la[0:32, a:b], 0.0, ALU.mult, ALU.add))
            link(dve.tensor_tensor_scan(cum[32:64, a:b][:, ::-1], one[32:64, a:b], la[32:64, a:b][:, ::-1], 0.0,
                                        ALU.mult, ALU.add))
        dve.tensor_scalar(wend[0:32, :], cum[0:32, 0:CTX], cum[0:32, CTX - 1:CTX], None, ALU.subtract)
        dve.tensor_scalar(wend[32:64, :], cum[32:64, 0:CTX], cum[32:64, 0:1], None, ALU.subtract).then_inc(*self.summed.up())
        dve.wait_ge(*self.decayed.at(1))
        dve.tensor_tensor(wend, wend, dt[:, 0:CTX], ALU.mult).then_inc(*self.ready.up())
        dve.wait_ge(*self.turned.at(1))
        dve.tensor_copy(self.dcol.rearrange("p i h -> p (i h)"), self.K.bank[:, BANKS - 1, 0:6 * 64])

    def tensor(self, pe, item):
        if item != self.LAST:
            return
        pe.wait_ge(*self.ready.at(1))
        for i, src in enumerate((self.wend, self.dt[:, CTX:T], self.cum[:, CTX:T])):
            for c in range(LT):
                mm = pe.transpose(self.K.bank[:, BANKS - 1, (2 * i + c) * 64:(2 * i + c) * 64 + 64], src[:, c * P:c * P + P],
                                  self.K.ident[self.R, 0:64])
        mm.then_inc(*self.turned.up())


WEND, DT, CUM = 0, 2, 4


def ssd_turn(K, xc, xl, bt, xt, bs):
    nc = K.nc
    turned, kept = K.counts(2)
    jobs = []
    for c in range(TT):
        for q in range(KI // 4):
            src = [(xc if c < LT else xl)[:, 4 * q + i, (c % LT) * P:(c % LT) * P + P] for i in range(4)]
            jobs.append((src, xt[:, c, q * 512:q * 512 + 512]))
    for c in range(LT):
        jobs.append(([bt[:, g, c * P:c * P + P] for g in range(SG)], bs[:, c, :, :].rearrange("p g n -> p (g n)")))
    with nc.Block() as block:
        @block.tensor
        def _(pe):
            for j, (src, _d) in enumerate(jobs):
                if j >= BANKS:
                    pe.wait_ge(*kept.at(j - BANKS + 1))
                for i, a in enumerate(src):
                    mm = pe.transpose(K.bank[:, j % BANKS, i * P:i * P + P], a, K.ident[:])
                mm.then_inc(*turned.up())

        @block.scalar
        def _(act):
            for j, (_s, dest) in enumerate(jobs):
                act.wait_ge(*turned.at(j + 1))
                act.activation(dest, K.bank[:, j % BANKS, :], ACT.Copy).then_inc(*kept.up())
    K.stage_end()


def ssd_context(K, wx, xt, xb, bs, dcol, state):
    nc = K.nc
    weighted, summed, vector_step = K.counts(3)
    with nc.Block() as block:
        @block.vector
        def _(dve):
            for d in range(2):
                if d:
                    dve.wait_ge(*summed.at(SG))
                for c in range(LT):
                    dve.tensor_tensor(wx[:, c, :].rearrange("p (h x) -> p h x", x=SP),
                                      xt[:, c, :].rearrange("p (h x) -> p h x", x=SP),
                                      last(dcol[:, WEND + c, 32 * d:32 * d + 32], SP), ALU.mult).then_inc(*weighted.up())
            xf, vector_steps = xt[:, LT:TT, :], Link(dve, vector_step)
            for d in (1, 0):
                for c in range(LT):
                    o = xb[:, c, :] if d else xf[:, c, :]
                    vector_steps(dve.tensor_tensor(o.rearrange("p (h x) -> p h x", x=SP),
                                                   xf[:, c, :].rearrange("p (h x) -> p h x", x=SP),
                                                   last(dcol[:, DT + c, 32 * d:32 * d + 32], SP), ALU.mult))

        @block.tensor
        def _(pe):
            for d in range(2):
                pe.wait_ge(*weighted.at(2 * d + 2))
                for g in range(SG):
                    for c in range(LT):
                        mm = pe.matmul(K.bank[:, SG * d + g, :], bs[:, c, g, :], wx[:, c, g * 512:g * 512 + 512],
                                       start=(c == 0), stop=(c == LT - 1))
                    mm.then_inc(*summed.up())

        @block.scalar
        def _(act):
            for i in range(2 * SG):
                act.wait_ge(*summed.at(i + 1))
                act.activation(state[:, i // SG, (i % SG) * 512:(i % SG) * 512 + 512], K.bank[:, i, :], ACT.Copy)
    K.stage_end()


def ssd_latent(K, xl, xf, xb, bt, ct, cb, state, cum, dcol, spare):
    nc = K.nc
    blocks = (((0, 0, True), (0, 1, False), (1, 1, True)), ((1, 0, False), (1, 1, True), (0, 0, True)))
    made, = K.counts(1)
    with nc.Block() as block:
        @block.tensor
        def _(pe):
            for g in range(SG):
                for s in range(LT):
                    mm = pe.matmul(K.bank[:, g, s * LAT:s * LAT + LAT], bt[:, g, CTX + s * P:CTX + s * P + P],
                                   ct[:, g, :], start=True, stop=True)
                mm.then_inc(*made.up())

        @block.vector
        def _(dve):
            for g in range(SG):
                dve.wait_ge(*made.at(g + 1))
                for d in range(2):
                    for b, (s, t, diag) in enumerate(blocks[d]):
                        src = K.bank[:, g, s * LAT + t * P:s * LAT + t * P + P]
                        if diag:
                            dve.tensor_tensor(cb[:, d, g, b, :], src, (K.tri_b if d else K.tri_f)[:], ALU.mult)
                        else:
                            dve.tensor_copy(cb[:, d, g, b, :], src)
    K.stage_end()

    NW, NX, NY, AHEAD = 6, 5, 3, 2
    PER_BANK = 8
    W = K.take(NW, 3, P)
    enter = [a.rearrange("p (i t) -> p i t", t=LAT)[:, i, :] for a in spare for i in range(4)]
    sums, minus = K.take(LAT, dtype=F32R), K.take(64, dtype=F32R)
    latent = cum[:, CTX:T]
    units = [(h // 8, h, d) for h in range(SI // SP) for d in range(2)]
    raised, opened, bounded, exped, weighted, entered, used, added, prepared, vector_step = K.counts(10)

    def on_act(u):
        return u % 4 < 3

    with nc.Block() as block:
        @block.tensor
        def _(pe):
            def spread(u):
                g, h, d = units[u]
                if u >= NX:
                    pe.wait_ge(*exped.at(u - NX + 1))
                r = 32 * d + h
                pe.matmul(K.bank[:, u % NX, 0:LAT], minus[:, r:r + 1].broadcast_to([P, P]), sums, start=True,
                          stop=True).then_inc(*raised.up())

            pe.wait_ge(*prepared.at(1))
            for u in range(NX - 1):
                spread(u)
            for u, (g, h, d) in enumerate(units):
                if u + NX - 1 < len(units):
                    spread(u + NX - 1)
                n_bank = u // PER_BANK
                if u % PER_BANK == 0 and n_bank >= NY:
                    pe.wait_ge(*added.at(n_bank - NY + 1))
                pe.wait_ge(*weighted.at(u + 1))
                pe.wait_ge(*entered.at(u + 1))
                o = K.bank[SP * (h % 2):SP * (h % 2) + SP, NX + n_bank % NY, (h // 2 % 2) * LAT:(h // 2 % 2) * LAT + LAT]
                x, mine = xb if d else xf, slice(h * SP, h * SP + SP)
                sa, (sb, tb, _diag) = blocks[d][0][0], blocks[d][2]
                w = W[:, u % NW, :, :]
                pe.matmul(o, x[:, sa, mine], w[:, 0:2, :].rearrange("p b t -> p (b t)"), start=(d == 0), stop=False)
                pe.matmul(o[:, tb * P:tb * P + P], x[:, sb, mine], w[:, 2, :], start=False, stop=False)
                pe.matmul(o, state[:, d, mine], enter[u % NW], start=False,
                          stop=(d == 1)).then_inc(*used.up())

        @block.vector
        def _(dve):
            link = Link(dve, vector_step)

            def bound(u):
                g, h, d = units[u]
                dve.wait_ge(*opened.at(u + 1))
                sa, (sb, tb, _diag) = blocks[d][0][0], blocks[d][2]
                w, row, r = W[:, u % NW, :, :].rearrange("p b t -> p (b t)"), K.bank[:, u % NX, 0:LAT], 32 * d + h
                if not on_act(u):
                    dve.tensor_scalar(w[:, 0:LAT], row, dcol[:, CUM + sa, r:r + 1], 0.0, ALU.add, ALU.max)
                dve.tensor_scalar(w[:, LAT:LAT + P], row[:, tb * P:tb * P + P], dcol[:, CUM + sb, r:r + 1], 0.0, ALU.add,
                                  ALU.max).then_inc(*bounded.up())

            def weigh(u):
                g, h, d = units[u]
                dve.wait_ge(*exped.at(u + 1))
                w = W[:, u % NW, 0:3, :]
                dve.tensor_tensor(w, w, cb[:, d, g, :, :], ALU.mult).then_inc(*weighted.up())

            def add(n_bank):
                dve.wait_ge(*used.at(PER_BANK * n_bank + PER_BANK))
                for i in range(2):
                    c = 2 * n_bank + i
                    ins = dve.scalar_tensor_tensor(xl[:, c, :], xl[:, c, :], K.col("ssd_d", c),
                                                   K.bank[:, NX + n_bank % NY, i * LAT:i * LAT + LAT], ALU.mult, ALU.add)
                ins.then_inc(*added.up())

            dve.tensor_scalar(minus[0:64, :], K.ident[0:64, 0:64], -1.0, None, ALU.mult)
            dve.tensor_scalar(minus[64:P, :], K.ident[64:P, 64:P], -1.0, None, ALU.mult)
            link(dve.tensor_copy(sums[0:64, :], latent))
            dve.tensor_tensor(sums[64:P, :], latent, sums[0:64, :].bitcast(F32), ALU.subtract).then_inc(*prepared.up())
            for u in range(AHEAD):
                bound(u)
            for u in range(len(units)):
                if u + AHEAD < len(units):
                    bound(u + AHEAD)
                weigh(u)
                if u % PER_BANK == 2 and u > PER_BANK:
                    add(u // PER_BANK - 1)
            add(len(units) // PER_BANK - 1)

        @block.scalar
        def _(act):
            def open_unit(u):
                g, h, d = units[u]
                act.wait_ge(*raised.at(u + 1))
                if u >= NW:
                    act.wait_ge(*used.at(u - NW + 1))
                w, row = W[:, u % NW, :, :], K.bank[:, u % NX, 0:LAT]
                if on_act(u):
                    act.activation(w[:, 0:2, :].rearrange("p b t -> p (b t)"), row, ACT.Relu,
                                   bias=dcol[:, CUM + blocks[d][0][0], 32 * d + h:32 * d + h + 1], scale=1.0)
                act.activation(enter[u % NW], row, ACT.Exp, scale=-1.0).then_inc(*opened.up())

            for u in range(AHEAD):
                open_unit(u)
            for u in range(len(units)):
                if u + AHEAD < len(units):
                    open_unit(u + AHEAD)
                act.wait_ge(*bounded.at(u + 1))
                w = W[:, u % NW, 0:3, :]
                act.activation(w, w, ACT.Exp, scale=-1.0).then_inc(*exped.up())

        @block.gpsimd
        def _(pool):
            for u, (g, h, d) in enumerate(units):
                pool.wait_ge(*opened.at(u + 1))
                pool.tensor_tensor(enter[u % NW], enter[u % NW], ct[:, g, :], ALU.mult).then_inc(*entered.up())
    K.stage_end()


def ssd_combine(K, xl, zs, sq):
    nc = K.nc
    gated, squared, summed, scalar_step = K.counts(4)
    rstd = zs[:, 0:SG, :]
    with nc.Block() as block:
        @block.tensor
        def _(pe):
            for g in range(SG):
                pe.wait_ge(*squared.at(4 * g + 4))
                for c in range(4):
                    mm = pe.matmul(K.bank[:, 2 * g, 0:LAT], K.ones[:], sq[:, 4 * g + c, :], start=(c == 0), stop=(c == 3))
                mm.then_inc(*summed.up())

        @block.vector
        def _(dve):
            for c in range(KI):
                dve.tensor_tensor(xl[:, c, :], xl[:, c, :], zs[:, c, :], ALU.mult).then_inc(*gated.up())

        @block.scalar
        def _(act):
            for c in range(KI):
                act.wait_ge(*gated.at(c + 1))
                act.activation(sq[:, c, :], xl[:, c, :], ACT.Square).then_inc(*squared.up())
            for g in range(SG):
                act.wait_ge(*summed.at(g + 1))
                act.activation(rstd[:, g, :], K.bank[:, 2 * g, 0:LAT], ACT.Ln, bias=K.small[:, 0:1],
                               scale=1.0 / 512).then_inc(*scalar_step.up())
            for g in range(SG):
                act.wait_ge(*scalar_step.at(g + 1))
                act.activation(rstd[:, g, :], rstd[:, g, :], ACT.Exp, scale=-0.5)
    K.stage_end()
    return lambda dve, c: dve.scalar_tensor_tensor(xl[:, c, :], xl[:, c, :], K.col("ssd_norm", c), rstd[:, c // 4, :],
                                                   ALU.mult, ALU.mult)


IN2 = [("qa", 4, "Copy"), ("ka", 4, "Copy"), ("qc", 4, "Copy"), ("kd", 4, "Copy"), ("xb", 4, "Copy"), ("kc", 1, "Copy"),
       ("vc", 1, "Copy"), ("ud", 4, "Gelu"), ("ga", 4, "Silu"), ("gb", 4, "Silu"), ("gc", 4, "Silu"), ("gd", 4, "Silu"),
       ("mg", 32, "Sigmoid")]


def hybrid_layer(K, out):
    normalise_in_place(K, CTX, "final_g")
    with K.scope():
        f = {name: K.take(n, LAT) for name, n, _func in IN2}
        f["va"], f["vd"], f["vs"] = K.take(LT, BW), K.take(LT, BW), K.take(LT, 256)
        f["gate"], f["fa"] = K.take(LT, 24), K.take(LAT)
        with K.scope():
            sparse, addmask = K.take(LT, BW), K.take(2 * P)
            with K.activations(KD * LAT):
                project2(K, f, {"o": sparse, "addmask": addmask})
            with K.scope():
                branches(K, f, SideWeights(K), sparse, addmask)
        merge(K, f, out)


class SideWeights:

    def __init__(self, K):
        self.K = K
        self.rg, self.spatial, self.spatial_b, self.ln = K.take(2, KB, P), K.take(8, P), K.take(P), K.take(BW)

    def load(self, sync):
        K = self.K
        sync.dma_start(self.rg, K.dram["rg_w"]).then_inc(*K.rg_loaded.up(16))
        sync.dma_start(self.spatial, K.dram["spatial_w"]).then_inc(*K.spatial_loaded.up(16))
        sync.dma_start(self.spatial_b[0:8, :], K.dram["spatial_b"]).then_inc(*K.spatial_loaded.up(16))
        sync.dma_start(self.ln, K.dram["ln_v_g"].partition_broadcast(P)).then_inc(*K.spatial_loaded.up(16))


class Pass:

    def __init__(self, q, k, v, row_bias, gate, o, add):
        self.q, self.k, self.v, self.row_bias, self.gate, self.o, self.add = q, k, v, row_bias, gate, o, add


def branches(K, f, side, sparse, addmask):
    forgetting = K.take(LT, BW)

    def head_rows(h):
        return slice(HD * (h % 2), HD * (h % 2) + HD)

    passes = [Pass(lambda h: f["qa"][head_rows(h), h // 2, :], lambda h: f["ka"][head_rows(h), h // 2, :],
                   lambda s, h: f["va"][:, s, h * HD:h * HD + HD], f["fa"], None, forgetting, False)]
    for branch, (kt, vt) in ((1, (0, 0)), (2, (2, 128))):
        passes.append(Pass(lambda h: f["qc"][head_rows(h), h // 2, :],
                           lambda h, kt=kt: f["kd"][head_rows(h), kt + h // 4, :],
                           lambda s, h, vt=vt: f["vs"][:, s, vt + (h // 4) * HD:vt + (h // 4) * HD + HD],
                           None, lambda t, b=branch: f["gate"][:, t, NH * b:NH * b + NH], sparse, True))
    with K.scope():
        attention(K, passes, addmask, SideBranches(K, f, side))
    turn_gate(K, ((forgetting, f["ga"]), (sparse, f["gc"])))


def project2(K, f, buffers):
    first = FIRST_TILE["in2"]
    rounds, tile = [], first
    func_of = {"Copy": ACT.Copy, "Gelu": ACT.Gelu, "Silu": ACT.Silu, "Sigmoid": ACT.Sigmoid}

    def h(k):
        return K.h_parts(LAT, k)

    def token_round(name, width, func):
        groups = token_products(K, tile, LAT, range(LT), width)
        rounds.append([Item(g, lambda act, bank, i=i: act.activation(f[name][:, i, :], bank[:, 0:width], func))
                       for i, g in enumerate(groups)])

    for name, n, func in IN2:
        if name == "ud":
            token_round("va", BW, ACT.Copy)
            tile += 4 * KD
            token_round("vs", 256, ACT.Copy)
            tile += 2 * KD
            rounds.append([Item(tile_products(tile, KD, h, LAT),
                                lambda act, bank: act.activation(f["fa"][0:8, :], bank[0:8, 0:LAT], ACT.Identity,
                                                                 bias=K.col("b_forget", rows=slice(0, 8)), scale=1.0))])
            tile += KD
            token_round("gate", 24, ACT.Sigmoid)
            tile += KD
            token_round("vd", BW, ACT.Gelu)
            tile += 4 * KD
        for j in range(n):
            dest = f[name][:, j, :]
            rounds.append([Item(tile_products(tile, KD, h, LAT),
                                lambda act, bank, dest=dest, func=func: act.activation(dest, bank[:, 0:LAT], func_of[func]))])
            tile += KD
    spare = [f["mg"][:, j, :] for j in range(KD + 2)]
    n_before = sum(n for _name, n, _func in IN2[:7])
    run_products(K, rounds, prepare=Normalise(K, CTX, "norm2", None, spare), beside=SparseSteps(K, f, n_before, **buffers), banks=4)


NEG = 1e30
SIDE = 3


def attention(K, passes, addmask, beside):
    nc = K.nc
    NS, NP = 5, 3
    s = K.take(NS, LAT)
    pt = K.take(NP, LT, P)
    top = K.take(NS, 2)
    tmp = K.take(BW)
    sums = K.take(len(passes) * LT, NH)
    units = [(p, i, t, h) for i, p in enumerate(passes) for t in range(LT) for h in range(NH)]
    scored, masked, negated, exped, turned, kept, used, emptied, vector_step = K.counts(9)
    SCORE, TURN, OUT, N_SCORE, AHEAD = 0, 4, 6, SIDE, 3
    with nc.Block() as block:
        @block.sync
        def _(sync):
            beside.side.load(sync)

        @block.tensor
        def _(pe):
            def score(u):
                p, _i, t, h = units[u]
                n = (t + 1) * P
                if u >= N_SCORE:
                    pe.wait_ge(*masked.at(u - N_SCORE + 1))
                b = K.bank[:, SCORE + u % N_SCORE, 0:n]
                mm = pe.matmul(b, p.q(h)[:, t * P:t * P + P], p.k(h)[:, 0:n], start=True, stop=p.row_bias is None)
                if p.row_bias is not None:
                    mm = pe.matmul(b, K.ident[0:NH, h:h + 1].broadcast_to([NH, P]), p.row_bias[0:NH, 0:n],
                                   start=False, stop=True)
                mm.then_inc(*scored.up())

            def turn(u):
                p, i, t, h = units[u]
                pe.wait_ge(*exped.at(u + 1))
                if u >= 2:
                    pe.wait_ge(*kept.at(u - 1))
                for c in range(t + 1):
                    mm = pe.transpose(K.bank[:, TURN + u % 2, c * P:c * P + P], s[:, u % NS, c * P:c * P + P], K.ident[:])
                mm.then_inc(*turned.up())

            def weigh(u):
                p, i, t, h = units[u]
                pe.wait_ge(*kept.at(u + 1))
                if h == 0 and i:
                    pe.wait_ge(*emptied.at(2 * i - 1 + t))
                for c in range(t + 1):
                    mm = pe.matmul(K.bank[:, OUT + t, h * HD:h * HD + HD], pt[:, u % NP, c, :], p.v(c, h),
                                   start=(c == 0), stop=(c == t))
                mm.then_inc(*used.up())

            n = len(units)
            for u in range(n + AHEAD + 1):
                if u < n:
                    score(u)
                if AHEAD <= u < n + AHEAD:
                    turn(u - AHEAD)
                if u > AHEAD:
                    weigh(u - AHEAD - 1)
                beside.tensor(pe, u)

        @block.vector
        def _(dve):
            link = Link(dve, vector_step)

            def finish(group):
                p, _i, t, _h = units[NH * group]
                dve.wait_ge(*used.at(NH * group + NH))
                total = sums[:, group, :]
                link(dve.reciprocal(total, total))
                if p.gate is not None:
                    link(dve.tensor_tensor(total, total, p.gate(t), ALU.mult))
                dest = tmp if p.add else p.o[:, t, :]
                dve.tensor_tensor(dest.rearrange("p (h v) -> p h v", v=HD),
                                  K.bank[:, OUT + t, :].rearrange("p (h v) -> p h v", v=HD),
                                  last(total, HD), ALU.mult).then_inc(*emptied.up())
                if p.add:
                    dve.wait_ge(*emptied.now())
                    link(dve.tensor_tensor(p.o[:, t, :], p.o[:, t, :], tmp, ALU.add))

            for u, (p, i, t, h) in enumerate(units):
                n = (t + 1) * P
                w = s[:, u % NS, 0:n]
                dve.wait_ge(*scored.at(u + 1))
                if u >= NS:
                    dve.wait_ge(*turned.at(u - NS + 1))
                dve.scalar_tensor_tensor(w, K.bank[:, SCORE + u % N_SCORE, 0:n], HD ** -0.5, addmask[:, 2 * P - n:2 * P],
                                         ALU.mult, ALU.add).then_inc(*masked.up())
                dve.wait_ge(*masked.now())
                m = top[:, u % NS, :]
                link(dve.reduce_max(m[:, 0:1], w, AX.X))
                dve.tensor_scalar(m[:, 1:2], m[:, 0:1], -1.0, None, ALU.mult).then_inc(*negated.up())
                if u % NH == AHEAD + 2 and u > NH:
                    finish(u // NH - 1)
                beside.vector(dve, u)
            finish(len(units) // NH - 1)

        @block.scalar
        def _(act):
            n = len(units)

            def keep(u):
                p, i, t, h = units[u]
                act.wait_ge(*turned.at(u + 1))
                if u >= NP:
                    act.wait_ge(*used.at(u - NP + 1))
                act.activation(pt[:, u % NP, 0:t + 1, :].rearrange("p c t -> p (c t)"),
                               K.bank[:, TURN + u % 2, 0:(t + 1) * P], ACT.Copy).then_inc(*kept.up())
            for u, (p, i, t, h) in enumerate(units):
                act.wait_ge(*negated.at(u + 1))
                w = s[:, u % NS, 0:(t + 1) * P]
                act.activation(w, w, ACT.Exp, bias=top[:, u % NS, 1:2], scale=1.0,
                               accum_out=sums[:, u // NH, h:h + 1]).then_inc(*exped.up())
                if u:
                    keep(u - 1)
                beside.scalar(act, u)
            keep(n - 1)
    K.stage_end()


def turn_gate(K, pairs):
    nc = K.nc
    (turned,) = K.counts(1)
    with nc.Block() as block:
        @block.tensor
        def _(pe):
            for i, (o, _gate) in enumerate(pairs):
                for j in range(KB):
                    for t in range(LT):
                        mm = pe.transpose(K.bank[:, KB * i + j, t * P:t * P + P], o[:, t, j * P:j * P + P], K.ident[:])
                    mm.then_inc(*turned.up())

        @block.vector
        def _(dve):
            for i, (_o, gate) in enumerate(pairs):
                for j in range(KB):
                    dve.wait_ge(*turned.at(KB * i + j + 1))
                    dve.tensor_tensor(gate[:, j, :], gate[:, j, :], K.bank[:, KB * i + j, 0:LAT], ALU.mult)
    K.stage_end()


class SparseSteps:
    SLOT = 32
    SETS = (("qa", "qn_a"), ("ka", "kn_a"), ("qc", "qn_c"), ("kd", "kn_c"))
    SQUARE, SUM, ROOT, SCALE, SPACING = -17, -15, -13, -11, 4
    SWAP, OWN, SWAPPED = 0, 1, 4
    FORGET, FORGET_SUM = 6, 8
    HIDDEN, SILU, TURN_HIDDEN, KEEP_HIDDEN = (8, 10), 14, 16, 18
    KEYS, KEY_SQUARE, KEY_SUM, KEY_ROOT, KEY_SCALE, VALUES = 20, 22, 24, 26, 28, 29
    SCORES, SHIFT, EXP, WEIGH, TURN, KEEP, PRODUCT, FINISH = 31, 33, 35, 37, 39, 41, 43, 45

    def __init__(self, K, f, begin, o, addmask):
        self.K, self.f, self.begin, self.o, self.addmask = K, f, begin, o, addmask
        S = self.SLOT
        self.sq, self.rt = f["mg"][:, 28:32, :], f["mg"][:, 24:28, :]
        self.head_ones = K.take(P)
        self.w1, self.w2 = K.take(2, CB // 2, P), K.take(2, P)
        self.tb, self.swapped = K.take(2, CB // 2, 2, NC), K.take(2, LAT)
        self.hid_t, self.hid, self.sums = K.take(2, P), K.take(4, NC), K.take(LT, NH)
        self.kn, self.krt, self.ksq = K.take(2, NC), K.take(2, NC), K.take(2, NC)
        self.vblk = K.take(2, 4, HD)
        self.mask, self.neg = K.take(LT, NC), K.take(LT, NC)
        self.prob, self.peak = K.take(LT, NH, S), K.take(LT, NH)
        self.live = self.prob[:, :, :, 0:NC]
        self.turned_p = K.take(LT, 2, P)
        self.e, self.one = K.take(LAT)[0:8, :], K.take(LAT)[0:8, :]
        (self.heads, self.masked, self.squared, self.summed, self.rooted, self.scaled, self.swaps, self.posed,
         self.logged, self.hidden, self.silued, self.keyed, self.key_squared, self.key_summed, self.key_rooted,
         self.normed) = K.counts(16)
        (self.valued, self.placed, self.scored, self.shifted, self.exped, self.ready, self.turned, self.kept, self.made,
         self.vector_step, self.scalar_step, self.pool_step, self.hid_turned, self.hid_kept) = K.counts(14)

    def sync(self, sync):
        K = self.K
        sync.dma_start(self.w1, K.dram["cmp_w1"]).then_inc(*K.cmp_loaded.up(16))
        sync.dma_start(self.w2, K.dram["cmp_w2"]).then_inc(*K.cmp_loaded.up(16))

    def gpsimd(self, pool):
        link = Link(pool, self.pool_step)
        link(pool.memset(self.head_ones, 0.0))
        for r in (slice(0, HD), slice(HD, P)):
            pool.memset(self.head_ones[r, r], 1.0).then_inc(*self.heads.up())
            pool.wait_ge(*self.heads.now())
        link(pool.memset(self.vblk, 0.0))
        link(pool.memset(self.prob, 0.0))
        link(pool.memset(self.mask, 1.0))
        for t in range(LT):
            pool.affine_select(out=self.mask[:, t, :], in_=self.mask[:, t, :], compare_op=ALU.is_ge, fill=0.0,
                               base=t * P - (CB - 1), pattern=[[-CS, NC]], channel_multiplier=1).then_inc(*self.masked.up())
            pool.wait_ge(*self.masked.now())

    def set_at(self, u, slot):
        i, rest = divmod(u - slot, self.SPACING)
        return i if 0 <= i < len(self.SETS) and not rest else None

    def tensor(self, pe, item):
        K, f, S, u = self.K, self.f, self.SLOT, item - self.begin
        i = self.set_at(u, self.SUM)
        if i is not None:
            if i == 0:
                pe.wait_ge(*self.heads.at(2))
            pe.wait_ge(*self.squared.at(i + 1))
            if i >= 2:
                pe.wait_ge(*self.rooted.at(i - 1))
            for half in range(2):
                mm = pe.matmul(K.bank[:, 4 + 2 * (i % 2) + half, :], self.head_ones,
                               self.sq[:, 2 * half:2 * half + 2, :].rearrange("p a t -> p (a t)"), start=True, stop=True)
            mm.then_inc(*self.summed.up())
        if u in self.HIDDEN:
            i = self.HIDDEN.index(u)
            pe.wait_ge(*K.cmp_loaded.now())
            pe.wait_ge(*self.posed.at(16))
            pe.wait_ge(*self.rooted.at(len(self.SETS)))
            for c in range(CB // 2):
                mm = pe.matmul(K.bank[0:2 * NC, 4 + i, 0:P], self.tb[:, i, c, :, :].rearrange("p g n -> p (g n)"),
                               self.w1[:, i, c, :], start=(c == 0), stop=(c == CB // 2 - 1))
            mm.then_inc(*self.hidden.up())
        if u == self.TURN_HIDDEN:
            pe.wait_ge(*self.silued.at(2))
            for i in range(2):
                mm = pe.transpose(K.bank[:, 6, 2 * i * NC:2 * i * NC + 2 * NC], self.hid_t[0:2 * NC, i, :],
                                  K.ident[0:2 * NC, 0:2 * NC])
            mm.then_inc(*self.hid_turned.up())
        if u == self.KEYS:
            pe.wait_ge(*self.hid_kept.at(1))
            for g in range(2):
                mm = pe.matmul(K.bank[:, 5, g * NC:g * NC + NC], self.w2[:, 0, :], self.hid[:, g, :], start=True, stop=True)
            mm.then_inc(*self.keyed.up())
            for g in range(2):
                for j in range(4):
                    mm = pe.matmul(K.bank[S * j:S * j + NC, 7, g * HD:g * HD + HD], self.hid[:, 2 + g, :],
                                   self.w2[:, 1, 0:HD], start=True, stop=True)
            mm.then_inc(*self.valued.up())
        if u == self.KEY_SUM:
            pe.wait_ge(*self.key_squared.at(1))
            pe.matmul(K.bank[:, 6, 0:2 * NC], self.head_ones, self.ksq.rearrange("p g c -> p (g c)"), start=True,
                      stop=True).then_inc(*self.key_summed.up())
        if u == self.SCORES:
            pe.wait_ge(*self.normed.at(1))
            pe.wait_ge(*self.placed.at(1))
            for t in range(LT):
                for h in range(NH):
                    r = slice(HD * (h % 2), HD * (h % 2) + HD)
                    mm = pe.matmul(K.bank[:, 4 + 2 * t + h % 2, (h // 2) * S:(h // 2) * S + NC],
                                   f["qc"][r, h // 2, t * P:t * P + P], self.kn[r, h // 4, :], start=True, stop=True)
            mm.then_inc(*self.scored.up())
        if u == self.TURN:
            pe.wait_ge(*self.ready.at(LT))
            for t in range(LT):
                for g in range(2):
                    mm = pe.transpose(K.bank[:, 4 + t, g * P:g * P + P],
                                      self.prob[:, t, 4 * g:4 * g + 4, :].rearrange("p h s -> p (h s)"), K.ident[:])
            mm.then_inc(*self.turned.up())
        if u == self.PRODUCT:
            pe.wait_ge(*self.kept.at(1))
            for t in range(LT):
                for g in range(2):
                    mm = pe.matmul(K.bank[:, 6 + t, g * 256:g * 256 + 256], self.turned_p[:, t, g, :],
                                   self.vblk[:, g, :, :].rearrange("p j v -> p (j v)"), start=True, stop=True)
            mm.then_inc(*self.made.up())

    def scalar(self, act, item, emptied):
        K, f, u = self.K, self.f, item - self.begin
        i = self.set_at(u, self.SQUARE)
        if i is not None:
            act.wait_ge(*emptied)
            if i:
                act.wait_ge(*self.summed.at(i))
            act.activation(self.sq, f[self.SETS[i][0]], ACT.Square).then_inc(*self.squared.up())
        i = self.set_at(u, self.ROOT)
        if i is not None:
            act.wait_ge(*self.summed.at(i + 1))
            if i:
                act.wait_ge(*self.scaled.at(i))
            b = 4 + 2 * (i % 2)
            rt = self.rt.rearrange("p (b a) t -> p b (a t)", a=2)
            rsqrt(act, Link(act, self.scalar_step), rt, K.bank[:, b:b + 2, :], K.small[:, 0:1], 1.0 / HD).then_inc(
                *self.rooted.up())
        if u == self.SWAP:
            for i, name in enumerate(("kc", "vc")):
                for half in range(2):
                    act.dma_start(self.swapped[HD * half:HD * half + HD, i, :],
                                  f[name][HD - HD * half:P - HD * half, 0, :]).then_inc(*self.swaps.up(16))
        if u == self.FORGET:
            act.wait_ge(*emptied)
            link, e = Link(act, self.scalar_step), self.e
            link(act.activation(e, f["fa"][0:8, :], ACT.Abs))
            link(act.activation(e, e, ACT.Exp, scale=-1.0))
            act.activation(e, e, ACT.Ln, bias=K.small[0:8, 1:2], scale=1.0).then_inc(*self.logged.up())
        if u == self.SILU:
            for i in range(2):
                act.wait_ge(*self.hidden.at(i + 1))
                act.activation(self.hid_t[0:2 * NC, i, :], K.bank[0:2 * NC, 4 + i, 0:P], ACT.Silu).then_inc(
                    *self.silued.up())
        if u == self.KEEP_HIDDEN:
            act.wait_ge(*self.hid_turned.at(1))
            act.activation(self.hid.rearrange("p g c -> p (g c)"), K.bank[:, 6, 0:4 * NC], ACT.Copy).then_inc(
                *self.hid_kept.up())
        if u == self.KEY_SQUARE:
            act.wait_ge(*self.keyed.at(1))
            act.activation(self.ksq.rearrange("p g c -> p (g c)"), K.bank[:, 5, 0:2 * NC], ACT.Square).then_inc(
                *self.key_squared.up())
        if u == self.KEY_ROOT:
            act.wait_ge(*self.key_summed.at(1))
            act.activation(self.krt.rearrange("p g c -> p (g c)"), K.bank[:, 6, 0:2 * NC], ACT.Sqrt,
                           bias=K.small[:, 0:1], scale=1.0 / HD).then_inc(*self.key_rooted.up())
        if u == self.EXP:
            act.wait_ge(*self.shifted.at(LT))
            for t in range(LT):
                act.activation(self.live[:, t, :, :], self.live[:, t, :, :], ACT.Exp).then_inc(*self.exped.up())
        if u == self.KEEP:
            act.wait_ge(*self.turned.at(1))
            for t in range(LT):
                ins = act.activation(self.turned_p[:, t, :, :].rearrange("p g t -> p (g t)"), K.bank[:, 4 + t, 0:2 * P],
                                     ACT.Copy)
            ins.then_inc(*self.kept.up())

    def pose(self, dve, own):
        K, f = self.K, self.f
        for i, name in enumerate(("kc", "vc")):
            for odd in range(2):
                r, g = slice(HD * odd, HD * odd + HD), odd if own else 1 - odd
                src = (f[name][r, 0, :] if own else self.swapped[r, i, :]).rearrange("p (n b e) -> p b e n", e=2, b=CS // 2)
                pos = K.col("cmp_pos", 0, CB, r).rearrange("p (b e) -> p b e", e=2)
                for a in range(2):
                    half = slice(a * CS // 2, a * CS // 2 + CS // 2)
                    dve.tensor_tensor(self.tb[r, i, half, g, :], src[:, :, odd, a:a + NC], last(pos[:, half, odd], NC),
                                      ALU.add).then_inc(*self.posed.up())

    def vector(self, dve, item, emptied):
        K, f, S, u = self.K, self.f, self.SLOT, item - self.begin
        link = Link(dve, self.vector_step)
        live, sums, peak = self.live, self.sums, self.peak
        i = self.set_at(u, self.SCALE)
        if i is not None:
            name, gain = self.SETS[i]
            dve.wait_ge(*self.rooted.at(i + 1))
            dve.scalar_tensor_tensor(f[name], f[name], K.col(gain), self.rt, ALU.mult, ALU.mult).then_inc(*self.scaled.up())
        if u == self.OWN:
            dve.wait_ge(*emptied)
            self.pose(dve, True)
        if u == self.SWAPPED:
            dve.wait_ge(*self.swaps.at(64))
            self.pose(dve, False)
        if u == self.FORGET_SUM:
            z, e, one = f["fa"][0:8, :], self.e, self.one
            link(dve.memset(one, 1.0))
            dve.wait_ge(*self.logged.at(1))
            link(dve.scalar_tensor_tensor(e, z, 0.0, e, ALU.min, ALU.subtract))
            link(dve.tensor_tensor_scan(z, one, e, 0.0, ALU.mult, ALU.add))
            dve.tensor_scalar(z, z, -float(HD) ** 0.5, None, ALU.mult)
            dve.memset(self.addmask[:, 0:P], 0.0)
            dve.tensor_scalar(self.addmask[:, P:2 * P], K.tri_b[:], 1.0, NEG, ALU.subtract, ALU.mult)
        if u == self.KEY_SCALE:
            dve.wait_ge(*self.masked.at(LT))
            dve.tensor_scalar(self.neg, self.mask, 1.0, NEG, ALU.subtract, ALU.mult)
            dve.wait_ge(*self.key_rooted.at(1))
            link(dve.reciprocal(self.krt, self.krt))
            dve.scalar_tensor_tensor(self.kn, K.bank[:, 5, 0:2 * NC].rearrange("p (g c) -> p g c", c=NC), K.col("kn_c"),
                                     self.krt, ALU.mult, ALU.mult).then_inc(*self.normed.up())
        if u == self.VALUES:
            dve.wait_ge(*self.valued.at(1))
            for g in range(2):
                for j in range(4):
                    r = slice(S * j, S * j + NC)
                    ins = dve.tensor_copy(self.vblk[r, g, j, :], K.bank[r, 7, g * HD:g * HD + HD])
            ins.then_inc(*self.placed.up())
        if u == self.SHIFT:
            dve.wait_ge(*self.scored.at(1))
            dve.wait_ge(*self.placed.at(1))
            for t in range(LT):
                for e in range(2):
                    sv = K.bank[:, 4 + 2 * t + e, 0:4 * S].rearrange("p (h s) -> p h s", s=S)[:, :, 0:NC]
                    link(dve.scalar_tensor_tensor(live[:, t, e:NH:2, :], sv, HD ** -0.5, mid(self.neg[:, t, :], 4), ALU.mult,
                                                  ALU.add))
                link(dve.tensor_reduce(peak[:, t, :], live[:, t, :, :], AX.X, ALU.max))
                dve.tensor_tensor(live[:, t, :, :], live[:, t, :, :], last(peak[:, t, :], NC),
                                  ALU.subtract).then_inc(*self.shifted.up())
        if u == self.WEIGH:
            for t in range(LT):
                dve.wait_ge(*self.exped.at(t + 1))
                link(dve.tensor_reduce(sums[:, t, :], live[:, t, :, :], AX.X, ALU.add))
                dve.tensor_tensor(live[:, t, :, :], live[:, t, :, :], mid(self.mask[:, t, :], NH), ALU.mult).then_inc(
                    *self.ready.up())
        if u == self.FINISH:
            dve.wait_ge(*self.made.at(1))
            dve.wait_ge(*emptied)
            for t in range(LT):
                link(dve.reciprocal(sums[:, t, :], sums[:, t, :]))
                link(dve.tensor_tensor(sums[:, t, :], sums[:, t, :], f["gate"][:, t, 0:NH], ALU.mult))
                dve.tensor_tensor(self.o[:, t, :].rearrange("p (h v) -> p h v", v=HD),
                                  K.bank[:, 6 + t, :].rearrange("p (h v) -> p h v", v=HD),
                                  last(sums[:, t, :], HD), ALU.mult)


class SideBranches:
    W = 4
    CONV, GATES, SPACING = 1, 4, 4
    SOFTPLUS, CENTRE, SQUARE, MASK, NORM = 5, 6, 8, 10, 11
    DECAYS, EXPS, SQUARES, ROOT, INPUT, SCAN, OUTPUT = 17, 18, 20, 21, 23, 24, 28
    MIX, TAKE, MIX_SPACING = 20, 21, 3

    def __init__(self, K, f, side):
        self.K, self.f, self.side = K, f, side
        self.xc, self.r, self.ig, self.a, self.m = (K.take(KB, LAT) for _ in range(5))
        self.sp, self.mean, self.var, self.squares = K.take(5, KB), K.take(LT), K.take(LT), K.take(LT, BW)
        (self.centred, self.conved, self.gated, self.sigmoided, self.absed, self.decays, self.exped, self.tanhed,
         self.scaled, self.rooted) = K.counts(10)
        self.middled, self.squared, self.deviated, self.normed, self.mixed, self.taken = K.counts(6)
        self.vector_step, self.scalar_step = K.counts(2)

    def tensor(self, pe, u):
        K, f = self.K, self.f
        j, rest = divmod(u - self.GATES, self.SPACING)
        if 0 <= j < KB and not rest:
            pe.wait_ge(*K.rg_loaded.now())
            pe.wait_ge(*self.conved.at(j + 1))
            if j:
                pe.wait_ge(*self.sigmoided.at(j))
            for gate in range(2):
                mm = pe.matmul(K.bank[:, SIDE, gate * LAT:gate * LAT + LAT], self.side.rg[:, gate, j, :], self.xc[:, j, :],
                               start=True, stop=True)
            mm.then_inc(*self.gated.up())
        j, rest = divmod(u - self.MIX, self.MIX_SPACING)
        if 0 <= j < KB and not rest:
            if j:
                pe.wait_ge(*self.taken.at(j))
            else:
                pe.wait_ge(*self.sigmoided.at(KB))
                pe.wait_ge(*self.normed.at(LT))
            for c in range(LT):
                for e in range(2):
                    g = 2 * j + e
                    b = K.bank[HD * e:HD * e + HD, SIDE, c * P:c * P + P]
                    pe.matmul(b, f["vd"][:, c, g * HD:g * HD + HD], self.side.spatial[:, g, :], start=True, stop=False)
                    mm = pe.matmul(b, K.ident[0:8, g:g + 1].broadcast_to([8, HD]), self.side.spatial_b[0:8, :], start=False,
                                   stop=True)
            mm.then_inc(*self.mixed.up())

    def scalar(self, act, u):
        K, f = self.K, self.f
        link = Link(act, self.scalar_step)
        if u == 0:
            for j in range(KB):
                act.activation(self.xc[:, j, :], f["xb"][:, j, :], ACT.Identity, bias=K.col("lru_conv_b", j),
                               scale=K.col("lru_conv_w", (self.W - 1) * KB + j)).then_inc(*self.centred.up())
            link(act.activation(self.sp[:, 0, :], K.col("lam", 0, KB), ACT.Abs))
            act.activation(self.sp[:, 0, :], self.sp[:, 0, :], ACT.Exp, scale=-1.0).then_inc(*self.absed.up())
        j, rest = divmod(u - self.GATES, self.SPACING)
        if 0 <= j < KB and not rest:
            act.wait_ge(*self.gated.at(j + 1))
            act.activation(self.r[:, j, :], K.bank[:, SIDE, 0:LAT], ACT.Sigmoid, bias=K.col("b_rg_a", j), scale=1.0)
            act.activation(self.ig[:, j, :], K.bank[:, SIDE, LAT:2 * LAT], ACT.Sigmoid, bias=K.col("b_rg_x", j),
                           scale=1.0).then_inc(*self.sigmoided.up())
        if u == self.EXPS:
            act.wait_ge(*self.decays.at(1))
            act.activation(self.a, self.r, ACT.Exp, scale=-1.0).then_inc(*self.exped.up())
            act.activation(self.m, self.r, ACT.Tanh).then_inc(*self.tanhed.up())
        if u == self.ROOT:
            act.wait_ge(*self.scaled.at(1))
            act.activation(self.m, self.m, ACT.Sqrt).then_inc(*self.rooted.up())
        if u == self.SQUARE:
            for t in range(LT):
                act.wait_ge(*self.middled.at(t + 1))
                act.activation(self.squares[:, t, :], f["vd"][:, t, :], ACT.Square,
                               accum_out=self.var[:, t:t + 1]).then_inc(*self.squared.up())
            act.wait_ge(*self.squared.at(LT))
            act.activation(self.var, self.var, ACT.Sqrt, bias=K.small[:, 0:1], scale=1.0 / BW).then_inc(*self.deviated.up())

    def vector(self, dve, u):
        K, f = self.K, self.f
        link = Link(dve, self.vector_step)
        xc, r, ig, a, m, sp = self.xc, self.r, self.ig, self.a, self.m, self.sp
        j = u - self.CONV
        if 0 <= j < KB:
            dve.wait_ge(*self.centred.at(j + 1))
            for tap in range(self.W - 1):
                s = self.W - 1 - tap
                ins = dve.scalar_tensor_tensor(xc[:, j, s:LAT], f["xb"][:, j, 0:LAT - s],
                                               K.col("lru_conv_w", tap * KB + j), xc[:, j, s:LAT], ALU.mult, ALU.add)
                if tap == self.W - 2:
                    ins.then_inc(*self.conved.up())
                else:
                    link(ins)
        if u == self.SOFTPLUS:
            dve.wait_ge(*self.absed.at(1))
            log1p_small(link, dve, sp[:, 0, :], sp[:, 1, :], sp[:, 2, :], sp[:, 3, :])
            link(dve.tensor_scalar(sp[:, 4, :], K.col("lam", 0, KB), -1.0, 0.0, ALU.mult, ALU.max))
            link(dve.tensor_tensor(sp[:, 0, :], sp[:, 0, :], sp[:, 4, :], ALU.add))
        if u == self.DECAYS:
            dve.wait_ge(*self.sigmoided.at(KB))
            for j in range(KB):
                ins = dve.tensor_scalar(r[:, j, :], r[:, j, :], sp[:, 0, j:j + 1], 8.0, ALU.mult, ALU.mult)
            ins.then_inc(*self.decays.up())
            link(dve.tensor_tensor(ig, ig, xc, ALU.mult))
        if u == self.SQUARES:
            dve.wait_ge(*self.tanhed.at(1))
            link(dve.tensor_tensor(xc, a, a, ALU.mult))
            dve.scalar_tensor_tensor(m, xc, 1.0, m, ALU.add, ALU.mult).then_inc(*self.scaled.up())
        if u == self.INPUT:
            dve.wait_ge(*self.rooted.at(1))
            link(dve.tensor_tensor(m, m, ig, ALU.mult))
        j = u - self.SCAN
        if 0 <= j < KB:
            link(dve.tensor_tensor_scan(xc[:, j, :], a[:, j, :], m[:, j, :], 0.0, ALU.mult, ALU.add))
        if u == self.OUTPUT:
            dve.tensor_tensor(f["gb"], f["gb"], xc, ALU.mult)

        t = u - self.CENTRE
        if 0 <= t < LT:
            link(dve.reduce_sum(self.mean[:, t:t + 1], f["vd"][:, t, :], AX.X))
            link(dve.tensor_scalar(self.mean[:, t:t + 1], self.mean[:, t:t + 1], 1.0 / BW, None, ALU.mult))
            dve.tensor_scalar(f["vd"][:, t, :], f["vd"][:, t, :], self.mean[:, t:t + 1], None,
                              ALU.subtract).then_inc(*self.middled.up())
        if u == self.MASK:
            dve.wait_ge(*K.spatial_loaded.now())
            link(dve.tensor_tensor(self.side.spatial, self.side.spatial, mid(K.tri_f[:], 8), ALU.mult))
        if u == self.NORM:
            dve.wait_ge(*self.deviated.at(1))
            link(dve.reciprocal(self.var, self.var))
            for t in range(LT):
                dve.scalar_tensor_tensor(f["vd"][:, t, :], f["vd"][:, t, :], self.var[:, t:t + 1], self.side.ln, ALU.mult,
                                         ALU.mult).then_inc(*self.normed.up())
        j, rest = divmod(u - self.TAKE, self.MIX_SPACING)
        if 0 <= j < KB and not rest:
            dve.wait_ge(*self.mixed.at(j + 1))
            dve.tensor_tensor(f["ud"][:, j, :], f["ud"][:, j, :], K.bank[:, SIDE, 0:LAT], ALU.mult).then_inc(*self.taken.up())
            dve.wait_ge(*self.taken.now())
            dve.tensor_tensor(f["gd"][:, j, :], f["gd"][:, j, :], f["ud"][:, j, :], ALU.mult)


def merge(K, f, out):
    nc = K.nc
    branches = ("ga", "gb", "gc", "gd")
    with K.activations(4 * KB * LAT):
        parts = Split(K, [(f[name][:, j, :], *K.h_parts(LAT, 4 * b + j))
                          for b, name in enumerate(branches) for j in range(KB)])
        tmp, total = K.take(LAT), K.take(LAT)
        merged_hi, merged_lo = K.take(KD, LAT, dtype=F32R), K.take(KD, LAT, dtype=F32R)
        first = FIRST_TILE["branch2"]
        rounds = []
        for n in range(KD):
            for b in range(4):
                def empty(dve, link, bank, n=n, b=b):
                    if b == 0:
                        return dve.tensor_tensor(total, bank[:, 0:LAT], f["mg"][:, b * KD + n, :], ALU.mult)
                    link(dve.tensor_tensor(tmp, bank[:, 0:LAT], f["mg"][:, b * KD + n, :], ALU.mult))
                    ins = dve.tensor_tensor(total, total, tmp, ALU.add)
                    if b == 3:
                        link(ins)
                        link(dve.tensor_copy(merged_hi[:, n, :], total))
                        ins = dve.tensor_tensor(merged_lo[:, n, :], total, merged_hi[:, n, :].bitcast(F32), ALU.subtract)
                    return ins
                rounds.append([Item(tile_products(first + (n * 4 + b) * KB, KB,
                                                  lambda k, b=b: K.h_parts(LAT, 4 * b + k), LAT), empty, "dve")])
        run_products(K, rounds, prepare=parts)
        run_products(K, residual_items(K, "out2", KD, lambda k: (merged_hi[:, k, :], merged_lo[:, k, :]), CTX, None))
    (stored,) = K.counts(1)
    with nc.Block() as block:
        @block.sync
        def _(sync):
            sync.dma_start(out, K.x[:, :, CTX:T]).then_inc(*stored.up(16))
            sync.wait_ge(*stored.at(16))
    K.stage_end()


def build(nc, dram, out):
    with ExitStack() as ctx:
        K = Kit(nc, ctx, dram)
        with K.scope():
            features = even_features(K)
            a2 = K.take(256)
            with K.activations(KD * T):
                modulator = Modulator(K, K.take(2, D))
                with K.scope():
                    setup(K, modulator, features[0], a2)
                even_projection(K, features[0], modulator)
            even_mixer(K, features, a2)
        feed_forward(K, 0, 0, blocks_of("mod1")[MOD_EVEN:])
        odd_mixer(K)
        feed_forward(K, 1, CTX)
        hybrid_layer(K, out)


def feature_columns(a):
    return a.reshape(-1, P).T


def feature_tiles(w):
    k, n = w.shape
    return w.reshape(k // P, P, n // P, P).transpose(2, 0, 1, 3).reshape(-1, P, P)


def token_tiles(w):
    k, n = w.shape
    return w.reshape(k // P, P, n // P, P).transpose(0, 2, 1, 3).reshape(-1, P, P)


def widened(w):
    return np.concatenate([w, np.zeros((w.shape[0], P - w.shape[1]), w.dtype)], axis=1)


def rows_to_partitions(w):
    return w.reshape(-1, P, w.shape[1]).transpose(1, 0, 2)


def lay_out(v):
    f32 = np.float32
    parts = {}
    for l in range(2):
        parts[f"mod{l}"] = [v["mod_w"][l].reshape(KD, P, 48, P).transpose(2, 0, 3, 1).reshape(-1, P, P)]
        up = v["ffn_w_up"][l]
        pair = np.concatenate([up[:, :FF].reshape(D, KF, 1, P), up[:, FF:].reshape(D, KF, 1, P)], axis=2)
        parts[f"up{l}"] = [feature_tiles(pair.reshape(D, 2 * FF))]
        parts[f"down{l}"] = [feature_tiles(v["ffn_w_down"][l])]
    w = v["even_w_in"][0]
    gq, gk, gv, gg, mq, mk, mv, mo, mg = np.split(w, np.cumsum([256, 256, 512, 512, 512, 512, 512, 512]), axis=1)
    small = np.zeros((D, 3, P), f32)
    small[:, 0, 0:16], small[:, 0, 32:48] = v["gla_a1"][0, 0], v["gla_a1"][0, 1]
    small[:, 1, 0:4], small[:, 1, 32:36] = mg[:, 0:4], mg[:, 8:12]
    small[:, 2, 0:4], small[:, 2, 32:36] = mg[:, 4:8], mg[:, 12:16]
    parts["even_in"] = [feature_tiles(x) for x in (gq, gk, gg, mq, mk)] + [token_tiles(x) for x in (gv, mv, mo)] + \
                       [feature_tiles(small.reshape(D, 3 * P))]
    parts["even_out"] = [feature_tiles(v["even_w_out"][0])]
    a2 = np.zeros((48, 256), f32)
    a2[0:16], a2[32:48] = v["gla_a2"][0, 0], v["gla_a2"][0, 1]

    w = v["ssd_w_in"][0]
    parts["ssd_in"] = [feature_tiles(w[:, SI:SI + 3072]), feature_tiles(widened(w[:, SI + 3072:])), feature_tiles(w[:, 0:SI])]
    parts["ssd_out"] = [feature_tiles(v["ssd_w_out"][0])]

    w = v["w_in_2"][0]
    names = ["qa", "ka", "va", "fa", "ga", "xb", "gb", "qc", "kc", "vc", "ks", "vs", "kw", "vw", "gate", "gc", "ud", "vd",
             "gd", "mg"]
    sizes = [BW, BW, BW, NH, BW, BW, BW, BW] + [128] * 6 + [24] + [BW] * 4 + [4096]
    z = dict(zip(names, np.split(w, np.cumsum(sizes)[:-1], axis=1)))
    z["kd"] = np.concatenate([z[n][:, g * HD:g * HD + HD] for n in ("ks", "kw") for g in (0, 0, 1, 1)], axis=1)
    parts["in2"] = []
    for name, n, _func in IN2:
        if name == "ud":
            parts["in2"] += [token_tiles(z["va"]), token_tiles(np.concatenate([z["vs"], z["vw"]], axis=1)),
                             feature_tiles(widened(z["fa"])), token_tiles(widened(z["gate"])), token_tiles(z["vd"])]
        parts["in2"].append(feature_tiles(z[name]))
    wb = v["w_branch_2"][0].reshape(4, KB, P, KD, P).transpose(3, 0, 1, 2, 4)
    parts["branch2"] = [wb.reshape(-1, P, P)]
    parts["out2"] = [feature_tiles(v["w_out_2"][0])]
    tiles = np.concatenate([t for name, _n in SEGMENTS for t in parts[name]], axis=0)
    weights = tiles.reshape(N_BLOCKS, TPB, P, P)[STREAM].transpose(0, 2, 1, 3).reshape(N_BLOCKS, P, TPB * P)

    cols = np.zeros((P, N_COLS), f32)

    def put(name, a):
        a = np.asarray(a)
        cols[0:a.shape[0], COL[name]:COL[name] + a.shape[1]] = a

    def taps(w):
        return np.concatenate([feature_columns(t) for t in w], axis=1)

    for l in range(2):
        put(f"mod_b{l}", feature_columns(v["mod_b"][l]))
        put(f"mix_g{l}", feature_columns(v["norm_mix_g"][l]))
        put(f"ffn_g{l}", feature_columns(v["norm_ffn_g"][l]))
        put(f"conv_w{l}", taps(v["ffn_conv_w"][l].reshape(9, 2 * FF)))
        put(f"conv_b{l}", feature_columns(v["ffn_conv_b"][l]))
    put("final_g", feature_columns(v["final_norm_g"]))
    put("gla_ab", feature_columns(v["gla_ab"][0].reshape(-1)))
    put("ml_conv_w", taps(v["ml_conv_w"][0]))
    put("ml_conv_b", feature_columns(v["ml_conv_b"][0]))
    put("gla_norm", feature_columns(v["gla_norm_g"][0]))
    put("ml_norm", feature_columns(v["ml_norm_g"][0]))
    gb = v["ml_gate_b"][0]
    for name, a in (("ml_li_b", 0), ("ml_lf_b", 4)):
        cols[0:4, COL[name]], cols[32:36, COL[name]] = gb[a:a + 4], gb[8 + a:12 + a]
    put("ssd_conv_w", taps(v["ssd_conv_w"][0]))
    put("ssd_conv_b", feature_columns(v["ssd_conv_b"][0]))
    put("ssd_d", feature_columns(np.repeat(v["ssd_d"][0], SP)))
    put("ssd_norm", feature_columns(v["ssd_norm_g"][0]))
    put("ssd_dt_b", v["ssd_dt_bias"][0].reshape(64, 1))
    put("ssd_a_log", v["ssd_a_log"][0].reshape(64, 1))
    put("norm2", feature_columns(v["norm_g_2"][0]))
    for name in ("qn_a", "kn_a", "qn_c", "kn_c"):
        put(name, np.tile(v[name + "_2"][0], 2).reshape(P, 1))
    put("b_forget", v["b_forget_2"][0].reshape(NH, 1))
    put("lru_conv_w", taps(v["conv_w_2"][0]))
    put("lru_conv_b", feature_columns(v["conv_b_2"][0]))
    put("b_rg_a", feature_columns(v["b_rg_a_2"][0]))
    put("b_rg_x", feature_columns(v["b_rg_x_2"][0]))
    put("lam", feature_columns(v["lru_lambda_2"][0]))
    put("cmp_pos", np.tile(v["cmp_pos_2"][0].T, (2, 1)))

    tokens = np.concatenate([v["ctx"][0], v["x"][0]], axis=0)
    w1 = np.stack([v["cmp_k_w1_2"][0], v["cmp_v_w1_2"][0]]).reshape(2, CB // 2, 2 * HD, P).transpose(2, 0, 1, 3)
    w2 = np.stack([np.tile(v[n][0], (1, 2)) for n in ("cmp_k_w2_2", "cmp_v_w2_2")], axis=1)
    rg = np.zeros((2, HD, 2, KB, 2, HD), f32)
    for gate, name in enumerate(("w_rg_a_2", "w_rg_x_2")):
        for e in range(2):
            rg[e, :, gate, :, e, :] = v[name][0][e::2].transpose(1, 0, 2)
    return {
        "weights": weights,
        "columns": cols,
        "tokens": rows_to_partitions(tokens.T),
        "cond": np.stack([v["c"][0], v["c_ctx"]]),
        "gla_a2": a2,
        "cmp_w1": w1,
        "cmp_w2": w2,
        "rg_w": rg.reshape(P, 2, KB, P),
        "spatial_w": v["w_spatial_2"][0].transpose(2, 0, 1),
        "spatial_b": v["b_spatial_2"][0],
        "ln_v_g": v["ln_v_g_2"][0],
    }


def kernel(**inputs):
    import concourse.bacc as bacc
    from concourse.bass_utils import run_bass_kernel_spmd

    laid = {name: np.ascontiguousarray(a) for name, a in lay_out({k: np.asarray(a) for k, a in inputs.items()}).items()}
    nc = bacc.Bacc("TRN2", target_bir_lowering=False, num_devices=1)
    dram = {name: nc.dram_tensor("in_" + name, a.shape, F32, kind="ExternalInput").ap() for name, a in laid.items()}
    out = nc.dram_tensor("out", (P, KD, LAT), F32, kind="ExternalOutput").ap()
    build(nc, dram, out)
    r = run_bass_kernel_spmd(nc, [{"in_" + name: a for name, a in laid.items()}], core_ids=[0])
    y = r.results[0]["out"]
    return y.transpose(2, 1, 0).reshape(1, LAT, D)
```
